# Optimizing a Trainium2 kernel written in Bass

```python
import jax, jax.numpy as jnp
from jax import lax
import numpy as np
import math

D_MODEL = 1024
BATCH = 1
SEQ = 256
DEPTH = 2

GRID_W = 64
CTX_LEN = 256
N_MIXERS = 2
HEAD_DIM = 64
DA_HEADS = D_MODEL // (2 * HEAD_DIM)
NA_HEADS = D_MODEL // HEAD_DIM
NA_WIN_ROWS = 8
NA_WIN_COLS = 16
D_FF = ((8 * D_MODEL + 3 * 256 - 1) // (3 * 256)) * 256
ROPE_THETA = 10000.0
Q_BLOCK = 128
EPS = 1e-6


def rmsnorm(x, g):
    xf = x.astype(jnp.float32)
    y = xf * lax.rsqrt(jnp.mean(xf * xf, axis=-1, keepdims=True) + EPS)
    return (y * g.astype(jnp.float32)).astype(x.dtype)

def adaln(cond, w, b):
    mod = jax.nn.silu(cond) @ w + b
    return jnp.split(mod, 6, axis=-1)

def modulate(xn, shift, scale):
    return xn * (1 + scale) + shift

def swiglu(h, w_gate_up, w_down):
    gu = h @ w_gate_up
    g, u = jnp.split(gu, 2, axis=-1)
    return (jax.nn.silu(g) * u) @ w_down

def axial_rope_tables(n):
    t = jnp.arange(n)
    row = (t // GRID_W).astype(jnp.float32)
    col = (t % GRID_W).astype(jnp.float32)
    half = HEAD_DIM // 2
    freqs = 1.0 / (ROPE_THETA ** (jnp.arange(0, half, 2, dtype=jnp.float32) / half))
    ar = row[:, None] * freqs
    ac = col[:, None] * freqs
    ang = jnp.concatenate([ar, ar, ac, ac], axis=-1)
    return jnp.cos(ang), jnp.sin(ang)

def rotate_half(x):
    x1, x2 = jnp.split(x, 2, axis=-1)
    return jnp.concatenate([-x2, x1], axis=-1)

def apply_rope(t, cos, sin):
    half = t.shape[-1] // 2
    rot = jnp.concatenate([rotate_half(t[..., :half]), rotate_half(t[..., half:])], axis=-1)
    shape = (t.shape[1],) + (1,) * (t.ndim - 3) + (t.shape[-1],)
    return t * cos.reshape(shape).astype(t.dtype) + rot * sin.reshape(shape).astype(t.dtype)

def diff_attention(h_lat, h_ctx, wqkv, lq1, lk1, lq2, lk2, subln, wo, lam_init, need_ctx_out):
    B, N, _ = h_lat.shape
    L = h_ctx.shape[1]
    scale = HEAD_DIM ** -0.5

    def proj(h):
        n = h.shape[1]
        q, k, v = jnp.split(h @ wqkv, 3, axis=-1)
        return (q.reshape(B, n, DA_HEADS, 2, HEAD_DIM),
                k.reshape(B, n, DA_HEADS, 2, HEAD_DIM),
                v.reshape(B, n, DA_HEADS, 2 * HEAD_DIM))

    q_l, k_l, v_l = proj(h_lat)
    q_c, k_c, v_c = proj(h_ctx)
    cos, sin = axial_rope_tables(N)
    q_l = apply_rope(q_l, cos, sin)
    k_l = apply_rope(k_l, cos, sin)

    f32 = jnp.float32
    lam = (jnp.exp(jnp.sum(lq1.astype(f32) * lk1.astype(f32)))
           - jnp.exp(jnp.sum(lq2.astype(f32) * lk2.astype(f32))) + lam_init)

    def attend(q_blk, k, v):
        s = jnp.einsum('bqhmd,bkhmd->bhmqk', q_blk, k).astype(f32) * scale
        p = jax.nn.softmax(s, axis=-1)
        p = p[:, :, 0] - lam * p[:, :, 1]
        return jnp.einsum('bhqk,bkhe->bqhe', p.astype(v.dtype), v)

    k_all = jnp.concatenate([k_c, k_l], axis=1)
    v_all = jnp.concatenate([v_c, v_l], axis=1)
    nblk = N // Q_BLOCK
    q_blocks = q_l.reshape(B, nblk, Q_BLOCK, DA_HEADS, 2, HEAD_DIM).transpose(1, 0, 2, 3, 4, 5)
    o_l = lax.map(lambda qb: attend(qb, k_all, v_all), q_blocks)
    o_l = o_l.transpose(1, 0, 2, 3, 4).reshape(B, N, DA_HEADS, 2 * HEAD_DIM)

    def finish(o, n):
        o = rmsnorm(o, subln) * (1.0 - lam_init)
        return o.reshape(B, n, D_MODEL) @ wo

    y_l = finish(o_l, N)
    y_c = finish(attend(q_c, k_c, v_c), L) if need_ctx_out else None
    return y_l, y_c

def neighbourhood_attention(h_lat, h_ctx, wqkv, rpb, wo, need_ctx_out):
    B, N, _ = h_lat.shape
    L = h_ctx.shape[1]
    rows = N // GRID_W
    wr = min(NA_WIN_ROWS, rows)
    scale = HEAD_DIM ** -0.5
    f32 = jnp.float32

    def proj(h):
        n = h.shape[1]
        q, k, v = jnp.split(h @ wqkv, 3, axis=-1)
        return tuple(t.reshape(B, n, NA_HEADS, HEAD_DIM) for t in (q, k, v))

    q_l, k_l, v_l = proj(h_lat)
    q_c, k_c, v_c = proj(h_ctx)
    kg = k_l.reshape(B, rows, GRID_W, NA_HEADS, HEAD_DIM)
    vg = v_l.reshape(B, rows, GRID_W, NA_HEADS, HEAD_DIM)
    qg = q_l.reshape(B, rows, GRID_W, NA_HEADS, HEAD_DIM).transpose(1, 0, 2, 3, 4)

    qc = np.arange(GRID_W)
    col_start = np.clip(qc - NA_WIN_COLS // 2, 0, GRID_W - NA_WIN_COLS)
    col_mask = (qc[None, :] >= col_start[:, None]) & (qc[None, :] < col_start[:, None] + NA_WIN_COLS)
    dc_idx = np.clip(qc[None, :] - qc[:, None] + NA_WIN_COLS - 1, 0, 2 * NA_WIN_COLS - 2)
    rpb_cols = rpb[:, :, dc_idx]
    col_mask = jnp.asarray(col_mask)[None, None, :, None, :]

    def row_block(args):
        q_row, r = args
        rs = jnp.clip(r - NA_WIN_ROWS // 2, 0, rows - wr)
        kb = lax.dynamic_slice_in_dim(kg, rs, wr, axis=1)
        vb = lax.dynamic_slice_in_dim(vg, rs, wr, axis=1)
        dr_idx = rs + jnp.arange(wr) - r + NA_WIN_ROWS - 1
        bias = rpb_cols[:, dr_idx].transpose(0, 2, 1, 3)
        s_band = jnp.einsum('bqhd,brkhd->bhqrk', q_row, kb).astype(f32) * scale + bias.astype(f32)
        s_band = jnp.where(col_mask, s_band, -jnp.inf)
        s_ctx = jnp.einsum('bqhd,bchd->bhqc', q_row, k_c).astype(f32) * scale
        s = jnp.concatenate([s_band.reshape(B, NA_HEADS, GRID_W, wr * GRID_W), s_ctx], axis=-1)
        p = jax.nn.softmax(s, axis=-1).astype(v_c.dtype)
        p_band = p[..., :wr * GRID_W].reshape(B, NA_HEADS, GRID_W, wr, GRID_W)
        p_ctx = p[..., wr * GRID_W:]
        return (jnp.einsum('bhqrk,brkhd->bqhd', p_band, vb)
                + jnp.einsum('bhqc,bchd->bqhd', p_ctx, v_c))

    o_l = lax.map(row_block, (qg, jnp.arange(rows)))
    y_l = o_l.transpose(1, 0, 2, 3, 4).reshape(B, N, D_MODEL) @ wo

    y_c = None
    if need_ctx_out:
        s = jnp.einsum('bqhd,bkhd->bhqk', q_c, k_c).astype(f32) * scale
        p = jax.nn.softmax(s, axis=-1).astype(v_c.dtype)
        y_c = jnp.einsum('bhqk,bkhd->bqhd', p, v_c).reshape(B, L, D_MODEL) @ wo
    return y_l, y_c

def first_inputs(seed: int = 0) -> dict:
    key = jax.random.key(seed)
    ks = jax.random.split(key, 24)
    D, F = D_MODEL, D_FF
    n_a = (DEPTH + 1) // 2
    n_b = DEPTH // 2
    nrm = jax.random.normal
    f32 = jnp.float32
    return {
        "x": nrm(ks[0], (BATCH, SEQ, D), f32),
        "c": nrm(ks[1], (BATCH, D), f32),
        "ctx": nrm(ks[2], (BATCH, CTX_LEN, D), f32),
        "c_ctx": nrm(ks[3], (D,), f32),
        "ada_w": nrm(ks[4], (DEPTH, D, 6 * D), f32) * D ** -0.5,
        "ada_b": nrm(ks[5], (DEPTH, 6 * D), f32) * 0.01,
        "norm_mix": 1.0 + 0.02 * nrm(ks[6], (DEPTH, D), f32),
        "norm_ffn": 1.0 + 0.02 * nrm(ks[7], (DEPTH, D), f32),
        "da_wqkv": nrm(ks[8], (n_a, D, 3 * D), f32) * D ** -0.5,
        "da_lambda_q1": nrm(ks[9], (n_a, HEAD_DIM), f32) * 0.1,
        "da_lambda_k1": nrm(ks[10], (n_a, HEAD_DIM), f32) * 0.1,
        "da_lambda_q2": nrm(ks[11], (n_a, HEAD_DIM), f32) * 0.1,
        "da_lambda_k2": nrm(ks[12], (n_a, HEAD_DIM), f32) * 0.1,
        "da_subln": 1.0 + 0.02 * nrm(ks[13], (n_a, 2 * HEAD_DIM), f32),
        "da_wo": nrm(ks[14], (n_a, D, D), f32) * D ** -0.5,
        "na_wqkv": nrm(ks[15], (n_b, D, 3 * D), f32) * D ** -0.5,
        "na_rpb": nrm(ks[16], (n_b, NA_HEADS, 2 * NA_WIN_ROWS - 1, 2 * NA_WIN_COLS - 1), f32) * 0.02,
        "na_wo": nrm(ks[17], (n_b, D, D), f32) * D ** -0.5,
        "ffn_w_gate_up": nrm(ks[18], (DEPTH, D, 2 * F), f32) * D ** -0.5,
        "ffn_w_down": nrm(ks[19], (DEPTH, F, D), f32) * F ** -0.5,
        "norm_final": 1.0 + 0.02 * nrm(ks[20], (D,), f32),
    }

def first_block(x, c, ctx, c_ctx, ada_w, ada_b, norm_mix, norm_ffn,
              da_wqkv, da_lambda_q1, da_lambda_k1, da_lambda_q2, da_lambda_k2, da_subln, da_wo,
              na_wqkv, na_rpb, na_wo, ffn_w_gate_up, ffn_w_down, norm_final):
    h, hc = x, ctx
    for i in range(DEPTH):
        last = i == DEPTH - 1
        sh_m, sc_m, g_m, sh_f, sc_f, g_f = (t[:, None, :] for t in adaln(c, ada_w[i], ada_b[i]))
        csh_m, csc_m, cg_m, csh_f, csc_f, cg_f = adaln(c_ctx, ada_w[i], ada_b[i])

        xn = modulate(rmsnorm(h, norm_mix[i]), sh_m, sc_m)
        xc = modulate(rmsnorm(hc, norm_mix[i]), csh_m, csc_m)
        j = i // N_MIXERS
        if i % N_MIXERS == 0:
            lam_init = 0.8 - 0.6 * float(np.exp(-0.3 * i))
            y, yc = diff_attention(xn, xc, da_wqkv[j], da_lambda_q1[j], da_lambda_k1[j],
                                   da_lambda_q2[j], da_lambda_k2[j], da_subln[j], da_wo[j],
                                   lam_init, not last)
        else:
            y, yc = neighbourhood_attention(xn, xc, na_wqkv[j], na_rpb[j], na_wo[j], not last)

        h = h + g_m * y
        h = h + g_f * swiglu(modulate(rmsnorm(h, norm_ffn[i]), sh_f, sc_f),
                             ffn_w_gate_up[i], ffn_w_down[i])
        if not last:
            hc = hc + cg_m * yc
            hc = hc + cg_f * swiglu(modulate(rmsnorm(hc, norm_ffn[i]), csh_f, csc_f),
                                    ffn_w_gate_up[i], ffn_w_down[i])
    return rmsnorm(h, norm_final)


DEPTH_2 = 1

D_CONV = D_MODEL
CONV_WIDTH = 3
MLA_HEADS = 8
QK_NOPE = 128
QK_ROPE = 64
V_HEAD = 128
Q_LORA = 256
KV_LORA = 128
MEM_LEN = 256
MEM_HEADS = 4
MEM_HEAD_DIM = D_MODEL // MEM_HEADS
N_EXPERTS = 16
EXPERT_FF = 1024
CAPACITY_FACTOR = 2
IN_COLS = 3 * D_CONV + Q_LORA + KV_LORA + QK_ROPE + 2 * D_MODEL


def rmsnorm_2(x, g):
    xf = x.astype(jnp.float32)
    y = xf * lax.rsqrt(jnp.mean(xf * xf, axis=-1, keepdims=True) + EPS)
    return (y * g.astype(jnp.float32)).astype(x.dtype)

def rotary_tables(seq):
    inv = 1.0 / (ROPE_THETA ** (jnp.arange(0, QK_ROPE, 2, dtype=jnp.float32) / QK_ROPE))
    ang = jnp.arange(seq, dtype=jnp.float32)[:, None] * inv[None, :]
    return jnp.cos(ang), jnp.sin(ang)

def apply_rope_2(v, cos, sin):
    vf = v.astype(jnp.float32)
    v1, v2 = jnp.split(vf, 2, axis=-1)
    out = jnp.concatenate([v1 * cos - v2 * sin, v1 * sin + v2 * cos], axis=-1)
    return out.astype(v.dtype)

def short_conv(v, w, b):
    y = lax.conv_general_dilated(
        v, w[:, None, :].astype(v.dtype), window_strides=(1,), padding=((1, 1),),
        dimension_numbers=("NWC", "WIO", "NWC"), feature_group_count=v.shape[-1])
    return y + b.astype(v.dtype)

def mla_attention(q_nope, q_rope, k_nope, k_rope, v):
    b, s, h, _ = q_nope.shape
    nb = s // Q_BLOCK
    scale = (QK_NOPE + QK_ROPE) ** -0.5
    qn = q_nope.reshape(b, nb, Q_BLOCK, h, QK_NOPE).transpose(1, 0, 2, 3, 4)
    qr = q_rope.reshape(b, nb, Q_BLOCK, h, QK_ROPE).transpose(1, 0, 2, 3, 4)

    def block(args):
        qn_b, qr_b = args
        sc = (jnp.einsum("bqhd,bkhd->bhqk", qn_b, k_nope)
              + jnp.einsum("bqhr,bkr->bhqk", qr_b, k_rope))
        p = jax.nn.softmax(sc.astype(jnp.float32) * scale, axis=-1).astype(v.dtype)
        return jnp.einsum("bhqk,bkhd->bqhd", p, v)

    o = lax.map(block, (qn, qr))
    return o.transpose(1, 0, 2, 3, 4).reshape(b, s, h * V_HEAD)

def memory_cross_attention(h, m, w_q, w_kv, w_o):
    b, s, _ = h.shape
    ml = m.shape[1]
    q = (h @ w_q).reshape(b, s, MEM_HEADS, MEM_HEAD_DIM)
    kv = (m @ w_kv).reshape(b, ml, 2, MEM_HEADS, MEM_HEAD_DIM)
    k, v = kv[:, :, 0], kv[:, :, 1]
    sc = jnp.einsum("bqhd,bkhd->bhqk", q, k).astype(jnp.float32) * (MEM_HEAD_DIM ** -0.5)
    p = jax.nn.softmax(sc, axis=-1).astype(v.dtype)
    o = jnp.einsum("bhqk,bkhd->bqhd", p, v).reshape(b, s, MEM_HEADS * MEM_HEAD_DIM)
    return o @ w_o

def expert_choice_moe(h, w_router, w_gate, w_up, w_down):
    b, s, d = h.shape
    cap = max(1, CAPACITY_FACTOR * s // N_EXPERTS)
    aff = jax.nn.softmax((h @ w_router).astype(jnp.float32), axis=-1)
    gates, idx = lax.top_k(jnp.swapaxes(aff, 1, 2), cap)
    xg = jax.vmap(lambda hb, ib: hb[ib])(h, idx)
    a = jax.nn.silu(jnp.einsum("becd,edf->becf", xg, w_gate)) * jnp.einsum("becd,edf->becf", xg, w_up)
    yo = jnp.einsum("becf,efd->becd", a, w_down) * gates[..., None].astype(h.dtype)
    return jax.vmap(lambda ib, vb: jnp.zeros((s, d), vb.dtype).at[ib.reshape(-1)].add(vb.reshape(-1, d)))(idx, yo)

def second_inputs(seed: int = 0) -> dict:
    key = jax.random.key(seed)
    ks = jax.random.split(key, 32)

    def w(k, shape, fan_in):
        return jax.random.normal(k, shape, jnp.float32) * fan_in ** -0.5

    def g(k, shape):
        return 1.0 + 0.02 * jax.random.normal(k, shape, jnp.float32)

    def bias(k, shape):
        return 0.02 * jax.random.normal(k, shape, jnp.float32)

    L = DEPTH_2
    return {
        "x": jax.random.normal(ks[0], (BATCH, SEQ, D_MODEL), jnp.float32),
        "mem": jax.random.normal(ks[1], (BATCH, MEM_LEN, D_MODEL), jnp.float32),
        "norm_mix_g": g(ks[2], (L, D_MODEL)),
        "w_in": w(ks[3], (L, D_MODEL, IN_COLS), D_MODEL),
        "conv_w": w(ks[4], (L, CONV_WIDTH, D_CONV), CONV_WIDTH),
        "conv_b": bias(ks[5], (L, D_CONV)),
        "w_conv_out": w(ks[6], (L, D_CONV, D_MODEL), D_CONV),
        "q_norm_g": g(ks[7], (L, Q_LORA)),
        "w_uq": w(ks[8], (L, Q_LORA, MLA_HEADS * (QK_NOPE + QK_ROPE)), Q_LORA),
        "kv_norm_g": g(ks[9], (L, KV_LORA)),
        "w_ukv": w(ks[10], (L, KV_LORA, MLA_HEADS * (QK_NOPE + V_HEAD)), KV_LORA),
        "w_mla_out": w(ks[11], (L, MLA_HEADS * V_HEAD, D_MODEL), MLA_HEADS * V_HEAD),
        "b_gate": bias(ks[12], (L, 2 * D_MODEL)),
        "w_mix_out": w(ks[13], (L, D_MODEL, D_MODEL), D_MODEL),
        "norm_mem_g": g(ks[14], (L, D_MODEL)),
        "norm_memkv_g": g(ks[15], (L, D_MODEL)),
        "w_mem_q": w(ks[16], (L, D_MODEL, MEM_HEADS * MEM_HEAD_DIM), D_MODEL),
        "w_mem_kv": w(ks[17], (L, D_MODEL, 2 * MEM_HEADS * MEM_HEAD_DIM), D_MODEL),
        "w_mem_out": w(ks[18], (L, MEM_HEADS * MEM_HEAD_DIM, D_MODEL), MEM_HEADS * MEM_HEAD_DIM),
        "norm_moe_g": g(ks[19], (L, D_MODEL)),
        "w_router": w(ks[20], (L, D_MODEL, N_EXPERTS), D_MODEL),
        "w_exp_gate": w(ks[21], (L, N_EXPERTS, D_MODEL, EXPERT_FF), D_MODEL),
        "w_exp_up": w(ks[22], (L, N_EXPERTS, D_MODEL, EXPERT_FF), D_MODEL),
        "w_exp_down": w(ks[23], (L, N_EXPERTS, EXPERT_FF, D_MODEL), EXPERT_FF),
        "norm_final_g": g(ks[24], (D_MODEL,)),
    }

def second_block(x, mem, norm_mix_g, w_in, conv_w, conv_b, w_conv_out, q_norm_g, w_uq, kv_norm_g,
              w_ukv, w_mla_out, b_gate, w_mix_out, norm_mem_g, norm_memkv_g, w_mem_q, w_mem_kv,
              w_mem_out, norm_moe_g, w_router, w_exp_gate, w_exp_up, w_exp_down, norm_final_g):
    b, s, _ = x.shape
    cos, sin = rotary_tables(s)
    splits = list(np.cumsum([D_CONV, D_CONV, D_CONV, Q_LORA, KV_LORA, QK_ROPE]))
    for l in range(DEPTH_2):
        h = rmsnorm_2(x, norm_mix_g[l])
        u = h @ w_in[l]
        xc, gb, gc, cq, ckv, kr, glog = jnp.split(u, splits, axis=-1)
        y_conv = (gb * short_conv(gc * xc, conv_w[l], conv_b[l])) @ w_conv_out[l]
        q = (rmsnorm_2(cq, q_norm_g[l]) @ w_uq[l]).reshape(b, s, MLA_HEADS, QK_NOPE + QK_ROPE)
        q_nope, q_rope = q[..., :QK_NOPE], apply_rope_2(q[..., QK_NOPE:], cos[None, :, None, :], sin[None, :, None, :])
        kv = (rmsnorm_2(ckv, kv_norm_g[l]) @ w_ukv[l]).reshape(b, s, MLA_HEADS, QK_NOPE + V_HEAD)
        k_nope, v = kv[..., :QK_NOPE], kv[..., QK_NOPE:]
        k_rope = apply_rope_2(kr, cos[None], sin[None])
        y_mla = mla_attention(q_nope, q_rope, k_nope, k_rope, v) @ w_mla_out[l]
        gates = jax.nn.sigmoid((glog + b_gate[l]).astype(jnp.float32)).astype(x.dtype)
        g_conv, g_mla = gates[..., :D_MODEL], gates[..., D_MODEL:]
        x = x + (g_conv * y_conv + g_mla * y_mla) @ w_mix_out[l]
        x = x + memory_cross_attention(rmsnorm_2(x, norm_mem_g[l]), rmsnorm_2(mem, norm_memkv_g[l]),
                                       w_mem_q[l], w_mem_kv[l], w_mem_out[l])
        x = x + expert_choice_moe(rmsnorm_2(x, norm_moe_g[l]), w_router[l], w_exp_gate[l],
                                  w_exp_up[l], w_exp_down[l])
    return rmsnorm_2(x, norm_final_g)


def setup_inputs(seed=0):
    out = dict(first_inputs(seed))
    for name, value in second_inputs(seed + 1).items():
        if name != "x":
            out[name + "_2"] = value
    return out


def reference(
    x, c, ctx, c_ctx, ada_w, ada_b, norm_mix, norm_ffn, da_wqkv, da_lambda_q1, da_lambda_k1,
    da_lambda_q2, da_lambda_k2, da_subln, da_wo, na_wqkv, na_rpb, na_wo, ffn_w_gate_up,
    ffn_w_down, norm_final, mem_2, norm_mix_g_2, w_in_2, conv_w_2, conv_b_2, w_conv_out_2,
    q_norm_g_2, w_uq_2, kv_norm_g_2, w_ukv_2, w_mla_out_2, b_gate_2, w_mix_out_2, norm_mem_g_2,
    norm_memkv_g_2, w_mem_q_2, w_mem_kv_2, w_mem_out_2, norm_moe_g_2, w_router_2, w_exp_gate_2,
    w_exp_up_2, w_exp_down_2, norm_final_g_2,
):
    x = first_block(
        x, c, ctx, c_ctx, ada_w, ada_b, norm_mix, norm_ffn, da_wqkv, da_lambda_q1, da_lambda_k1,
        da_lambda_q2, da_lambda_k2, da_subln, da_wo, na_wqkv, na_rpb, na_wo, ffn_w_gate_up,
        ffn_w_down, norm_final,
    )
    return second_block(
        x, mem_2, norm_mix_g_2, w_in_2, conv_w_2, conv_b_2, w_conv_out_2, q_norm_g_2, w_uq_2,
        kv_norm_g_2, w_ukv_2, w_mla_out_2, b_gate_2, w_mix_out_2, norm_mem_g_2, norm_memkv_g_2,
        w_mem_q_2, w_mem_kv_2, w_mem_out_2, norm_moe_g_2, w_router_2, w_exp_gate_2, w_exp_up_2,
        w_exp_down_2, norm_final_g_2,
    )


_drawn_inputs = setup_inputs


def setup_inputs(seed=0):
    import zlib

    import numpy as np

    out = dict(_drawn_inputs(seed))
    spreads = {}
    factors = {'norm_mix': 2.88,
     'da_lambda_q1': 4.303,
     'da_lambda_k1': 8.0,
     'da_subln': 3.575,
     'na_rpb': 8.0,
     'norm_mix_g_2': 2.962,
     'conv_b_2': 5.307,
     'q_norm_g_2': 8.0,
     'kv_norm_g_2': 8.0,
     'b_gate_2': 5.979,
     'norm_mem_g_2': 8.0,
     'norm_memkv_g_2': 8.0,
     'norm_moe_g_2': 3.894,
     'norm_final_g_2': 2.828}
    for name, (base, spread) in spreads.items():
        noise = np.random.default_rng([zlib.crc32(name.encode()), seed]).standard_normal(out[name].shape)
        drawn = base * np.exp(spread * noise) if base else spread * noise
        out[name] = __import__('jax').numpy.asarray(drawn.astype(out[name].dtype))
    for name, factor in factors.items():
        out[name] = (out[name] * factor).astype(out[name].dtype)
    return out
```

```python
from contextlib import ExitStack

import numpy as np

import concourse.bass as bass
from concourse import mybir

F32 = mybir.dt.float32
I32 = mybir.dt.int32
U32 = mybir.dt.uint32
ALU = mybir.AluOpType
ACT = mybir.ActivationFunctionType
AX = mybir.AxisListType

P = 128
D = 1024
KC = D // P
CTX = 256
LAT = 256
TOK = CTX + LAT
FF = 2816
FC = FF // P
GRID_W = 64
HEADS = 16
HD = 64
RPB_R, RPB_C = 15, 31
NEG = -1e30
EPS = 1e-6
LAM_INIT = 0.8 - 0.6 * float(np.exp(-0.3 * 0))
MLA_H = 8
MEM_H = 4
NE = 16
CAP = 2 * LAT // NE
SLOTS = 8
UNIT = KC * P
WIDE = FC // 2 * P

_COLS = [("mix0", 8), ("mix1", 8), ("ffn0", 8), ("ffn1", 8), ("final", 8), ("mix2", 8), ("mem", 8), ("memkv", 8),
         ("moe", 8), ("final2", 8), ("qn", 2), ("kvn", 1), ("subln", 1), ("conv_w", 24), ("conv_b", 8),
         ("b_gate", 16), ("ada_b", 96)]
COL, _n = {}, 0
for _name, _w in _COLS:
    COL[_name] = (_n, _n + _w)
    _n += _w
NCOLS = _n

_CONST = [("ident", 128), ("ones", 128), ("rot_a", 128), ("rot_b", 128), ("cos_a", LAT), ("sin_a", LAT),
          ("cos_b", LAT), ("sin_b", LAT), ("mask", GRID_W), ("inv", 3), ("token", 2), ("experts", NE * CAP)]
CONST, _n = {}, 0
for _name, _w in _CONST:
    CONST[_name] = (_n, _n + _w)
    _n += _w
NCONST = _n


class Stage:

    def __init__(self, name, weights, units, chunks, owner, width=UNIT, share=None):
        self.name, self.weights, self.units, self.chunks, self.owner, self.width = (
            name, weights, units, chunks, owner, width)
        self.share = share

    def raises(self, c):
        if self.share is None:
            return "used", self.u0 + (c + 1) * self.units // self.chunks
        cs, us = self.share
        if us and c % cs == cs - 1:
            return "used", self.u0 + (c // cs + 1) * us
        return "chunk", self.k0 + (c - c // cs if us else c) + 1


def plan():
    stages = [
        Stage("ada0a", ("ada0", 0), 16, 2, "D"),
        Stage("q0", ("wqkv0", 0), 8, 8, "A"), Stage("k0", ("wqkv0", 8), 8, 8, "A"),
        Stage("v0", ("wqkv0", 16), 8, 8, "A", share=(4, 4)), Stage("rope0", None, 0, 8, "D", share=(8, 0)),
        Stage("ada0b", ("ada0", 16), 32, 4, "D"),
        Stage("wo0", ("wo0", 0), 8, 8, "D"),
        Stage("ada1a", ("ada1", 0), 8, 1, "D"), Stage("ada1b", ("ada1", 8), 8, 1, "D"),
        Stage("gu0", ("gu0", 0), 2 * FC, 2 * FC, "AD"), Stage("down0", ("down0", 0), 16, 8, "D", WIDE),
        Stage("ada1c", ("ada1", 16), 8, 1, "D"), Stage("ada1d", ("ada1", 24), 8, 1, "D"),
        Stage("q1", ("wqkv1", 0), 8, 8, "A"), Stage("k1", ("wqkv1", 8), 8, 8, "A"),
        Stage("v1", ("wqkv1", 16), 8, 8, "A", share=(4, 4)),
        Stage("ada1e", ("ada1", 32), 16, 2, "D"),
        Stage("wo1", ("wo1", 0), 8, 8, "D"),
        Stage("gu1", ("gu1", 0), 2 * FC, 2 * FC, "AD"), Stage("down1", ("down1", 0), 16, 8, "D", WIDE),
        Stage("memk", ("memkv", 0), 8, 8, "A"), Stage("memv", ("memkv", 8), 8, 4, "A", share=(2, 4)),
        Stage("win", ("win", 0), 27, 27, "A"), Stage("wing", ("win", 27), 16, 16, "A"),
        Stage("winr", ("win", 43), 1, 1, "A"),
        Stage("uq", ("uq", 0), 3, 12, "A", share=(4, 1)), Stage("uk", ("ukv", 0), 1, 8, "A", share=(8, 1)),
        Stage("uv", ("ukv", 1), 1, 4, "A", share=(4, 1)), Stage("rope2", None, 0, 3, "D", share=(3, 0)),
        Stage("conv", ("conv_out", 0), 8, 8, "D"), Stage("mla", ("mla_out", 0), 8, 8, "D"),
        Stage("mix", ("mix_out", 0), 8, 8, "D"),
        Stage("memq", ("memq", 0), 8, 8, "A"), Stage("memo", ("memo", 0), 8, 8, "D"),
        Stage("scatter", None, 0, 8, "D", share=(8, 0)),
    ]
    unit = chunk = a = d = k = 0
    for s in stages:
        if s.name == "scatter":
            s.expert_unit = unit
        s.u0, s.c0, s.a0, s.d0, s.k0 = unit, chunk, a, d, k
        unit += s.units
        chunk += s.chunks
        a += {"A": s.chunks, "D": 0, "AD": s.chunks // 2}[s.owner]
        d += {"D": s.chunks, "A": 0, "AD": s.chunks // 2}[s.owner]
        s.a1, s.d1, s.c1 = a, d, chunk
        if s.share:
            k += s.chunks - (s.chunks // s.share[0] if s.share[1] else 0)
    return {s.name: s for s in stages}


class Steps:

    def __init__(self, eng, sem):
        self.eng, self.sem, self.n = eng, sem, 0

    def link(self, ins):
        self.n += 1
        ins.then_inc(self.sem, 1)
        self.eng.wait_ge(self.sem, self.n)


def diffusion_moe_kernel(nc, t, out, stop=None):
    st = plan()
    ctx = ExitStack()
    with ctx:
        def sb(name, shape, dt=F32):
            return ctx.enter_context(nc.sbuf_tensor(name, shape, dt))

        def sem(name):
            return ctx.enter_context(nc.semaphore(name))

        ring = sb("ring", [P, SLOTS, WIDE])
        hT = sb("hT", [P, KC, TOK])
        xn = sb("xn", [P, KC, TOK])
        big = sb("big", [P, 12288])
        aux = sb("aux", [P, 11264])
        work = sb("work", [P, 6144])
        cst = sb("cst", [P, NCONST])
        cols = sb("cols", [P, NCOLS])
        cond = sb("cond", [P, KC, 2])
        scond = sb("scond", [P, KC, 2])
        mod = sb("mod", [P, 2, 48, 2])
        gain = sb("gain", [P, 4, KC, 2])
        lamv = sb("lamv", [P, 4, HD])
        lams = sb("lams", [P, 8])
        small = sb("small", [P, 192])
        wr = sb("wr", [P, KC, NE])

        rpb_copies = nc.dram_tensor("rpb_copies", (GRID_W, HEADS * RPB_R * RPB_C), F32, kind="Internal").ap()
        ps = ctx.enter_context(nc.psum_tensor("ps", [P, 8, 512], F32))

        def const(name):
            a, b = CONST[name]
            return cst[:, a:b]

        def col(name, k=0, n=1):
            a = COL[name][0] + k
            return cols[:, a:a + n]

        ident, ones = const("ident"), const("ones")
        lat = slice(CTX, TOK)
        sq = work[:, 0:KC * TOK].rearrange("p (k t) -> p k t", k=KC)
        diag = work[:, 4096:4608].rearrange("p (a b) -> p a b", b=P)
        var, rs, tmp = small[:, 0:32], small[:, 32:64], small[:, 64:96]
        qk = big[:, 0:16 * TOK].rearrange("p (c t) -> p c t", c=16)
        vv = big[:, 8192:12288].rearrange("p (k d) -> p k d", k=4)
        hid = big[:, 0:FC * TOK].rearrange("p (k t) -> p k t", k=FC)
        silu_out = work[:, 5120:6144].rearrange("p (b t) -> p b t", b=2)
        ropet = work[:, 0:2048].rearrange("p (b c t) -> p b c t", b=4, c=2)
        bias = aux[:, 0:8192].rearrange("p (q h k) -> p q h k", q=2, h=HEADS)
        u = big[:, 0:44 * LAT].rearrange("p (c t) -> p c t", c=44)
        mq = aux[:, 0:12 * LAT].rearrange("p (c t) -> p c t", c=12)
        mk = aux[:, 3072:5120].rearrange("p (c t) -> p c t", c=8)
        mv = aux[:, 5120:7168].rearrange("p (k d) -> p k d", k=2)
        memk = aux[:, 7168:9216].rearrange("p (c t) -> p c t", c=8)
        memv = aux[:, 9216:11264].rearrange("p (k d) -> p k d", k=2)
        x2 = xn[:, :, 0:LAT]
        h2 = hT[:, :, lat]
        memT = xn[:, :, lat]
        E = work[:, 0:2048].rearrange("p (b c n) -> p b c n", b=2, c=2)
        PR = work[:, 2048:3072].rearrange("p (b n) -> p b n", b=2)
        PT = work[:, 3072:5120].rearrange("p (b n) -> p b n", b=4)
        amax, anm = small[:, 96:100], small[:, 100:104]
        asum, arec = small[:, 104:108], small[:, 108:112]
        hs = big[:, 0:2048].rearrange("p (s d) -> p s d", s=2)
        sel = big[:, 2048:3072].rearrange("p (s n) -> p s n", s=2)
        gsel = big[:, 3072:4096].rearrange("p (s n) -> p s n", s=2)
        gT = big[:, 4096:5120].rearrange("p (g t) -> p g t", g=4)
        xg = big[:, 5120:9216].rearrange("p (k n) -> p k n", k=KC)
        xe = big[:, 9216:9472].rearrange("p (k n) -> p k n", k=KC)
        sg = big[:, 9472:9728]
        he = big[:, 9728:9984].rearrange("p (k n) -> p k n", k=KC)
        aff = big[:, 9984:10016].rearrange("p (s e) -> p s e", s=2)
        affT = big[0:NE, 10240:10496]
        top = big[0:NE, 10496:10528]
        topi = big[0:NE, 10528:10560].bitcast(U32)
        topf = big[0:NE, 10560:10592]
        spread = big[0:NE, 10592:11616].rearrange("p (a n) -> p a n", a=2)
        yT = aux[:, 0:4096].rearrange("p (k n) -> p k n", k=KC)
        yo = aux[:, 4096:8192].rearrange("p (g d) -> p g d", g=4)

        s_small = sem("small_inputs_loaded")
        s_bias = sem("rpb_loaded")
        s_copies = sem("rpb_copied")
        s_biasm = sem("bias_masked")
        s_mem = sem("mem_loaded")
        s_land = [sem(f"unit_landed_{i}") for i in range(SLOTS)]
        s_used = sem("unit_used")
        s_chunk = sem("chunk_computed")
        s_freeA = sem("chunk_read_by_scalar")
        s_freeD = sem("chunk_read_by_vector")
        s_scond = sem("silu_of_cond")
        s_gain = sem("gains")
        s_lamin = sem("lambda_sums")
        s_lamex = sem("lambda_exps")
        s_sqA = sem("squares_by_scalar")
        s_sqD = sem("squares_by_vector")
        s_stat = sem("mean_squares")
        s_diag = sem("rstd_diagonals")
        s_bc = sem("rstd_broadcast")
        s_nD = sem("normed_by_vector")
        s_nA = sem("shifted_by_scalar")
        s_scores = sem("scores")
        s_max = sem("score_max")
        s_exp = sem("exps")
        s_prob = sem("probs")
        s_pt = sem("probs_transposed")
        s_ptsb = sem("probs_transposed_in_sbuf")
        s_pv = sem("heads_out")
        s_osb = sem("heads_out_in_sbuf")
        s_conv = sem("conv_ready")
        s_rmax = sem("router_max")
        s_rexp = sem("router_exp")
        s_moe = sem("moe_pe")
        s_moeD = sem("moe_vector")
        s_moeA = sem("moe_scalar")
        s_g = sem("expert_gate")
        s_up = sem("expert_up")
        s_sg = sem("expert_silu")
        s_he = sem("expert_hidden")
        s_xe = sem("expert_tokens")
        s_y = sem("expert_out")
        s_yT = sem("expert_out_in_sbuf")
        s_out = sem("output_stored")
        c_dve = sem("vector_steps")
        c_act = sem("scalar_steps")
        c_pool = sem("pool_steps")

        norms = [
            ("n0", hT[:, :, :], xn[:, :, :], KC, TOK, "mix0", 0, 0),
            ("sub", xn[:, :, :], xn[:, :, :], KC, TOK, "subln", 2, None),
            ("n1", hT[:, :, :], xn[:, :, :], KC, TOK, "ffn0", 0, 1),
            ("n2", hT[:, :, :], xn[:, :, :], KC, TOK, "mix1", 0, 2),
            ("n3", h2, x2, KC, LAT, "ffn1", 0, 3),
            ("nmem", memT, memT, KC, LAT, "memkv", 0, None),
            ("nf", h2, h2, KC, LAT, "final", 0, None),
            ("nmix", h2, x2, KC, LAT, "mix2", 0, None),
            ("nq", u[:, 24:26, :], u[:, 24:26, :], 2, LAT, "qn", 1, None),
            ("nkv", u[:, 26:27, :], u[:, 26:27, :], 1, LAT, "kvn", 2, None),
            ("nq2", h2, x2, KC, LAT, "mem", 0, None),
            ("nmoe", h2, x2, KC, LAT, "moe", 0, None),
            ("nout", h2, x2, KC, LAT, "final2", 0, None),
        ]
        NORM, nd, na, sd = {}, 0, 0, 0
        for n, (name, src, dst, nk, T, g, inv, m) in enumerate(norms):
            nd += nk
            sd += nk == KC
            na += nk if m is not None else 0
            NORM[name] = dict(n=n, src=src, dst=dst, nk=nk, T=T, g=g, inv=inv, m=m, nd=nd, na=na, sd=sd)
        MODS = [(0, 0), (0, 3), (1, 0), (1, 3)]

        def da_jobs():
            for h in range(8):
                for q in range(4):
                    n = CTX if q < 2 else TOK
                    yield dict(
                        n=n, da=True, scale=1.0,
                        scores=[[(qk[64 * c:64 * c + 64, h, q * P:q * P + P], qk[64 * c:64 * c + 64, 8 + h, 0:n], 0, n)]
                                for c in range(2)],
                        groups=[[(None, k) for k in range(n // P)]],
                        pv=[[(0, P, q * P, vv[:, k, h * P:h * P + P], k * P, P, k == 0, k == n // P - 1)
                             for k in range(n // P)]],
                        first=q == 0, evac=xn[:, h, :] if q == 3 else None, out=(0, P, TOK))

        def na_jobs():
            for h in range(HEADS):
                o, c = 64 * (h % 2), h // 2
                yield dict(
                    n=TOK, da=False, scale=1.0,
                    scores=[[(qk[o:o + 64, c, CTX + p * P:CTX + p * P + P], qk[o:o + 64, 8 + c, :], 0, TOK),
                             (ident, bias[:, p, h, :], CTX, LAT)] for p in range(2)],
                    groups=[[(p, 2 * g + k) for k in range(2) for p in range(2)] for g in range(2)],
                    pv=[[(o, 64, 0, vv[:, 2 * g + k, h * 64:h * 64 + 64], k * 256, 256, g + k == 0, g + k == 2)
                         for k in range(2)] for g in range(2)],
                    first=h % 2 == 0, evac=xn[:, c, 0:LAT] if h % 2 else None, out=(0, P, LAT))

        def mla_jobs():
            for h in range(MLA_H):
                o = 64 * (h % 2)
                yield dict(
                    n=LAT, da=False, scale=float(192 ** -0.5),
                    scores=[[(mq[:, h, p * P:p * P + P], mk[:, h, :], 0, LAT),
                             (mq[o:o + 64, 8 + h // 2, p * P:p * P + P], u[o:o + 64, 43, :], 0, LAT)]
                            for p in range(2)],
                    groups=[[(p, k) for k in range(2) for p in range(2)]],
                    pv=[[(0, P, 0, mv[:, k, h * P:h * P + P], k * 256, 256, k == 0, k == 1) for k in range(2)]],
                    first=True, evac=x2[:, h, :], out=(0, P, LAT))

        def mem_jobs():
            for h in range(MEM_H):
                yield dict(
                    n=LAT, da=False, scale=1.0 / 16.0,
                    scores=[[(mq[:, 2 * h + k, p * P:p * P + P], memk[:, 2 * h + k, :], 0, LAT) for k in range(2)]
                            for p in range(2)],
                    groups=[[(p, k) for k in range(2) for p in range(2)]],
                    pv=[[(0, P, 256 * e, memv[:, k, h * 256 + e * P:h * 256 + e * P + P], k * 256, 256, k == 0, k == 1)
                         for e in range(2) for k in range(2)]],
                    first=True, evac=x2[:, 2 * h:2 * h + 2, :], out=(0, P, 2 * LAT))

        JOBS, jobs, job_groups, job_outs = {}, [], [], []
        for name, made in (("da", da_jobs()), ("na", na_jobs()), ("mla", mla_jobs()), ("mem", mem_jobs())):
            a = len(jobs)
            for j in made:
                j["g0"] = sum(job_groups)
                j["o"] = sum(job_outs)
                job_groups.append(len(j["groups"]))
                job_outs.append(1 if j["evac"] is not None else 0)
                jobs.append(j)
            JOBS[name] = (a, len(jobs), sum(job_groups), sum(job_outs))
        g_end = sum(job_groups)

        def groups_before(j):
            return jobs[j]["g0"] if j < len(jobs) else g_end

        block = ctx.enter_context(nc.Block())

        @block.sync
        def _(sp):
            sp.dma_start(cst[:, :], t["consts"]).then_inc(s_small, 16)
            sp.dma_start(cond[:, :, :], t["cond"]).then_inc(s_small, 16)
            sp.dma_start(cols[:, :], t["cols"]).then_inc(s_small, 16)
            sp.dma_start(hT[:, :, 0:CTX], t["ctxT"]).then_inc(s_small, 16)
            sp.dma_start(hT[:, :, lat], t["xT"]).then_inc(s_small, 16)

            def stream(src, u0, off, n, width):
                full = n // SLOTS if n >= 2 * SLOTS and u0 >= SLOTS else 0

                def load(i, j):
                    s = (u0 + j) % SLOTS
                    if u0 + j >= SLOTS or not isinstance(i, int):
                        sp.wait_ge(s_used, i * SLOTS + (u0 + j - SLOTS + 1))
                    sp.dma_start(ring[:, s, 0:width], src[i * SLOTS + (off + j)]).then_inc(s_land[s], 16)

                if full:
                    with sp.Fori(0, full) as i:
                        for j in range(SLOTS):
                            load(i, j)
                for j in range(full * SLOTS, n):
                    load(0, j)

            for s in st.values():
                if s.units:
                    stream(t[s.weights[0]], s.u0, s.weights[1], s.units, s.width)
            u0 = st["scatter"].expert_unit
            with sp.Fori(0, NE) as e:
                for part, name in enumerate(("gate", "up", "down")):
                    for j in range(8):
                        s = (u0 + j) % SLOTS
                        sp.wait_ge(s_used, e * 24 + (u0 + 8 * part + j - SLOTS + 1))
                        sp.dma_start(ring[:, s, 0:UNIT], t[name][e * 8 + j]).then_inc(s_land[s], 16)
            sp.wait_ge(s_nD, NORM["nout"]["nd"])
            sp.dma_start(out, x2).then_inc(s_out, 16)
            sp.wait_ge(s_out, 16)

        @block.gpsimd
        def _(pool):
            pool.dma_start(lamv[:, :, :].rearrange("p a b -> p (a b)"),
                           bass.AP(t["lam"].tensor, 0, [[0, P], [1, 4 * HD]])).then_inc(s_lamin, 16)
            pool.dma_start(wr[:, :, :], t["wr"]).then_inc(s_bias, 16)
            table = HEADS * RPB_R * RPB_C
            pool.dma_start(rpb_copies, bass.AP(t["rpb"].tensor, 0, [[0, GRID_W], [1, table]])).then_inc(s_copies, 16)
            pool.wait_ge(s_copies, 16)
            for r in range(4):
                for rr in range(4):
                    o = 64 * (r % 2)
                    pool.dma_start(
                        bias[o:o + 64, r // 2, :, rr * GRID_W:(rr + 1) * GRID_W],
                        bass.AP(rpb_copies.tensor, (rr - r + 7) * RPB_C + 15,
                                [[table - 1, GRID_W], [RPB_R * RPB_C, HEADS], [1, GRID_W]])).then_inc(s_bias, 16)
            pool.wait_ge(s_bias, 17 * 16)
            pool.wait_ge(s_small, 80)
            bm = aux[:, 0:8192].rearrange("p (n c) -> p n c", c=GRID_W)
            pool.tensor_tensor(bm, bm, const("mask").unsqueeze(1).to_broadcast([P, P, GRID_W]),
                               ALU.add).then_inc(s_biasm, 1)
            pool.wait_ge(s_used, st["v1"].u0 + 8)
            pool.dma_start(memT, t["memT"]).then_inc(s_mem, 16)

        @block.tensor
        def _(pe):
            def landed(u0, i, j, per=SLOTS):
                pe.wait_ge(s_land[(u0 + j) % SLOTS], i * (16 * per // SLOTS) + 16 * ((u0 + j) // SLOTS + 1))

            def slot(u0, j):
                return (u0 + j) % SLOTS

            def begin(s):
                if s.a0:
                    pe.wait_ge(s_freeA, s.a0)
                if s.d0:
                    pe.wait_ge(s_freeD, s.d0)

            def bank_free(s, i, c, per=0):
                if c < 4 and isinstance(i, int):
                    return
                if s.owner == "AD":
                    base, sm = (s.a0, s_freeA) if c % 2 == 0 else (s.d0, s_freeD)
                    pe.wait_ge(sm, i * (per // 2) + (base + c // 2 - 2 + 1))
                elif s.owner == "A":
                    pe.wait_ge(s_freeA, i * per + (s.a0 + c - 3))
                else:
                    pe.wait_ge(s_freeD, i * per + (s.d0 + c - 3))

            def bank(s, c):
                return (s.c0 + c) % 4

            def computed(s, c, mm):
                if s.raises(c)[0] == "used":
                    mm.then_inc(s_used, s.share[1])
                else:
                    mm.then_inc(s_chunk, 1)

            def rows(s, rhs, T, nk=KC, per_chunk=1):
                begin(s)
                kper = nk // per_chunk

                def unit(i, j):
                    c, part = j // per_chunk, j % per_chunk
                    landed(s.u0, i, j)
                    if part == 0:
                        bank_free(s, i, c, SLOTS // per_chunk)
                    for k in range(kper):
                        kk = part * kper + k
                        mm = pe.matmul(ps[:, bank(s, c), 0:T], ring[:, slot(s.u0, j), k * P:(k + 1) * P], rhs(kk),
                                       start=kk == 0, stop=kk == nk - 1)
                        if k == kper - 1:
                            mm.then_inc(s_used, 1)

                full = s.units // SLOTS if s.units >= 2 * SLOTS else 0
                if full:
                    with pe.Fori(0, full) as i:
                        for j in range(SLOTS):
                            unit(i, j)
                for j in range(full * SLOTS, s.units):
                    unit(0, j)

            def ada(s, l):
                begin(s)
                for g in range(s.chunks):
                    bank_free(s, 0, g)
                    for j in range(8):
                        landed(s.u0, 0, 8 * g + j)
                        for k in range(KC):
                            mm = pe.matmul(ps[:, bank(s, g), 2 * j:2 * j + 2],
                                           ring[:, slot(s.u0, j), k * P:(k + 1) * P], scond[:, k, :],
                                           start=k == 0, stop=k == KC - 1)
                        mm.then_inc(s_used, 1)

            def tokens(s, lhs, ntile):
                begin(s)
                c = 0
                for g in range(2):
                    for j in range(4):
                        landed(s.u0, 0, 4 * g + j)
                    s0 = slot(s.u0, 4 * g)
                    for q in range(ntile):
                        bank_free(s, 0, c)
                        for k in range(KC):
                            mm = pe.matmul(ps[:, bank(s, c), 0:512], lhs(k, q),
                                           ring[:, s0:s0 + 4, k * P:(k + 1) * P], start=k == 0, stop=k == KC - 1)
                        computed(s, c, mm)
                        c += 1

            def norm_stat(name):
                N = NORM[name]
                nk, nt = N["nk"], N["T"] // P
                pe.wait_ge(s_sqA, N["n"] + 1)
                if nk == KC:
                    pe.wait_ge(s_sqD, N["sd"])
                inv = const("inv")[:, N["inv"]:N["inv"] + 1]
                if name == "sub":
                    for h in range(KC):
                        for q in range(nt):
                            mm = pe.matmul(ps[:, 4, 4 * h + q:4 * h + q + 1], sq[:, h, q * P:(q + 1) * P], inv,
                                           start=True, stop=True)
                else:
                    for q in range(nt):
                        for k in range(nk):
                            mm = pe.matmul(ps[:, 4, q:q + 1], sq[:, k, q * P:(q + 1) * P], inv,
                                           start=k == 0, stop=k == nk - 1)
                mm.then_inc(s_stat, 1)

            diags = [0]

            def norm_bc(name):
                N = NORM[name]
                for _ in range(KC if name == "sub" else 1):
                    diags[0] += 1
                    b = 5 + diags[0] % 2
                    pe.wait_ge(s_diag, diags[0])
                    pe.matmul(ps[:, b, 0:N["T"]], ones, diag[:, 0:N["T"] // P, :], start=True,
                              stop=True).then_inc(s_bc, 1)

            def attention(name):
                a, b, _, _ = JOBS[name]

                def scores(j):
                    J, bf = jobs[j], j % 2
                    if j >= 2:
                        pe.wait_ge(s_exp, j - 1)
                    for p in range(2):
                        for n, (l, r, o, w) in enumerate(J["scores"][p]):
                            mm = pe.matmul(ps[:, 4 + 2 * bf + p, o:o + w], l, r, start=n == 0,
                                           stop=n == len(J["scores"][p]) - 1)
                    mm.then_inc(s_scores, 1)

                def turn(j):
                    J, bf = jobs[j], j % 2
                    pe.wait_ge(s_prob, j + 1)
                    for g, blocks in enumerate(J["groups"]):
                        G = J["g0"] + g
                        if G >= 2:
                            pe.wait_ge(s_ptsb, G - 1)
                        for n, (p, k) in enumerate(blocks):
                            src = PR[:, bf, k * P:(k + 1) * P] if p is None else E[:, bf, p, k * P:(k + 1) * P]
                            mm = pe.transpose(ps[:, G % 2, n * P:(n + 1) * P], src, ident)
                        mm.then_inc(s_pt, 1)

                def values(j):
                    J = jobs[j]
                    if J["first"] and J["o"] >= 2:
                        pe.wait_ge(s_osb, J["o"] - 1)
                    for g, mms in enumerate(J["pv"]):
                        G = J["g0"] + g
                        pe.wait_ge(s_ptsb, G + 1)
                        for o, m, c, v, r, w, first, last in mms:
                            mm = pe.matmul(ps[o:o + m, 2 + J["o"] % 2, c:c + w], v, PT[:, G % 4, r:r + w],
                                           start=first, stop=last)
                        mm.then_inc(s_pv, 1)

                for i in range(a, b + 2):
                    if i < b:
                        scores(i)
                    if a <= i - 1 < b:
                        turn(i - 1)
                    if a <= i - 2 < b:
                        values(i - 2)

            def all_read(s):
                if s.a1:
                    pe.wait_ge(s_freeA, s.a1)
                if s.d1:
                    pe.wait_ge(s_freeD, s.d1)

            def rope(s, srcs, rot):
                begin(s)
                for c, pair in enumerate(srcs):
                    bank_free(s, 0, c)
                    for n, a in enumerate(pair):
                        mm = pe.matmul(ps[:, bank(s, c), n * LAT:(n + 1) * LAT], rot, a, start=True, stop=True)
                    computed(s, c, mm)

            pe.wait_ge(s_small, 80)
            pe.wait_ge(s_scond, 1)
            norm_stat("n0")
            ada(st["ada0a"], 0)
            norm_bc("n0")
            pe.wait_ge(s_nA, NORM["n0"]["na"])
            rows(st["q0"], lambda k: xn[:, k, :], TOK)
            rows(st["k0"], lambda k: xn[:, k, :], TOK)
            tokens(st["v0"], lambda k, q: xn[:, k, q * P:(q + 1) * P], 4)
            rope(st["rope0"], [[qk[:, 2 * c, lat], qk[:, 2 * c + 1, lat]] for c in range(8)], const("rot_a"))
            ada(st["ada0b"], 0)
            all_read(st["ada0b"])
            attention("da")
            norm_stat("sub")
            norm_bc("sub")
            pe.wait_ge(s_nD, NORM["sub"]["nd"])
            rows(st["wo0"], lambda k: xn[:, k, :], TOK)
            ada(st["ada1a"], 1)
            norm_stat("n1")
            ada(st["ada1b"], 1)
            norm_bc("n1")
            pe.wait_ge(s_nA, NORM["n1"]["na"])
            rows(st["gu0"], lambda k: xn[:, k, :], TOK)
            pe.wait_ge(s_freeD, st["gu0"].d1)
            rows(st["down0"], lambda k: hid[:, k, :], TOK, nk=FC, per_chunk=2)
            ada(st["ada1c"], 1)
            norm_stat("n2")
            ada(st["ada1d"], 1)
            norm_bc("n2")
            pe.wait_ge(s_nA, NORM["n2"]["na"])
            rows(st["q1"], lambda k: xn[:, k, lat], LAT)
            rows(st["k1"], lambda k: xn[:, k, :], TOK)
            tokens(st["v1"], lambda k, q: xn[:, k, q * P:(q + 1) * P], 4)
            ada(st["ada1e"], 1)
            all_read(st["ada1e"])
            pe.wait_ge(s_biasm, 1)
            attention("na")
            pe.wait_ge(s_osb, JOBS["na"][3])
            rows(st["wo1"], lambda k: x2[:, k, :], LAT)
            norm_stat("n3")
            norm_bc("n3")
            pe.wait_ge(s_nA, NORM["n3"]["na"])
            rows(st["gu1"], lambda k: x2[:, k, :], LAT)
            norm_stat("nmem")
            norm_bc("nmem")
            pe.wait_ge(s_freeD, st["gu1"].d1)
            rows(st["down1"], lambda k: hid[:, k, 0:LAT], LAT, nk=FC, per_chunk=2)
            pe.wait_ge(s_nD, NORM["nmem"]["nd"])
            rows(st["memk"], lambda k: memT[:, k, :], LAT)
            norm_stat("nf")
            norm_bc("nf")
            tokens(st["memv"], lambda k, q: memT[:, k, q * P:(q + 1) * P], 2)
            norm_stat("nmix")
            norm_bc("nmix")
            pe.wait_ge(s_nD, NORM["nmix"]["nd"])
            rows(st["win"], lambda k: x2[:, k, :], LAT)
            rows(st["wing"], lambda k: x2[:, k, :], LAT)
            rows(st["winr"], lambda k: x2[:, k, :], LAT)
            for name in ("nq", "nkv"):
                norm_stat(name)
                norm_bc(name)
            pe.wait_ge(s_nD, NORM["nkv"]["nd"])
            small_rows = [("uq", 4, 2, lambda k: u[:, 24 + k, :]), ("uk", 8, 1, lambda k: u[:, 26, :])]
            for name, mper, nk, rhs in small_rows:
                s = st[name]
                begin(s)
                for c in range(s.chunks):
                    j = c // mper
                    if c % mper == 0:
                        landed(s.u0, 0, j)
                    bank_free(s, 0, c)
                    for k in range(nk):
                        n = (c % mper) * nk + k
                        mm = pe.matmul(ps[:, bank(s, c), 0:LAT], ring[:, slot(s.u0, j), n * P:(n + 1) * P], rhs(k),
                                       start=k == 0, stop=k == nk - 1)
                    computed(s, c, mm)
            s = st["uv"]
            begin(s)
            landed(s.u0, 0, 0)
            for c in range(4):
                computed(s, c, pe.matmul(ps[:, bank(s, c), 0:512], u[:, 26, (c // 2) * P:(c // 2 + 1) * P],
                                         ring[:, slot(s.u0, 0), (c % 2) * 512:(c % 2 + 1) * 512], start=True,
                                         stop=True))
            rope(st["rope2"], [[mq[:, 8, :], mq[:, 9, :]], [mq[:, 10, :], mq[:, 11, :]], [u[:, 43, :]]],
                 const("rot_b"))
            all_read(st["rope2"])
            attention("mla")
            pe.wait_ge(s_osb, JOBS["mla"][3])
            pe.wait_ge(s_conv, 1)
            rows(st["conv"], lambda k: u[:, 8 + k, :], LAT)
            rows(st["mla"], lambda k: x2[:, k, :], LAT)
            pe.wait_ge(s_freeD, st["mla"].d1)
            rows(st["mix"], lambda k: u[:, 16 + k, :], LAT)
            norm_stat("nq2")
            norm_bc("nq2")
            pe.wait_ge(s_nD, NORM["nq2"]["nd"])
            rows(st["memq"], lambda k: x2[:, k, :], LAT)
            all_read(st["memq"])
            attention("mem")
            pe.wait_ge(s_osb, JOBS["mem"][3])
            rows(st["memo"], lambda k: x2[:, k, :], LAT)
            norm_stat("nmoe")
            norm_bc("nmoe")
            pe.wait_ge(s_nD, NORM["nmoe"]["nd"])
            for q in range(2):
                for k in range(KC):
                    mm = pe.matmul(ps[:, 6, NE * q:NE * q + NE], x2[:, k, q * P:(q + 1) * P], wr[:, k, :],
                                   start=k == 0, stop=k == KC - 1)
            mm.then_inc(s_moe, 1)
            for q in range(2):
                for k in range(KC):
                    mm = pe.transpose(ps[:, 2 * q + k // 4, (k % 4) * P:(k % 4 + 1) * P],
                                      x2[:, k, q * P:(q + 1) * P], ident)
            mm.then_inc(s_moe, 1)
            pe.wait_ge(s_moeD, 1)
            for q in range(2):
                mm = pe.transpose(ps[0:NE, 7, q * P:(q + 1) * P], aff[:, q, :], ident)
            mm.then_inc(s_moe, 1)
            pe.wait_ge(s_moeD, 2)
            for a in range(2):
                mm = pe.matmul(ps[:, 4 + a, :], ones[0:NE, :], spread[:, a, :], start=True, stop=True)
            mm.then_inc(s_moe, 1)
            pe.wait_ge(s_moeD, 3)
            pe.wait_ge(s_moeA, 1)
            for k in range(KC):
                if k >= 4:
                    pe.wait_ge(s_moeA, 2 + k - 4)
                for q in range(2):
                    mm = pe.matmul(ps[:, k % 4, :], hs[:, q, k * P:(k + 1) * P], sel[:, q, :], start=q == 0,
                                   stop=q == 1)
                mm.then_inc(s_moe, 1)
            pe.wait_ge(s_moeD, 4)
            for g in range(4):
                for q in range(2):
                    mm = pe.transpose(ps[:, 6 + g // 2, (g % 2) * LAT + q * P:(g % 2) * LAT + (q + 1) * P],
                                      gsel[:, q, g * P:(g + 1) * P], ident)
            mm.then_inc(s_moe, 1)

            u0 = st["scatter"].expert_unit

            def expert(e):
                pe.wait_ge(s_xe, e + 1)
                for part, rhs in enumerate((xe, xe, he)):
                    if part == 2:
                        pe.wait_ge(s_he, e + 1)
                    for j in range(8):
                        n = 8 * part + j
                        pe.wait_ge(s_land[(u0 + n) % SLOTS], e * 48 + 16 * ((u0 + n) // SLOTS + 1))
                        for k in range(KC):
                            mm = pe.matmul(ps[:, part, j * CAP:(j + 1) * CAP],
                                           ring[:, (u0 + n) % SLOTS, k * P:(k + 1) * P], rhs[:, k, :],
                                           start=k == 0, stop=k == KC - 1)
                        mm.then_inc(s_used, 1)

            with pe.Fori(0, NE - 1) as e:
                expert(e)
            expert(NE - 1)
            pe.wait_ge(s_yT, NE)
            pe.wait_ge(s_moeD, 5)
            for g in range(4):
                for k in range(KC):
                    mm = pe.transpose(ps[:, 2 * (g % 2) + 4 * (g // 2) + k // 4, (k % 4) * P:(k % 4 + 1) * P],
                                      yT[:, k, g * P:(g + 1) * P], ident)
                mm.then_inc(s_moe, 1)
            s = st["scatter"]
            for c in range(KC):
                if c == 0:
                    pe.wait_ge(s_moeA, 9 + 4)
                bank_free(s, 0, c)
                for g in range(4):
                    mm = pe.matmul(ps[:, bank(s, c), 0:LAT], yo[:, g, c * P:(c + 1) * P], gT[:, g, :],
                                   start=g == 0, stop=g == 3)
                computed(s, c, mm)
            norm_stat("nout")
            norm_bc("nout")

        def chunk_ready(eng, s, i, c, per=0):
            which, n = s.raises(c)
            eng.wait_ge(s_used if which == "used" else s_chunk, i * (per * s.units // s.chunks) + n)

        READY = {
            "n0": [(s_small, 80)], "sub": [(s_osb, JOBS["da"][3])], "n1": [(s_freeD, st["wo0"].d1)],
            "n2": [(s_freeD, st["down0"].d1)], "n3": [(s_freeD, st["wo1"].d1)], "nmem": [(s_mem, 16)],
            "nf": [(s_freeD, st["down1"].d1)], "nmix": [(s_nD, NORM["nf"]["nd"])],
            "nq": [(s_freeA, st["winr"].a1)], "nkv": [(s_freeA, st["winr"].a1)],
            "nq2": [(s_freeD, st["mix"].d1)], "nmoe": [(s_freeD, st["memo"].d1)],
            "nout": [(s_freeD, st["scatter"].d1)],
        }

        @block.scalar
        def _(act):
            steps = Steps(act, c_act)

            def squares(name):
                N = NORM[name]
                n = 4 if N["nk"] == KC else N["nk"]
                for sm, v in READY[name]:
                    act.wait_ge(sm, v)
                if N["n"]:
                    act.wait_ge(s_stat, N["n"])
                act.activation(sq[:, 0:n, 0:N["T"]], N["src"][:, 0:n, :], ACT.Square).then_inc(s_sqA, 1)

            def shift(name):
                N = NORM[name]
                l, part = MODS[N["m"]]
                for k in range(KC):
                    act.wait_ge(s_nD, N["nd"] - KC + k + 1)
                    if N["T"] == TOK:
                        act.activation(xn[:, k, 0:CTX], xn[:, k, 0:CTX], ACT.Identity,
                                       bias=mod[:, l, 8 * part + k, 0:1])
                        dst = xn[:, k, lat]
                    else:
                        dst = xn[:, k, 0:LAT]
                    act.activation(dst, dst, ACT.Identity, bias=mod[:, l, 8 * part + k, 1:2]).then_inc(s_nA, 1)

            def copy_out(s, dst, T=None, scale=1.0, func=ACT.Copy, bias_col=None):
                for c in range(s.chunks):
                    chunk_ready(act, s, 0, c)
                    d = dst(c)
                    src = ps[:, (s.c0 + c) % 4, 0:d.shape[-1]]
                    if bias_col is not None:
                        act.activation(d, src, func, bias=bias_col(c)).then_inc(s_freeA, 1)
                    else:
                        act.activation(d, src, func, scale=scale).then_inc(s_freeA, 1)

            def silu(s, T):
                def one(i, m):
                    chunk_ready(act, s, i, 2 * m, 8)
                    if m >= 2 or not isinstance(i, int):
                        act.wait_ge(s_freeD, i * 4 + (s.d0 + m - 1))
                    act.activation(silu_out[:, m % 2, 0:T], ps[:, (s.c0 + 2 * m) % 4, 0:T],
                                   ACT.Silu).then_inc(s_freeA, 1)
                full = s.units // SLOTS
                with act.Fori(0, full) as i:
                    for m in range(4):
                        one(i, m)
                for m in range(4 * full, FC):
                    one(0, m)

            def exps(j):
                J, bf = jobs[j], j % 2
                act.wait_ge(s_max, j + 1)
                if j >= 2:
                    act.wait_ge(s_pt, groups_before(j - 1))
                for p in range(2):
                    mm = act.activation(E[:, bf, p, 0:J["n"]], ps[:, 4 + 2 * bf + p, 0:J["n"]], ACT.Exp,
                                        bias=anm[:, 2 * bf + p:2 * bf + p + 1], scale=J["scale"],
                                        accum_out=asum[:, 2 * bf + p:2 * bf + p + 1])
                mm.then_inc(s_exp, 1)

            def turned(j):
                J = jobs[j]
                for g, blocks in enumerate(J["groups"]):
                    G, w = J["g0"] + g, len(blocks) * P
                    act.wait_ge(s_pt, G + 1)
                    if G >= 4:
                        act.wait_ge(s_pv, G - 3)
                    act.activation(PT[:, G % 4, 0:w], ps[:, G % 2, 0:w], ACT.Copy).then_inc(s_ptsb, 1)

            def attention(name):
                a, b, _, _ = JOBS[name]
                for i in range(a, b + 1):
                    if i < b:
                        exps(i)
                    if a <= i - 1:
                        turned(i - 1)

            act.wait_ge(s_small, 80)
            act.activation(scond[:, :, :], cond[:, :, :], ACT.Silu).then_inc(s_scond, 1)
            squares("n0")
            act.wait_ge(s_gain, 1)
            act.activation(lams[:, 2:4], lams[:, 0:2], ACT.Exp).then_inc(s_lamex, 1)
            act.wait_ge(s_gain, 2)
            shift("n0")
            copy_out(st["q0"], lambda c: qk[:, c, :], scale=0.125)
            copy_out(st["k0"], lambda c: qk[:, 8 + c, :])
            copy_out(st["v0"], lambda c: vv[:, c % 4, (c // 4) * 512:(c // 4 + 1) * 512])
            attention("da")
            squares("sub")
            squares("n1")
            shift("n1")
            silu(st["gu0"], TOK)
            squares("n2")
            shift("n2")
            copy_out(st["q1"], lambda c: qk[:, c, lat], scale=0.125)
            copy_out(st["k1"], lambda c: qk[:, 8 + c, :])
            copy_out(st["v1"], lambda c: vv[:, c % 4, (c // 4) * 512:(c // 4 + 1) * 512])
            attention("na")
            squares("n3")
            shift("n3")
            silu(st["gu1"], LAT)
            squares("nmem")
            squares("nf")
            copy_out(st["memk"], lambda c: memk[:, c, :])
            copy_out(st["memv"], lambda c: memv[:, c % 2, (c // 2) * 512:(c // 2 + 1) * 512])
            squares("nmix")
            s = st["win"]
            full = s.units // SLOTS
            with act.Fori(0, full) as i:
                for c in range(SLOTS):
                    chunk_ready(act, s, i, c, SLOTS)
                    act.activation(big[:, bass.ds(i * (SLOTS * LAT) + c * LAT, LAT)], ps[:, (s.c0 + c) % 4, 0:LAT],
                                   ACT.Copy).then_inc(s_freeA, 1)
            for c in range(full * SLOTS, s.units):
                chunk_ready(act, s, 0, c)
                act.activation(u[:, c, :], ps[:, (s.c0 + c) % 4, 0:LAT], ACT.Copy).then_inc(s_freeA, 1)
            copy_out(st["wing"], lambda c: u[:, 27 + c, :], func=ACT.Sigmoid, bias_col=lambda c: col("b_gate", c))
            copy_out(st["winr"], lambda c: u[:, 43, :])
            squares("nq")
            squares("nkv")
            copy_out(st["uq"], lambda c: mq[:, c, :])
            copy_out(st["uk"], lambda c: mk[:, c, :])
            copy_out(st["uv"], lambda c: mv[:, c // 2, (c % 2) * 512:(c % 2 + 1) * 512])
            attention("mla")
            squares("nq2")
            copy_out(st["memq"], lambda c: mq[:, c, :])
            attention("mem")
            squares("nmoe")
            act.wait_ge(s_rmax, 1)
            for q in range(2):
                ins = act.activation(aff[:, q, :], ps[:, 6, NE * q:NE * (q + 1)], ACT.Exp,
                                     bias=small[:, 120 + q:121 + q], accum_out=small[:, 122 + q:123 + q])
            ins.then_inc(s_rexp, 1)
            act.wait_ge(s_moe, 2)
            for q in range(2):
                ins = act.activation(hs[:, q, :].rearrange("p (a b) -> p a b", a=2), ps[:, 2 * q:2 * q + 2, :],
                                     ACT.Copy)
            ins.then_inc(s_moeA, 1)
            for k in range(KC):
                act.wait_ge(s_moe, 5 + k)
                act.activation(xg[:, k, :], ps[:, k % 4, :], ACT.Copy).then_inc(s_moeA, 1)
            u0 = st["scatter"].expert_unit

            def expert(e):
                act.wait_ge(s_used, e * 24 + (u0 + 8))
                act.activation(sg, ps[:, 0, 0:8 * CAP], ACT.Silu).then_inc(s_sg, 1)
                act.wait_ge(s_used, e * 24 + (u0 + 24))
                act.activation(yT[:, :, bass.ds(e * CAP, CAP)],
                               ps[:, 2, 0:8 * CAP].rearrange("p (k n) -> p k n", k=KC), ACT.Copy).then_inc(s_yT, 1)

            with act.Fori(0, NE) as e:
                expert(e)
            for g in range(4):
                act.wait_ge(s_moe, 14 + g)
                b = 2 * (g % 2) + 4 * (g // 2)
                act.activation(yo[:, g, :].rearrange("p (a b) -> p a b", a=2), ps[:, b:b + 2, :],
                               ACT.Copy).then_inc(s_moeA, 1)
            squares("nout")

        @block.vector
        def _(dve):
            steps = Steps(dve, c_dve)
            link = steps.link
            neg_lam = lams[:, 5:6]
            gsub = small[:, 124:125]

            def squares(name):
                N = NORM[name]
                for sm, v in READY[name]:
                    dve.wait_ge(sm, v)
                if N["n"]:
                    dve.wait_ge(s_stat, N["n"])
                dve.tensor_tensor(sq[:, 4:8, 0:N["T"]], N["src"][:, 4:8, :], N["src"][:, 4:8, :],
                                  ALU.mult).then_inc(s_sqD, 1)

            def rstd(name, n):
                dve.wait_ge(s_stat, NORM[name]["n"] + 1)
                v, y, z = var[:, 0:n], rs[:, 0:n], tmp[:, 0:n]
                link(dve.tensor_scalar(v, ps[:, 4, 0:n], EPS, None, ALU.add))
                link(dve.tensor_scalar(y.bitcast(I32), v.bitcast(I32), -0.5, float(0x5F3759DF), ALU.mult, ALU.add))
                for _ in range(4):
                    link(dve.tensor_tensor(z, y, y, ALU.mult))
                    link(dve.scalar_tensor_tensor(z, z, -0.5, v, ALU.mult, ALU.mult))
                    link(dve.scalar_tensor_tensor(y, z, 1.5, y, ALU.add, ALU.mult))

            diags = [0]

            def broadcast(r, nt):
                if diags[0]:
                    dve.wait_ge(s_bc, diags[0])
                diags[0] += 1
                dve.tensor_tensor(diag[:, 0:nt, :], ident.unsqueeze(1).to_broadcast([P, nt, P]),
                                  r.unsqueeze(2).to_broadcast([P, nt, P]), ALU.mult).then_inc(s_diag, 1)
                dve.wait_ge(s_bc, diags[0])
                return ps[:, 5 + diags[0] % 2, 0:nt * P]

            def norm(name):
                N = NORM[name]
                nt = N["T"] // P
                rstd(name, nt)
                bc = broadcast(rs[:, 0:nt], nt)
                for k in range(N["nk"]):
                    src, dst = N["src"][:, k, :], N["dst"][:, k, :]
                    if N["m"] is None:
                        ins = dve.scalar_tensor_tensor(dst, src, col(N["g"], k), bc, ALU.mult, ALU.mult)
                    elif N["T"] == TOK:
                        for c, sl in enumerate((slice(0, CTX), lat)):
                            ins = dve.scalar_tensor_tensor(dst[:, sl], src[:, sl], gain[:, N["m"], k, c:c + 1],
                                                           bc[:, sl], ALU.mult, ALU.mult)
                    else:
                        ins = dve.scalar_tensor_tensor(dst, src, gain[:, N["m"], k, 1:2], bc, ALU.mult, ALU.mult)
                    ins.then_inc(s_nD, 1)

            def head_norms():
                rstd("sub", 32)
                link(dve.tensor_scalar(gsub, col("subln"), 1.0 - LAM_INIT, None, ALU.mult))
                for h in range(KC):
                    bc = broadcast(rs[:, 4 * h:4 * h + 4], 4)
                    dve.scalar_tensor_tensor(xn[:, h, :], xn[:, h, :], gsub, bc, ALU.mult, ALU.mult).then_inc(s_nD, 1)

            def ada(s, l, part):
                for g in range(s.chunks):
                    chunk_ready(dve, s, 0, g)
                    a = 8 * (part + g)
                    dve.tensor_tensor(mod[:, l, a:a + 8, :],
                                      ps[:, (s.c0 + g) % 4, 0:16].rearrange("p (m c) -> p m c", c=2),
                                      col("ada_b", 48 * l + a, 8).unsqueeze(2).to_broadcast([P, 8, 2]),
                                      ALU.add).then_inc(s_freeD, 1)

            def gains(m, after, g):
                l, part = MODS[m]
                dve.wait_ge(s_freeD, after.d1)
                dve.scalar_tensor_tensor(gain[:, m, :, :], mod[:, l, 8 * (part + 1):8 * (part + 2), :], 1.0,
                                         col(g, 0, 8).unsqueeze(2).to_broadcast([P, 8, 2]), ALU.add,
                                         ALU.mult).then_inc(s_gain, 1)

            def gated_add(s, l, part, T):
                for c in range(KC):
                    chunk_ready(dve, s, 0, c)
                    b = (s.c0 + c) % 4
                    if T == TOK:
                        dve.scalar_tensor_tensor(hT[:, c, 0:CTX], ps[:, b, 0:CTX], mod[:, l, 8 * part + c, 0:1],
                                                 hT[:, c, 0:CTX], ALU.mult, ALU.add)
                    dve.scalar_tensor_tensor(hT[:, c, lat], ps[:, b, T - LAT:T], mod[:, l, 8 * part + c, 1:2],
                                             hT[:, c, lat], ALU.mult, ALU.add).then_inc(s_freeD, 1)

            def add(s):
                for c in range(KC):
                    chunk_ready(dve, s, 0, c)
                    dve.tensor_tensor(hT[:, c, lat], ps[:, (s.c0 + c) % 4, 0:LAT], hT[:, c, lat],
                                      ALU.add).then_inc(s_freeD, 1)

            def products(s, T):
                def one(i, m):
                    chunk_ready(dve, s, i, 2 * m + 1, 8)
                    dve.wait_ge(s_freeA, i * 4 + (s.a0 + m + 1))
                    dve.tensor_tensor(big[:, bass.ds(i * (4 * TOK) + m * TOK, T)], silu_out[:, m % 2, 0:T],
                                      ps[:, (s.c0 + 2 * m + 1) % 4, 0:T], ALU.mult).then_inc(s_freeD, 1)
                full = s.units // SLOTS
                with dve.Fori(0, full) as i:
                    for m in range(4):
                        one(i, m)
                for m in range(4 * full, FC):
                    one(0, m)

            def rope(s, xs, cos, sin):
                for c, x in enumerate(xs):
                    chunk_ready(dve, s, 0, c)
                    n = x.shape[1]
                    a, b = ropet[:, 2 * (c % 2), 0:n, :], ropet[:, 2 * (c % 2) + 1, 0:n, :]
                    rot = ps[:, (s.c0 + c) % 4, 0:n * LAT].rearrange("p (n t) -> p n t", n=n)
                    dve.tensor_tensor(a, x, cos.unsqueeze(1).to_broadcast([P, n, LAT]), ALU.mult)
                    link(dve.tensor_tensor(b, rot, sin.unsqueeze(1).to_broadcast([P, n, LAT]), ALU.mult))
                    dve.tensor_tensor(x, a, b, ALU.add).then_inc(s_freeD, 1)

            def maxima(j):
                J, bf = jobs[j], j % 2
                dve.wait_ge(s_scores, j + 1)
                m = amax[:, 2 * bf:2 * bf + 2]
                link(dve.tensor_reduce(m, ps[:, 4 + 2 * bf:6 + 2 * bf, 0:J["n"]], AX.X, ALU.max))
                dve.tensor_scalar(anm[:, 2 * bf:2 * bf + 2], m, -J["scale"], None, ALU.mult).then_inc(s_max, 1)

            def normalise(j):
                J, bf = jobs[j], j % 2
                dve.wait_ge(s_exp, j + 1)
                r = arec[:, 2 * bf:2 * bf + 2]
                link(dve.reciprocal(r, asum[:, 2 * bf:2 * bf + 2]))
                n = J["n"]
                if J["da"]:
                    dve.tensor_scalar(r[:, 1:2], r[:, 1:2], neg_lam, None, ALU.mult)
                    link(dve.tensor_scalar(PR[:, bf, 0:n], E[:, bf, 0, 0:n], r[:, 0:1], None, ALU.mult))
                    dve.scalar_tensor_tensor(PR[:, bf, 0:n], E[:, bf, 1, 0:n], r[:, 1:2], PR[:, bf, 0:n], ALU.mult,
                                             ALU.add).then_inc(s_prob, 1)
                else:
                    for p in range(2):
                        ins = dve.tensor_scalar(E[:, bf, p, 0:n], E[:, bf, p, 0:n], r[:, p:p + 1], None, ALU.mult)
                    ins.then_inc(s_prob, 1)

            def outs(j):
                J = jobs[j]
                if J["evac"] is None:
                    return
                dve.wait_ge(s_pv, groups_before(j + 1))
                src = ps[:, 2 + J["o"] % 2, 0:J["out"][2]]
                if len(J["evac"].shape) == 3:
                    src = src.rearrange("p (a t) -> p a t", a=2)
                dve.tensor_copy(J["evac"], src).then_inc(s_osb, 1)

            def attention(name):
                a, b, _, _ = JOBS[name]
                for i in range(a, b + 2):
                    if i < b:
                        maxima(i)
                    if a <= i - 1 < b:
                        normalise(i - 1)
                    if a <= i - 2 < b:
                        outs(i - 2)

            dve.wait_ge(s_lamin, 16)
            v = lamv[:, :, :].rearrange("p (a b) d -> p a b d", b=2)
            pr = small[:, 128:192].rearrange("p (a d) -> p a d", a=1)
            for a in range(2):
                link(dve.tensor_tensor(small[:, 128:192], lamv[:, 2 * a, :], lamv[:, 2 * a + 1, :], ALU.mult))
                ins = dve.tensor_reduce(lams[:, a:a + 1], small[:, 128:192], AX.X, ALU.add)
                if a == 0:
                    link(ins)
            ins.then_inc(s_gain, 1)
            squares("n0")
            ada(st["ada0a"], 0, 0)
            gains(0, st["ada0a"], "mix0")
            dve.wait_ge(s_lamex, 1)
            link(dve.tensor_tensor(lams[:, 4:5], lams[:, 3:4], lams[:, 2:3], ALU.subtract))
            link(dve.tensor_scalar(neg_lam, lams[:, 4:5], -LAM_INIT, None, ALU.add))
            dve.wait_ge(s_gain, 2)
            norm("n0")
            rope(st["rope0"], [qk[:, 2 * c:2 * c + 2, lat] for c in range(8)], const("cos_a"), const("sin_a"))
            ada(st["ada0b"], 0, 2)
            gains(1, st["ada0b"], "ffn0")
            attention("da")
            squares("sub")
            head_norms()
            gated_add(st["wo0"], 0, 2, TOK)
            squares("n1")
            ada(st["ada1a"], 1, 0)
            ada(st["ada1b"], 1, 1)
            gains(2, st["ada1b"], "mix1")
            norm("n1")
            products(st["gu0"], TOK)
            gated_add(st["down0"], 0, 5, TOK)
            squares("n2")
            ada(st["ada1c"], 1, 2)
            ada(st["ada1d"], 1, 3)
            norm("n2")
            ada(st["ada1e"], 1, 4)
            gains(3, st["ada1e"], "ffn1")
            attention("na")
            gated_add(st["wo1"], 1, 2, LAT)
            squares("n3")
            norm("n3")
            products(st["gu1"], LAT)
            squares("nmem")
            norm("nmem")
            gated_add(st["down1"], 1, 5, LAT)
            squares("nf")
            norm("nf")
            squares("nmix")
            norm("nmix")
            norm("nq")
            norm("nkv")
            link(dve.tensor_tensor(u[:, 0:8, :], u[:, 0:8, :], u[:, 16:24, :], ALU.mult))
            for k in range(KC):
                ins = dve.tensor_scalar(u[:, 16 + k, :], u[:, k, :], col("conv_w", 8 + k), col("conv_b", k), ALU.mult,
                                        ALU.add)
            link(ins)
            for tap, o, i in ((0, slice(1, LAT), slice(0, LAT - 1)), (2, slice(0, LAT - 1), slice(1, LAT))):
                for k in range(KC):
                    ins = dve.scalar_tensor_tensor(u[:, 16 + k, o], u[:, k, i], col("conv_w", 8 * tap + k),
                                                   u[:, 16 + k, o], ALU.mult, ALU.add)
                link(ins)
            dve.tensor_tensor(u[:, 8:16, :], u[:, 8:16, :], u[:, 16:24, :], ALU.mult).then_inc(s_conv, 1)
            rope(st["rope2"], [mq[:, 8:10, :], mq[:, 10:12, :], u[:, 43:44, :]], const("cos_b"), const("sin_b"))
            attention("mla")
            s = st["conv"]
            for c in range(KC):
                chunk_ready(dve, s, 0, c)
                dve.tensor_tensor(u[:, c, :], ps[:, (s.c0 + c) % 4, 0:LAT], u[:, 27 + c, :], ALU.mult)\
                   .then_inc(s_freeD, 1)
            s = st["mla"]
            for c in range(KC):
                chunk_ready(dve, s, 0, c)
                link(dve.tensor_tensor(u[:, 16 + c, :], ps[:, (s.c0 + c) % 4, 0:LAT], u[:, 35 + c, :], ALU.mult))
                dve.tensor_tensor(u[:, 16 + c, :], u[:, 16 + c, :], u[:, c, :], ALU.add).then_inc(s_freeD, 1)
            add(st["mix"])
            squares("nq2")
            norm("nq2")
            attention("mem")
            add(st["memo"])
            squares("nmoe")
            norm("nmoe")
            dve.wait_ge(s_moe, 1)
            link(dve.tensor_reduce(small[:, 118:120], ps[:, 6, 0:2 * NE].rearrange("p (q e) -> p q e", q=2), AX.X,
                                   ALU.max))
            dve.tensor_scalar(small[:, 120:122], small[:, 118:120], -1.0, None, ALU.mult).then_inc(s_rmax, 1)
            dve.wait_ge(s_rexp, 1)
            link(dve.reciprocal(small[:, 126:128], small[:, 122:124]))
            dve.tensor_tensor(aff, aff, small[:, 126:128].unsqueeze(2).to_broadcast([P, 2, NE]),
                              ALU.mult).then_inc(s_moeD, 1)
            dve.wait_ge(s_moe, 3)
            link(dve.tensor_copy(affT, ps[0:NE, 7, 0:LAT]))
            for r in range(CAP // 8):
                a = slice(8 * r, 8 * r + 8)
                link(dve.max(top[:, a], affT))
                link(dve.max_index(topi[:, a], top[:, a], affT))
                link(dve.match_replace(affT, top[:, a], affT, -1.0))
            link(dve.tensor_copy(topf, topi))
            blocks = const("experts")[0:NE, :].rearrange("p (e n) -> p e n", e=NE)
            for a, v in enumerate((topf, top)):
                ins = dve.tensor_tensor(spread[:, a, :].rearrange("p (e n) -> p e n", e=NE), blocks,
                                        v.unsqueeze(1).to_broadcast([NE, NE, CAP]), ALU.mult)
            ins.then_inc(s_moeD, 1)
            dve.wait_ge(s_moe, 4)
            for q in range(2):
                ins = dve.tensor_scalar(sel[:, q, :], ps[:, 4, :], const("token")[:, q:q + 1], None, ALU.is_equal)
            ins.then_inc(s_moeD, 1)
            dve.wait_ge(s_moeD, 3)
            for q in range(2):
                ins = dve.tensor_tensor(gsel[:, q, :], ps[:, 5, :], sel[:, q, :], ALU.mult)
            ins.then_inc(s_moeD, 1)
            dve.wait_ge(s_moe, 13)
            dve.tensor_copy(gT.rearrange("p (a g) t -> p a (g t)", a=2), ps[:, 6:8, :]).then_inc(s_moeD, 1)
            dve.wait_ge(s_moeA, 9)
            dve.tensor_copy(xe, xg[:, :, 0:CAP]).then_inc(s_xe, 1)
            u0 = st["scatter"].expert_unit

            def expert(e, last):
                dve.wait_ge(s_sg, e + 1)
                dve.wait_ge(s_used, e * 24 + (u0 + 16))
                dve.tensor_tensor(he.rearrange("p k n -> p (k n)"), sg, ps[:, 1, 0:8 * CAP],
                                  ALU.mult).then_inc(s_he, 1)
                if not last:
                    dve.tensor_copy(xe, xg[:, :, bass.ds(e * CAP + CAP, CAP)]).then_inc(s_xe, 1)

            with dve.Fori(0, NE - 1) as e:
                expert(e, False)
            expert(NE - 1, True)
            add(st["scatter"])
            squares("nout")
            norm("nout")


def _rope_tables(seq, first):
    f = np.float32
    if first:
        half = HD // 2
        freqs = (f(1.0) / (f(10000.0) ** (np.arange(0, half, 2, dtype=f) / f(half)))).astype(f)
        pos = np.arange(seq)
        ar = (pos // GRID_W).astype(f)[:, None] * freqs
        ac = (pos % GRID_W).astype(f)[:, None] * freqs
        ang = np.concatenate([ar, ar, ac, ac], axis=-1)
    else:
        inv = (f(1.0) / (f(10000.0) ** (np.arange(0, HD, 2, dtype=f) / f(HD)))).astype(f)
        a = np.arange(seq, dtype=f)[:, None] * inv
        ang = np.concatenate([a, a], axis=-1)
    ang = np.concatenate([ang, ang], axis=-1).T
    return np.cos(ang).astype(f), np.sin(ang).astype(f)


def _rotation(half):
    m = np.zeros((P, P), np.float32)
    for b in range(0, P, 2 * half):
        for j in range(half):
            m[b + half + j, b + j] = -1.0
            m[b + j, b + half + j] = 1.0
    return m


def _constants():
    c = np.zeros((P, NCONST), np.float32)

    def put(name, v):
        c[:, CONST[name][0]:CONST[name][1]] = v
    put("ident", np.eye(P))
    put("ones", 1.0)
    put("rot_a", _rotation(HD // 4))
    put("rot_b", _rotation(HD // 2))
    for n, first in (("a", True), ("b", False)):
        cos, sin = _rope_tables(LAT, first)
        put("cos_" + n, cos)
        put("sin_" + n, sin)
    q = np.arange(P) % GRID_W
    start = np.clip(q - 8, 0, GRID_W - 16)
    k = np.arange(GRID_W)
    inside = (k[None, :] >= start[:, None]) & (k[None, :] < start[:, None] + 16)
    put("mask", np.where(inside, 0.0, NEG))
    put("inv", np.array([[1.0 / 1024, 1.0 / 256, 1.0 / 128]]))
    put("token", np.arange(P)[:, None] + np.array([[0, P]]))
    e = np.arange(NE * CAP) // CAP
    put("experts", (np.arange(P)[:, None] == e[None, :]).astype(np.float32))
    return c


def _blocks(w):
    K, M = w.shape
    return np.ascontiguousarray(w.reshape(K // P, P, M // P, P).transpose(2, 1, 0, 3)).reshape(M // P, P, K)


def _features(x):
    return np.ascontiguousarray(x.reshape(x.shape[0], -1, P).transpose(2, 1, 0))


def _column(v):
    return v.reshape(-1, P).T


def kernel(**inputs):
    import concourse.bacc as bacc
    from concourse.bass_utils import run_bass_kernel_spmd

    a = {k: np.asarray(v) for k, v in inputs.items()}
    arrays = {
        "consts": _constants(),
        "cond": np.ascontiguousarray(np.stack([a["c_ctx"], a["c"][0]]).reshape(2, KC, P).transpose(2, 1, 0)),
        "ctxT": _features(a["ctx"][0]), "xT": _features(a["x"][0]), "memT": _features(a["mem_2"][0]),
        "lam": np.concatenate([a["da_lambda_q1"], a["da_lambda_k1"], a["da_lambda_q2"], a["da_lambda_k2"]]),
        "rpb": np.ascontiguousarray(a["na_rpb"][0]),
        "wr": np.ascontiguousarray(a["w_router_2"][0].reshape(KC, P, NE).transpose(1, 0, 2)),
    }
    vectors = {
        "mix0": a["norm_mix"][0], "mix1": a["norm_mix"][1], "ffn0": a["norm_ffn"][0], "ffn1": a["norm_ffn"][1],
        "final": a["norm_final"], "mix2": a["norm_mix_g_2"][0], "mem": a["norm_mem_g_2"][0],
        "memkv": a["norm_memkv_g_2"][0], "moe": a["norm_moe_g_2"][0], "final2": a["norm_final_g_2"],
        "qn": a["q_norm_g_2"][0], "kvn": a["kv_norm_g_2"][0], "subln": a["da_subln"][0],
        "conv_w": a["conv_w_2"][0], "conv_b": a["conv_b_2"][0], "b_gate": a["b_gate_2"][0], "ada_b": a["ada_b"],
    }
    arrays["cols"] = np.ascontiguousarray(np.concatenate([_column(vectors[n]) for n, _ in _COLS], axis=1))
    for l in range(2):
        arrays[f"ada{l}"] = _blocks(a["ada_w"][l])
        gu = _blocks(a["ffn_w_gate_up"][l]).reshape(2, FC, P, D)
        arrays[f"gu{l}"] = np.ascontiguousarray(gu.transpose(1, 0, 2, 3)).reshape(2 * FC, P, D)
        arrays[f"down{l}"] = _blocks(a["ffn_w_down"][l]).reshape(KC, P, 2, WIDE).transpose(0, 2, 1, 3)            .reshape(2 * KC, P, WIDE)
    arrays["wqkv0"], arrays["wqkv1"] = _blocks(a["da_wqkv"][0]), _blocks(a["na_wqkv"][0])
    arrays["wo0"], arrays["wo1"] = _blocks(a["da_wo"][0]), _blocks(a["na_wo"][0])
    w = a["w_in_2"][0]
    kr = w[:, 3456:3520]
    arrays["win"] = _blocks(np.concatenate([w[:, 0:3456], w[:, 3520:5568], kr, kr], axis=1))
    wq = a["w_uq_2"][0].reshape(256, MLA_H, 192)
    wq = np.concatenate([wq[:, :, 0:P].reshape(256, -1), wq[:, :, P:].reshape(256, -1)], axis=1)
    arrays["uq"] = np.ascontiguousarray(_blocks(wq).reshape(3, 4, P, 256).transpose(0, 2, 1, 3)).reshape(3, P, D)
    wkv = a["w_ukv_2"][0].reshape(P, MLA_H, 2, P)
    arrays["ukv"] = np.ascontiguousarray(wkv.transpose(2, 0, 1, 3)).reshape(2, P, D)
    for n, src in (("conv_out", "w_conv_out_2"), ("mla_out", "w_mla_out_2"), ("mix_out", "w_mix_out_2"),
                   ("memq", "w_mem_q_2"), ("memkv", "w_mem_kv_2"), ("memo", "w_mem_out_2")):
        arrays[n] = _blocks(a[src][0])
    for n, src in (("gate", "w_exp_gate_2"), ("up", "w_exp_up_2"), ("down", "w_exp_down_2")):
        w = a[src][0].reshape(NE, KC, P, KC, P).transpose(0, 3, 2, 1, 4)
        arrays[n] = np.ascontiguousarray(w).reshape(NE * KC, P, D)

    nc = bacc.Bacc("TRN2", target_bir_lowering=False, num_devices=1)
    t = {n: nc.dram_tensor(f"in_{n}", v.shape, mybir.dt.from_np(v.dtype), kind="ExternalInput").ap()
         for n, v in arrays.items()}
    out = nc.dram_tensor("out_0", (P, KC, LAT), F32, kind="ExternalOutput").ap()
    diffusion_moe_kernel(nc, t, out)
    r = run_bass_kernel_spmd(nc, [{f"in_{n}": v for n, v in arrays.items()}], core_ids=[0])
    got = r.results[0]["out_0"]
    return got.transpose(2, 1, 0).reshape(1, LAT, D)
```

```python
from contextlib import ExitStack

import numpy as np

import concourse.bass as bass
from concourse import mybir

F32 = mybir.dt.float32
I32 = mybir.dt.int32
U32 = mybir.dt.uint32
ALU = mybir.AluOpType
ACT = mybir.ActivationFunctionType
AX = mybir.AxisListType

P = 128
D = 1024
KC = D // P
CTX = 256
LAT = 256
TOK = CTX + LAT
FF = 2816
FC = FF // P
GRID_W = 64
HEADS = 16
HD = 64
RPB_R, RPB_C = 15, 31
NEG = -1e30
EPS = 1e-6
LAM_INIT = 0.8 - 0.6 * float(np.exp(-0.3 * 0))
MLA_H = 8
MEM_H = 4
NE = 16
CAP = 2 * LAT // NE
SLOTS = 8
UNIT = KC * P
WIDE = FC // 2 * P

_COLS = [("mix0", 8), ("mix1", 8), ("ffn0", 8), ("ffn1", 8), ("final", 8), ("mix2", 8), ("mem", 8), ("memkv", 8),
         ("moe", 8), ("qn", 2), ("kvn", 1), ("subln", 1), ("conv_w", 24), ("conv_b", 8),
         ("b_gate", 16), ("ada_b", 96)]
COL, _n = {}, 0
for _name, _w in _COLS:
    COL[_name] = (_n, _n + _w)
    _n += _w
NCOLS = _n

_CONST = [("ident", 128), ("ones", 128), ("rot_a", 128), ("rot_b", 128), ("cos_a", LAT), ("sin_a", LAT),
          ("cos_b", LAT), ("sin_b", LAT), ("mask", GRID_W), ("inv", 3 * 32), ("token", 2), ("halves", 2), ("experts", NE * CAP)]
CONST, _n = {}, 0
for _name, _w in _CONST:
    CONST[_name] = (_n, _n + _w)
    _n += _w
NCONST = _n


class Stage:

    readers = []

    def __init__(self, name, weights, units, chunks, owner, width=UNIT, share=None):
        self.name, self.weights, self.units, self.chunks, self.owner, self.width = (
            name, weights, units, chunks, owner, width)
        self.share = share

    def raises(self, c):
        if self.share is None:
            return "used", self.u0 + (c + 1) * self.units // self.chunks
        cs, us = self.share
        if us and c % cs == cs - 1:
            return "used", self.u0 + (c // cs + 1) * us
        return "chunk", self.k0 + (c - c // cs if us else c) + 1


def plan():
    def ada(l, g):
        return [Stage(f"ada{l}{g}", (f"ada{l}", 16 * g), 16, 1, "A"),
                Stage(f"turn{l}{g}", None, 0, 1, "D", share=(1, 0))]

    stages = [
        *ada(0, 0),
        Stage("q0", ("wqkv0", 0), 8, 8, "A"), Stage("k0", ("wqkv0", 8), 8, 8, "A"),
        Stage("v0", ("wqkv0", 16), 8, 8, "A", share=(4, 4)), Stage("rope0", None, 0, 8, "D", share=(8, 0)),
        *ada(0, 1), *ada(0, 2),
        Stage("wo0", ("wo0", 0), 8, 8, "D"),
        *ada(1, 0),
        Stage("gu0", ("gu0", 0), 2 * FC, 2 * FC, "AD"), Stage("down0", ("down0", 0), 16, 8, "D", WIDE),
        *ada(1, 1),
        Stage("q1", ("wqkv1", 0), 8, 8, "A"), Stage("k1", ("wqkv1", 8), 8, 8, "A"),
        Stage("v1", ("wqkv1", 16), 8, 8, "A", share=(4, 4)),
        *ada(1, 2),
        Stage("wo1", ("wo1", 0), 8, 8, "D"),
        Stage("memk", ("memkv", 0), 8, 8, "A"), Stage("memv", ("memkv", 8), 8, 4, "A", share=(2, 4)),
        Stage("gu1", ("gu1", 0), 2 * FC, 2 * FC, "AD"), Stage("down1", ("down1", 0), 16, 8, "D", WIDE),
        Stage("win", ("win", 0), 27, 27, "A"), Stage("wing", ("win", 27), 16, 16, "A"),
        Stage("winr", ("win", 43), 1, 1, "A"),
        Stage("uq", ("uq", 0), 3, 12, "A", share=(4, 1)), Stage("uk", ("ukv", 0), 1, 8, "A", share=(8, 1)),
        Stage("uv", ("ukv", 1), 1, 4, "A", share=(4, 1)), Stage("rope2", None, 0, 3, "D", share=(3, 0)),
        Stage("conv", ("conv_out", 0), 8, 8, "D"), Stage("mla", ("mla_out", 0), 8, 8, "D"),
        Stage("mix", ("mix_out", 0), 8, 8, "D"),
        Stage("memq", ("memq", 0), 8, 8, "A"), Stage("memo", ("memo", 0), 8, 8, "D"),
        Stage("experts", None, 0, 0, "D"),
    ]
    Stage.readers.clear()
    unit = chunk = a = d = k = 0
    for s in stages:
        s.u0, s.c0, s.a0, s.d0, s.k0 = unit, chunk, a, d, k
        for c in range(s.chunks):
            by = s.owner[c % len(s.owner)]
            Stage.readers.append((by, (a if by == "A" else d) + c // len(s.owner) + 1))
        unit += s.units
        chunk += s.chunks
        a += {"A": s.chunks, "D": 0, "AD": s.chunks // 2}[s.owner]
        d += {"D": s.chunks, "A": 0, "AD": s.chunks // 2}[s.owner]
        s.a1, s.d1, s.c1 = a, d, chunk
        if s.share:
            k += s.chunks - (s.chunks // s.share[0] if s.share[1] else 0)
    return {s.name: s for s in stages}


class Steps:

    def __init__(self, eng, sem):
        self.eng, self.sem, self.n = eng, sem, 0

    def link(self, ins):
        self.n += 1
        ins.then_inc(self.sem, 1)
        self.eng.wait_ge(self.sem, self.n)


def diffusion_moe_kernel(nc, t, out, stop=None):
    st = plan()
    ctx = ExitStack()
    with ctx:
        def sb(name, shape, dt=F32):
            return ctx.enter_context(nc.sbuf_tensor(name, shape, dt))

        def sem(name):
            return ctx.enter_context(nc.semaphore(name))

        ring = sb("ring", [P, SLOTS, WIDE])
        hT = sb("hT", [P, KC, TOK])
        xn = sb("xn", [P, KC, TOK])
        big = sb("big", [P, 12288])
        aux = sb("aux", [P, 11264])
        work = sb("work", [P, 6144])
        cst = sb("cst", [P, NCONST])
        cols = sb("cols", [P, NCOLS])
        cond = sb("cond", [P, KC, 2])
        scond = sb("scond", [P, KC, 32])
        mod = sb("mod", [P, 2, 48, 2])
        gain = sb("gain", [P, 4, KC, 2])
        lamv = sb("lamv", [P, 4, HD])
        lams = sb("lams", [P, 8])
        small = sb("small", [P, 192])
        wr = sb("wr", [P, KC, NE])

        rpb_copies = nc.dram_tensor("rpb_copies", (GRID_W, HEADS * RPB_R * RPB_C), F32, kind="Internal").ap()
        ps = ctx.enter_context(nc.psum_tensor("ps", [P, 8, 512], F32))

        def const(name):
            a, b = CONST[name]
            return cst[:, a:b]

        def col(name, k=0, n=1):
            a = COL[name][0] + k
            return cols[:, a:a + n]

        ident, ones = const("ident"), const("ones")
        thirty = sb("thirty", [P, 1])
        lat = slice(CTX, TOK)
        sq = work[:, 0:KC * TOK].rearrange("p (k t) -> p k t", k=KC)
        diag = work[:, 4096:4608].rearrange("p (a b) -> p a b", b=P)
        var, rs, tmp = small[:, 0:32], small[:, 32:64], small[:, 64:96]
        qk = big[:, 0:16 * TOK].rearrange("p (c t) -> p c t", c=16)
        vv = big[:, 8192:12288].rearrange("p (k d) -> p k d", k=4)
        hid = big[:, 0:FC * TOK].rearrange("p (k t) -> p k t", k=FC)
        stats = work[:, 4608:5120]
        stats2 = work[:, 5120:6144].rearrange("p (b t) -> p b t", b=2)
        silu_out = work[:, 5120:6144].rearrange("p (b t) -> p b t", b=2)
        ropet = work[:, 0:2048].rearrange("p (b c t) -> p b c t", b=4, c=2)
        bias = aux[:, 0:8192].rearrange("p (q h k) -> p q h k", q=2, h=HEADS)
        u = big[:, 0:44 * LAT].rearrange("p (c t) -> p c t", c=44)
        mq = aux[:, 0:12 * LAT].rearrange("p (c t) -> p c t", c=12)
        mk = aux[:, 3072:5120].rearrange("p (c t) -> p c t", c=8)
        mv = aux[:, 5120:7168].rearrange("p (k d) -> p k d", k=2)
        memk = aux[:, 7168:9216].rearrange("p (c t) -> p c t", c=8)
        memv = aux[:, 9216:11264].rearrange("p (k d) -> p k d", k=2)
        x2 = xn[:, :, 0:LAT]
        h2 = hT[:, :, lat]
        memT = xn[:, :, lat]
        E = work[:, 0:3072].rearrange("p (b c n) -> p b c n", b=3, c=2)
        PT = work[:, 3072:5120].rearrange("p (b n) -> p b n", b=4)
        amax, anm = small[:, 96:100], small[:, 100:104]
        asum, arec = small[:, 104:108], small[:, 108:112]
        hs = big[:, 0:2048].rearrange("p (s d) -> p s d", s=2)
        sel = big[:, 2048:3072].rearrange("p (s n) -> p s n", s=2)
        gsel = big[:, 3072:5120].rearrange("p (s e h n) -> p s e h n", s=2, e=NE, h=2)
        xg = big[:, 5120:9216].rearrange("p (k n) -> p k n", k=KC)
        xe = big[:, 9216:9728].rearrange("p (k n) -> p k n", k=KC)
        gT = aux[:, 0:2048].rearrange("p (g t) -> p g t", g=NE // 2)
        gx = aux[:, 2048:2560].rearrange("p (h t) -> p h t", h=2)
        sg, hp = aux[:, 2560:3072], aux[:, 3072:3584]
        hTe = aux[:, 3584:4096].rearrange("p (c n) -> p c n", c=4)
        ye = aux[:, 4096:4608]
        grow = aux[:, 4608:5632]
        otok = aux[:, 5632:7680].rearrange("p (q d) -> p q d", q=2)
        aff = big[:, 9984:10016].rearrange("p (s e) -> p s e", s=2)
        affT = big[0:NE, 10240:10496]
        top = big[0:NE, 10496:10528]
        topi = big[0:NE, 10528:10560].bitcast(U32)
        topf = big[0:NE, 10560:10592]
        spread = big[0:NE, 10592:11616].rearrange("p (a n) -> p a n", a=2)

        s_small = sem("small_inputs_loaded")
        s_bias = sem("rpb_loaded")
        s_copies = sem("rpb_copied")
        s_biasm = sem("bias_masked")
        s_mem = sem("mem_loaded")
        s_land = [sem(f"unit_landed_{i}") for i in range(SLOTS)]
        s_used = sem("unit_used")
        s_chunk = sem("chunk_computed")
        s_freeA = sem("chunk_read_by_scalar")
        s_freeD = sem("chunk_read_by_vector")
        s_grow = sem("final_weight_loaded")
        s_acopy = sem("group_sums_in_sbuf")
        s_part = sem("group_sums")
        s_scond = sem("silu_of_cond")
        s_gain = sem("gains")
        s_lamin = sem("lambda_sums")
        s_lamex = sem("lambda_exps")
        s_sqA = sem("squares_by_scalar")
        s_sqD = sem("squares_by_vector")
        s_stat = sem("mean_squares")
        s_diag = sem("rstd_diagonals")
        s_bc = sem("rstd_broadcast")
        s_nD = sem("normed_by_vector")
        s_nA = sem("shifted_by_scalar")
        s_scores = sem("scores")
        s_max = sem("score_max")
        s_exp = sem("exps")
        s_prob = sem("probs")
        s_pt = sem("probs_transposed")
        s_ptsb = sem("probs_transposed_in_sbuf")
        s_pv = sem("heads_out")
        s_osb = sem("heads_out_in_sbuf")
        s_conv = sem("conv_ready")
        s_rmax = sem("router_max")
        s_rexp = sem("router_exp")
        s_moe = sem("moe_pe")
        s_moeD = sem("moe_vector")
        s_moeA = sem("moe_scalar")
        s_sg = sem("expert_silu")
        s_he = sem("expert_hidden")
        s_xe = sem("expert_tokens")
        s_gx = sem("expert_gates_staged")
        s_hturn = sem("expert_hidden_turned")
        s_hT = sem("expert_hidden_turned_in_sbuf")
        s_ye = sem("expert_out_in_sbuf")
        s_scat = sem("expert_out_scattered")
        s_ssq = sem("output_squares")
        s_res = sem("output_rows")
        s_out = sem("output_stored")
        c_dve = sem("vector_steps")
        c_act = sem("scalar_steps")
        c_pool = sem("pool_steps")

        norms = [
            ("n0", hT[:, :, :], xn[:, :, :], KC, TOK, "mix0", 0, 0),
            ("sub", xn[:, :, :], xn[:, :, :], KC, TOK, "subln", 2, None),
            ("n1", hT[:, :, :], xn[:, :, :], KC, TOK, "ffn0", 0, 1),
            ("n2", hT[:, :, :], xn[:, :, :], KC, TOK, "mix1", 0, 2),
            ("nmem", memT, memT, KC, LAT, "memkv", 0, None),
            ("n3", h2, x2, KC, LAT, "ffn1", 0, 3),
            ("nf", h2, h2, KC, LAT, "final", 0, None),
            ("nmix", h2, x2, KC, LAT, "mix2", 0, None),
            ("nq", u[:, 24:26, :], u[:, 24:26, :], 2, LAT, "qn", 1, None),
            ("nkv", u[:, 26:27, :], u[:, 26:27, :], 1, LAT, "kvn", 2, None),
            ("nq2", h2, x2, KC, LAT, "mem", 0, None),
            ("nmoe", h2, x2, KC, LAT, "moe", 0, None),
        ]
        NORM, nd, na, sd = {}, 0, 0, 0
        for n, (name, src, dst, nk, T, g, inv, m) in enumerate(norms):
            nd += nk
            sd += nk == KC
            na += nk if m is not None else 0
            NORM[name] = dict(n=n, src=src, dst=dst, nk=nk, T=T, g=g, inv=inv, m=m, nd=nd, na=na, sd=sd)
        MODS = [(0, 0), (0, 3), (1, 0), (1, 3)]

        def da_jobs():
            for h in range(8):
                for q in range(4):
                    n = CTX if q < 2 else TOK
                    yield dict(
                        n=n, da=True, scale=1.0,
                        scores=[[(qk[64 * c:64 * c + 64, h, q * P:q * P + P], qk[64 * c:64 * c + 64, 8 + h, 0:n], 0, n)]
                                for c in range(2)],
                        groups=[[(None, k) for k in range(n // P)]],
                        pv=[[(0, P, q * P, vv[:, k, h * P:h * P + P], k * P, P, k == 0, k == n // P - 1)
                             for k in range(n // P)]],
                        first=q == 0, evac=xn[:, h, :] if q == 3 else None, out=(0, P, TOK))

        def na_jobs():
            for h in range(HEADS):
                o, c = 64 * (h % 2), h // 2
                yield dict(
                    n=TOK, da=False, scale=1.0,
                    scores=[[(qk[o:o + 64, c, CTX + p * P:CTX + p * P + P], qk[o:o + 64, 8 + c, :], 0, TOK),
                             (ident, bias[:, p, h, :], CTX, LAT)] for p in range(2)],
                    groups=[[(p, 2 * g + k) for k in range(2) for p in range(2)] for g in range(2)],
                    pv=[[(o, 64, 0, vv[:, 2 * g + k, h * 64:h * 64 + 64], k * 256, 256, g + k == 0, g + k == 2)
                         for k in range(2)] for g in range(2)],
                    first=h % 2 == 0, evac=xn[:, c, 0:LAT] if h % 2 else None, out=(0, P, LAT))

        def mla_jobs():
            for h in range(MLA_H):
                o = 64 * (h % 2)
                yield dict(
                    n=LAT, da=False, scale=float(192 ** -0.5),
                    scores=[[(mq[:, h, p * P:p * P + P], mk[:, h, :], 0, LAT),
                             (mq[o:o + 64, 8 + h // 2, p * P:p * P + P], u[o:o + 64, 43, :], 0, LAT)]
                            for p in range(2)],
                    groups=[[(p, k) for k in range(2) for p in range(2)]],
                    pv=[[(0, P, 0, mv[:, k, h * P:h * P + P], k * 256, 256, k == 0, k == 1) for k in range(2)]],
                    first=True, evac=x2[:, h, :], out=(0, P, LAT))

        def mem_jobs():
            for h in range(MEM_H):
                yield dict(
                    n=LAT, da=False, scale=1.0 / 16.0,
                    scores=[[(mq[:, 2 * h + k, p * P:p * P + P], memk[:, 2 * h + k, :], 0, LAT) for k in range(2)]
                            for p in range(2)],
                    groups=[[(p, k) for k in range(2) for p in range(2)]],
                    pv=[[(0, P, 256 * e, memv[:, k, h * 256 + e * P:h * 256 + e * P + P], k * 256, 256, k == 0, k == 1)
                         for e in range(2) for k in range(2)]],
                    first=True, evac=x2[:, 2 * h:2 * h + 2, :], out=(0, P, 2 * LAT))

        JOBS, jobs, job_groups, job_outs = {}, [], [], []
        for name, made in (("da", da_jobs()), ("na", na_jobs()), ("mla", mla_jobs()), ("mem", mem_jobs())):
            a = len(jobs)
            for j in made:
                j["g0"] = sum(job_groups)
                j["o"] = sum(job_outs)
                job_groups.append(len(j["groups"]))
                job_outs.append(1 if j["evac"] is not None else 0)
                jobs.append(j)
            JOBS[name] = (a, len(jobs), sum(job_groups), sum(job_outs))
        g_end = sum(job_groups)

        def groups_before(j):
            return jobs[j]["g0"] if j < len(jobs) else g_end

        block = ctx.enter_context(nc.Block())

        @block.sync
        def _(sp):
            sp.dma_start(cst[:, :], t["consts"]).then_inc(s_small, 16)
            sp.dma_start(cond[:, :, :], t["cond"]).then_inc(s_small, 16)
            sp.dma_start(cols[:, :], t["cols"]).then_inc(s_small, 16)
            sp.dma_start(hT[:, :, 0:CTX], t["ctxT"]).then_inc(s_small, 16)
            sp.dma_start(hT[:, :, lat], t["xT"]).then_inc(s_small, 16)

            def stream(src, u0, off, n, width):
                full = n // SLOTS if n > 3 * SLOTS and u0 >= SLOTS else 0

                def load(i, j):
                    s = (u0 + j) % SLOTS
                    if u0 + j >= SLOTS or not isinstance(i, int):
                        sp.wait_ge(s_used, i * SLOTS + (u0 + j - SLOTS + 1))
                    sp.dma_start(ring[:, s, 0:width], src[i * SLOTS + (off + j)]).then_inc(s_land[s], 16)

                if full:
                    with sp.Fori(0, full) as i:
                        for j in range(SLOTS):
                            load(i, j)
                for j in range(full * SLOTS, n):
                    load(0, j)

            for s in st.values():
                if s.units:
                    stream(t[s.weights[0]], s.u0, s.weights[1], s.units, s.width)
            u0 = st["experts"].u0
            with sp.Fori(0, NE // 2) as pair:
                for part, name in enumerate(("gate", "up", "down")):
                    for j in range(16):
                        n = 16 * part + j
                        s = (u0 + n) % SLOTS
                        sp.wait_ge(s_used, pair * 48 + (u0 + n - SLOTS + 1))
                        sp.dma_start(ring[:, s, 0:UNIT],
                                     t[name][pair * 16 + (KC * (j % 2) + j // 2)]).then_inc(s_land[s], 16)
            for q in range(2):
                sp.wait_ge(s_res, q + 1)
                sp.dma_start(out[q], otok[:, q, :]).then_inc(s_out, 16)
            sp.wait_ge(s_out, 32)

        @block.gpsimd
        def _(pool):
            pool.dma_start(lamv[:, :, :].rearrange("p a b -> p (a b)"),
                           bass.AP(t["lam"].tensor, 0, [[0, P], [1, 4 * HD]])).then_inc(s_lamin, 16)
            pool.dma_start(wr[:, :, :], t["wr"]).then_inc(s_bias, 16)
            table = HEADS * RPB_R * RPB_C
            pool.dma_start(rpb_copies, bass.AP(t["rpb"].tensor, 0, [[0, GRID_W], [1, table]])).then_inc(s_copies, 16)
            pool.wait_ge(s_copies, 16)
            for r in range(4):
                for rr in range(4):
                    o = 64 * (r % 2)
                    pool.dma_start(
                        bias[o:o + 64, r // 2, :, rr * GRID_W:(rr + 1) * GRID_W],
                        bass.AP(rpb_copies.tensor, (rr - r + 7) * RPB_C + 15,
                                [[table - 1, GRID_W], [RPB_R * RPB_C, HEADS], [1, GRID_W]])).then_inc(s_bias, 16)
            pool.wait_ge(s_bias, 17 * 16)
            pool.wait_ge(s_small, 80)
            bm = aux[:, 0:8192].rearrange("p (n c) -> p n c", c=GRID_W)
            pool.tensor_tensor(bm, bm, const("mask").unsqueeze(1).to_broadcast([P, P, GRID_W]),
                               ALU.add).then_inc(s_biasm, 1)
            pool.wait_ge(s_used, st["v1"].u0 + 8)
            pool.dma_start(memT, t["memT"]).then_inc(s_mem, 16)
            pool.wait_ge(s_used, st["mix"].u0)
            pool.dma_start(grow, bass.AP(t["final2"].tensor, 0, [[0, P], [1, D]])).then_inc(s_grow, 16)

        @block.tensor
        def _(pe):
            def landed(u0, i, j, per=SLOTS):
                pe.wait_ge(s_land[(u0 + j) % SLOTS], i * (16 * per // SLOTS) + 16 * ((u0 + j) // SLOTS + 1))

            def slot(u0, j):
                return (u0 + j) % SLOTS

            def banks_read(s):
                if s.a0:
                    pe.wait_ge(s_freeA, s.a0)
                if s.d0:
                    pe.wait_ge(s_freeD, s.d0)

            def bank_free(s, i, c, per=0):
                if isinstance(i, int):
                    if s.c0 + c >= 4:
                        by, n = Stage.readers[s.c0 + c - 4]
                        pe.wait_ge(s_freeA if by == "A" else s_freeD, n)
                elif s.owner == "AD":
                    base, sm = (s.a0, s_freeA) if c % 2 == 0 else (s.d0, s_freeD)
                    pe.wait_ge(sm, i * (per // 2) + (base + c // 2 - 2 + 1))
                elif s.owner == "A":
                    pe.wait_ge(s_freeA, i * per + (s.a0 + c - 3))
                else:
                    pe.wait_ge(s_freeD, i * per + (s.d0 + c - 3))

            def bank(s, c):
                return (s.c0 + c) % 4

            def computed(s, c, mm):
                if s.raises(c)[0] == "used":
                    mm.then_inc(s_used, s.share[1])
                else:
                    mm.then_inc(s_chunk, 1)

            def rows(s, rhs, T, nk=KC, per_chunk=1, ready=None):
                kper = nk // per_chunk
                rest = s.units % SLOTS if s.units > 3 * SLOTS else s.units

                def unit(i, j):
                    c, part = j // per_chunk, j % per_chunk
                    landed(s.u0, i, j)
                    if part == 0:
                        bank_free(s, i, c, SLOTS // per_chunk)
                    for k in range(kper):
                        kk = part * kper + k
                        if ready and j == 0:
                            pe.wait_ge(ready[0], ready[1] + kk)
                        mm = pe.matmul(ps[:, bank(s, c), 0:T], ring[:, slot(s.u0, j), k * P:(k + 1) * P], rhs(kk),
                                       start=kk == 0, stop=kk == nk - 1)
                    mm.then_inc(s_used, 1)

                for j in range(rest):
                    unit(0, j)
                if s.units > rest:
                    if rest < 4:
                        banks_read(s)
                    with pe.Fori(0, (s.units - rest) // SLOTS) as i:
                        for j in range(SLOTS):
                            unit(i, rest + j)

            def ada(l, g):
                s = st[f"ada{l}{g}"]
                bank_free(s, 0, 0)
                for j in range(16):
                    k, part = j // 2, j % 2
                    landed(s.u0, 0, j)
                    for half in range(2):
                        o = 64 * part + 32 * half
                        mm = pe.matmul(ps[o:o + 32, bank(s, 0), :], scond[:, k, :],
                                       ring[:, slot(s.u0, j), half * 512:(half + 1) * 512], start=k == 0,
                                       stop=k == KC - 1)
                    mm.then_inc(s_used, 1)

            def ada_turn(l, g):
                s = st[f"turn{l}{g}"]
                pe.wait_ge(s_freeA, s.a0)
                bank_free(s, 0, 0)
                for c in range(4):
                    mm = pe.transpose(ps[:, bank(s, 0), c * P:(c + 1) * P], stats[:, c * P:(c + 1) * P], ident)
                computed(s, 0, mm)

            def tokens(s, lhs, ntile):
                c = 0
                for g in range(2):
                    for j in range(4):
                        landed(s.u0, 0, 4 * g + j)
                    s0 = slot(s.u0, 4 * g)
                    for q in range(ntile):
                        bank_free(s, 0, c)
                        for k in range(KC):
                            mm = pe.matmul(ps[:, bank(s, c), 0:512], lhs(k, q),
                                           ring[:, s0:s0 + 4, k * P:(k + 1) * P], start=k == 0, stop=k == KC - 1)
                        computed(s, c, mm)
                        c += 1

            def norm_stat(name):
                N = NORM[name]
                nk, nt = N["nk"], N["T"] // P
                pe.wait_ge(s_sqA, N["n"] + 1)
                if nk == KC:
                    pe.wait_ge(s_sqD, N["sd"])
                inv = const("inv")[:, 32 * N["inv"]:32 * N["inv"] + 32]
                if name == "sub":
                    for h in range(KC):
                        o = 32 * (h % 4)
                        mm = pe.matmul(ps[o:o + 32, 5 + h // 4, :], inv, sq[:, h, :], start=True, stop=True)
                    mm.then_inc(s_part, 1)
                    pe.wait_ge(s_acopy, N["n"] + 1)
                    for b in range(2):
                        for q in range(nt):
                            mm = pe.transpose(ps[:, 4 + 3 * b, q * P:(q + 1) * P], stats2[:, b, q * P:(q + 1) * P],
                                              ident)
                    mm.then_inc(s_stat, 1)
                    return
                ng = min(nk, 4)
                for k in range(nk):
                    o = 32 * (k % 4)
                    mm = pe.matmul(ps[o:o + 32, 5, 0:N["T"]], inv, sq[:, k, 0:N["T"]], start=k < 4,
                                   stop=k + 4 >= nk)
                mm.then_inc(s_part, 1)
                pe.wait_ge(s_acopy, N["n"] + 1)
                for q in range(nt):
                    mm = pe.matmul(ps[:, 4, q:q + 1], stats[0:32 * ng, q * P:(q + 1) * P],
                                   thirty[0:32 * ng, :], start=True, stop=True)
                mm.then_inc(s_stat, 1)

            diags = [0]

            def norm_bc(name):
                N = NORM[name]
                for _ in range(KC if name == "sub" else 1):
                    diags[0] += 1
                    b = 6 + diags[0] % 2
                    pe.wait_ge(s_diag, diags[0])
                    pe.matmul(ps[:, b, 0:N["T"]], ones, diag[:, 0:N["T"] // P, :], start=True,
                              stop=True).then_inc(s_bc, 1)

            def attention(name):
                a, b, _, _ = JOBS[name]

                def scores(j):
                    J, bf = jobs[j], j % 2
                    if j >= 2:
                        pe.wait_ge(s_exp, j - 1)
                    for p in range(2):
                        for n, (l, r, o, w) in enumerate(J["scores"][p]):
                            mm = pe.matmul(ps[:, 4 + 2 * bf + p, o:o + w], l, r, start=n == 0,
                                           stop=n == len(J["scores"][p]) - 1)
                    mm.then_inc(s_scores, 1)

                def turn(j):
                    J, bf = jobs[j], j % 3
                    pe.wait_ge(s_prob, j + 1)
                    for g, blocks in enumerate(J["groups"]):
                        G = J["g0"] + g
                        if G >= 2:
                            pe.wait_ge(s_ptsb, G - 1)
                        for n, (p, k) in enumerate(blocks):
                            src = E[:, bf, p or 0, k * P:(k + 1) * P]
                            mm = pe.transpose(ps[:, G % 2, n * P:(n + 1) * P], src, ident)
                        mm.then_inc(s_pt, 1)

                def values(j):
                    J = jobs[j]
                    if J["first"] and J["o"] >= 2:
                        pe.wait_ge(s_osb, J["o"] - 1)
                    for g, mms in enumerate(J["pv"]):
                        G = J["g0"] + g
                        pe.wait_ge(s_ptsb, G + 1)
                        for o, m, c, v, r, w, first, last in mms:
                            mm = pe.matmul(ps[o:o + m, 2 + J["o"] % 2, c:c + w], v, PT[:, G % 4, r:r + w],
                                           start=first, stop=last)
                        mm.then_inc(s_pv, 1)

                for i in range(a, b + 3):
                    if i < b:
                        scores(i)
                    if a <= i - 2 < b:
                        turn(i - 2)
                    if a <= i - 3 < b:
                        values(i - 3)

            def all_read(s):
                if s.a1:
                    pe.wait_ge(s_freeA, s.a1)
                if s.d1:
                    pe.wait_ge(s_freeD, s.d1)

            def rope(s, srcs, rot):
                for c, pair in enumerate(srcs):
                    bank_free(s, 0, c)
                    for n, a in enumerate(pair):
                        mm = pe.matmul(ps[:, bank(s, c), n * LAT:(n + 1) * LAT], rot, a, start=True, stop=True)
                    computed(s, c, mm)

            def heads_read(name):
                pe.wait_ge(s_osb, JOBS[name][3])

            pe.wait_ge(s_small, 80)
            pe.wait_ge(s_scond, 2)
            norm_stat("n0")
            ada(0, 0)
            norm_bc("n0")
            ada_turn(0, 0)
            rows(st["q0"], lambda k: xn[:, k, :], TOK, ready=(s_nA, NORM["n0"]["na"] - KC + 1))
            rows(st["k0"], lambda k: xn[:, k, :], TOK)
            tokens(st["v0"], lambda k, q: xn[:, k, q * P:(q + 1) * P], 4)
            pe.wait_ge(s_freeA, st["k0"].a1)
            rope(st["rope0"], [[qk[:, 2 * c, lat], qk[:, 2 * c + 1, lat]] for c in range(8)], const("rot_a"))
            ada(0, 1)
            ada_turn(0, 1)
            all_read(st["turn01"])
            attention("da")
            heads_read("da")
            ada(0, 2)
            ada_turn(0, 2)
            norm_stat("sub")
            norm_bc("sub")
            rows(st["wo0"], lambda k: xn[:, k, :], TOK, ready=(s_nD, NORM["sub"]["nd"] - KC + 1))
            ada(1, 0)
            ada_turn(1, 0)
            norm_stat("n1")
            norm_bc("n1")
            rows(st["gu0"], lambda k: xn[:, k, :], TOK, ready=(s_nA, NORM["n1"]["na"] - KC + 1))
            pe.wait_ge(s_freeD, st["gu0"].d1)
            rows(st["down0"], lambda k: hid[:, k, :], TOK, nk=FC, per_chunk=2)
            ada(1, 1)
            ada_turn(1, 1)
            norm_stat("n2")
            norm_bc("n2")
            rows(st["q1"], lambda k: xn[:, k, lat], LAT, ready=(s_nA, NORM["n2"]["na"] - KC + 1))
            rows(st["k1"], lambda k: xn[:, k, :], TOK)
            tokens(st["v1"], lambda k, q: xn[:, k, q * P:(q + 1) * P], 4)
            ada(1, 2)
            ada_turn(1, 2)
            norm_stat("nmem")
            norm_bc("nmem")
            pe.wait_ge(s_nD, NORM["nmem"]["nd"])
            all_read(st["turn12"])
            pe.wait_ge(s_biasm, 1)
            attention("na")
            heads_read("na")
            rows(st["wo1"], lambda k: x2[:, k, :], LAT)
            rows(st["memk"], lambda k: memT[:, k, :], LAT)
            norm_stat("n3")
            norm_bc("n3")
            tokens(st["memv"], lambda k, q: memT[:, k, q * P:(q + 1) * P], 2)
            rows(st["gu1"], lambda k: x2[:, k, :], LAT, ready=(s_nA, NORM["n3"]["na"] - KC + 1))
            pe.wait_ge(s_freeD, st["gu1"].d1)
            rows(st["down1"], lambda k: hid[:, k, 0:LAT], LAT, nk=FC, per_chunk=2)
            norm_stat("nf")
            norm_bc("nf")
            norm_stat("nmix")
            norm_bc("nmix")
            rows(st["win"], lambda k: x2[:, k, :], LAT, ready=(s_nD, NORM["nmix"]["nd"] - KC + 1))
            rows(st["wing"], lambda k: x2[:, k, :], LAT)
            rows(st["winr"], lambda k: x2[:, k, :], LAT)
            for name in ("nq", "nkv"):
                norm_stat(name)
                norm_bc(name)
            pe.wait_ge(s_nD, NORM["nkv"]["nd"])
            small_rows = [("uq", 4, 2, lambda k: u[:, 24 + k, :]), ("uk", 8, 1, lambda k: u[:, 26, :])]
            for name, mper, nk, rhs in small_rows:
                s = st[name]
                for c in range(s.chunks):
                    j = c // mper
                    if c % mper == 0:
                        landed(s.u0, 0, j)
                    bank_free(s, 0, c)
                    for k in range(nk):
                        n = (c % mper) * nk + k
                        mm = pe.matmul(ps[:, bank(s, c), 0:LAT], ring[:, slot(s.u0, j), n * P:(n + 1) * P], rhs(k),
                                       start=k == 0, stop=k == nk - 1)
                    computed(s, c, mm)
            s = st["uv"]
            landed(s.u0, 0, 0)
            for c in range(4):
                bank_free(s, 0, c)
                computed(s, c, pe.matmul(ps[:, bank(s, c), 0:512], u[:, 26, (c // 2) * P:(c // 2 + 1) * P],
                                         ring[:, slot(s.u0, 0), (c % 2) * 512:(c % 2 + 1) * 512], start=True,
                                         stop=True))
            pe.wait_ge(s_freeA, st["uq"].a1)
            rope(st["rope2"], [[mq[:, 8, :], mq[:, 9, :]], [mq[:, 10, :], mq[:, 11, :]], [u[:, 43, :]]],
                 const("rot_b"))
            all_read(st["rope2"])
            attention("mla")
            heads_read("mla")
            pe.wait_ge(s_conv, 1)
            rows(st["conv"], lambda k: u[:, 8 + k, :], LAT)
            rows(st["mla"], lambda k: x2[:, k, :], LAT)
            pe.wait_ge(s_freeD, st["mla"].d1)
            rows(st["mix"], lambda k: u[:, 16 + k, :], LAT)
            norm_stat("nq2")
            norm_bc("nq2")
            rows(st["memq"], lambda k: x2[:, k, :], LAT, ready=(s_nD, NORM["nq2"]["nd"] - KC + 1))
            all_read(st["memq"])
            attention("mem")
            heads_read("mem")
            rows(st["memo"], lambda k: x2[:, k, :], LAT)
            norm_stat("nmoe")
            norm_bc("nmoe")
            pe.wait_ge(s_nD, NORM["nmoe"]["nd"])
            for q in range(2):
                for k in range(KC):
                    mm = pe.matmul(ps[:, 6, NE * q:NE * q + NE], x2[:, k, q * P:(q + 1) * P], wr[:, k, :],
                                   start=k == 0, stop=k == KC - 1)
            mm.then_inc(s_moe, 1)
            for q in range(2):
                for k in range(KC):
                    mm = pe.transpose(ps[:, 2 * q + k // 4, (k % 4) * P:(k % 4 + 1) * P],
                                      x2[:, k, q * P:(q + 1) * P], ident)
            mm.then_inc(s_moe, 1)
            pe.wait_ge(s_moeD, 1)
            for q in range(2):
                mm = pe.transpose(ps[0:NE, 7, q * P:(q + 1) * P], aff[:, q, :], ident)
            mm.then_inc(s_moe, 1)
            pe.wait_ge(s_moeD, 2)
            for a in range(2):
                mm = pe.matmul(ps[:, 4 + a, :], ones[0:NE, :], spread[:, a, :], start=True, stop=True)
            mm.then_inc(s_moe, 1)
            pe.wait_ge(s_moeD, 3)
            pe.wait_ge(s_moeA, 1)
            for k in range(KC):
                if k >= 4:
                    pe.wait_ge(s_moeA, 2 + k - 4)
                for q in range(2):
                    mm = pe.matmul(ps[:, k % 4, :], hs[:, q, k * P:(k + 1) * P], sel[:, q, :], start=q == 0,
                                   stop=q == 1)
                mm.then_inc(s_moe, 1)
            pe.wait_ge(s_moeD, 4)
            for g in range(NE // 2):
                for q in range(2):
                    mm = pe.transpose(ps[:, 4 + g // 2, (g % 2) * LAT + q * P:(g % 2) * LAT + (q + 1) * P],
                                      gsel[:, q, 2 * g:2 * g + 2, :, :].rearrange("p e h n -> p (e h n)"), ident)
            mm.then_inc(s_moe, 1)
            pe.wait_ge(s_moeA, 9)
            for q in range(2):
                for k in range(KC):
                    pe.matmul(ps[:, 2 * q + k // 4, (k % 4) * P:(k % 4 + 1) * P], h2[:, k, q * P:(q + 1) * P], ident,
                              start=k % 4 == 0, stop=False, skip_group_check=True)
            pe.wait_ge(s_moeA, 11)

            u0 = st["experts"].u0

            def product(pair, part, lhs):
                for j in range(16):
                    k, e = j // 2, j % 2
                    n = 16 * part + j
                    pe.wait_ge(s_land[(u0 + n) % SLOTS], pair * 96 + 16 * ((u0 + n) // SLOTS + 1))
                    for h in range(2):
                        o = 64 * e + 32 * h
                        mm = pe.matmul(ps[o:o + 32, (4, 5, 7)[part], :], lhs(k, e),
                                       ring[:, (u0 + n) % SLOTS, h * 512:(h + 1) * 512], start=k == 0,
                                       stop=k == KC - 1)
                    mm.then_inc(s_used, 1)

            with pe.Fori(0, NE // 2) as pair:
                pe.wait_ge(s_xe, pair + 1)
                for part in range(2):
                    product(pair, part, lambda k, e: xe[:, k, e * CAP:(e + 1) * CAP])
                pe.wait_ge(s_he, pair + 1)
                for c in range(4):
                    mm = pe.transpose(ps[:, 6, c * P:(c + 1) * P], hp[:, c * P:(c + 1) * P], ident)
                mm.then_inc(s_hturn, 1)
                pe.wait_ge(s_hT, pair + 1)
                product(pair, 2, lambda k, e: hTe[:, k % 4, 64 * e + 32 * (k // 4):64 * e + 32 * (k // 4) + 32])
                pe.wait_ge(s_ye, pair + 1)
                pe.wait_ge(s_gx, pair + 1)
                for q in range(2):
                    for h in range(2):
                        mm = pe.matmul(ps[:, 2 * q + h, :], gx[:, h, q * P:(q + 1) * P], ye, start=False, stop=False,
                                       skip_group_check=True)
                mm.then_inc(s_scat, 1)

        def chunk_ready(eng, s, i, c, per=0):
            which, n = s.raises(c)
            eng.wait_ge(s_used if which == "used" else s_chunk, i * (per * s.units // s.chunks) + n)

        READY = {
            "n0": [(s_small, 80)], "sub": [(s_osb, JOBS["da"][3])], "n1": [(s_freeD, st["wo0"].d1)],
            "n2": [(s_freeD, st["down0"].d1)], "n3": [(s_freeD, st["wo1"].d1)], "nmem": [(s_mem, 16)],
            "nf": [(s_freeD, st["down1"].d1)], "nmix": [(s_nD, NORM["nf"]["nd"])],
            "nq": [(s_freeA, st["winr"].a1)], "nkv": [(s_freeA, st["winr"].a1)],
            "nq2": [(s_freeD, st["mix"].d1)], "nmoe": [(s_freeD, st["memo"].d1)],
        }

        @block.scalar
        def _(act):
            steps = Steps(act, c_act)

            def squares(name):
                N = NORM[name]
                n = 4 if N["nk"] == KC else N["nk"]
                for sm, v in READY[name]:
                    act.wait_ge(sm, v)
                if N["n"]:
                    act.wait_ge(s_stat, N["n"])
                act.activation(sq[:, 0:n, 0:N["T"]], N["src"][:, 0:n, :], ACT.Square).then_inc(s_sqA, 1)

            def group_sums(name):
                N = NORM[name]
                act.wait_ge(s_part, N["n"] + 1)
                if name == "sub":
                    act.activation(stats2, ps[:, 5:7, :], ACT.Copy).then_inc(s_acopy, 1)
                else:
                    g = 32 * min(N["nk"], 4)
                    act.activation(stats[0:g, 0:N["T"]], ps[0:g, 5, 0:N["T"]], ACT.Copy).then_inc(s_acopy, 1)

            def ada_rows(l, g):
                s = st[f"ada{l}{g}"]
                chunk_ready(act, s, 0, 0)
                act.activation(stats, ps[:, s.c0 % 4, :], ACT.Copy).then_inc(s_freeA, 1)

            def shift(name):
                N = NORM[name]
                l, part = MODS[N["m"]]
                for k in range(KC):
                    act.wait_ge(s_nD, N["nd"] - KC + k + 1)
                    if N["T"] == TOK:
                        act.activation(xn[:, k, 0:CTX], xn[:, k, 0:CTX], ACT.Identity,
                                       bias=mod[:, l, 8 * part + k, 0:1])
                        dst = xn[:, k, lat]
                    else:
                        dst = xn[:, k, 0:LAT]
                    act.activation(dst, dst, ACT.Identity, bias=mod[:, l, 8 * part + k, 1:2]).then_inc(s_nA, 1)

            def copy_out(s, dst, T=None, scale=1.0, func=ACT.Copy, bias_col=None):
                for c in range(s.chunks):
                    chunk_ready(act, s, 0, c)
                    d = dst(c)
                    src = ps[:, (s.c0 + c) % 4, 0:d.shape[-1]]
                    if bias_col is not None:
                        act.activation(d, src, func, bias=bias_col(c)).then_inc(s_freeA, 1)
                    else:
                        act.activation(d, src, func, scale=scale).then_inc(s_freeA, 1)

            def silu(s, T):
                def one(i, m):
                    chunk_ready(act, s, i, 2 * m, 8)
                    if m >= 2 or not isinstance(i, int):
                        act.wait_ge(s_freeD, i * 4 + (s.d0 + m - 1))
                    act.activation(silu_out[:, m % 2, 0:T], ps[:, (s.c0 + 2 * m) % 4, 0:T],
                                   ACT.Silu).then_inc(s_freeA, 1)
                for m in range(2):
                    one(0, m)
                with act.Fori(0, (FC - 2) // 4) as i:
                    for m in range(4):
                        one(i, 2 + m)

            def exps(j):
                J, bf = jobs[j], j % 2
                act.wait_ge(s_max, j + 1)
                if j >= 3:
                    act.wait_ge(s_pt, groups_before(j - 2))
                for p in range(2):
                    mm = act.activation(E[:, j % 3, p, 0:J["n"]], ps[:, 4 + 2 * bf + p, 0:J["n"]], ACT.Exp,
                                        bias=anm[:, 2 * bf + p:2 * bf + p + 1], scale=J["scale"],
                                        accum_out=asum[:, 2 * bf + p:2 * bf + p + 1])
                mm.then_inc(s_exp, 1)

            def turned(j):
                J = jobs[j]
                for g, blocks in enumerate(J["groups"]):
                    G, w = J["g0"] + g, len(blocks) * P
                    act.wait_ge(s_pt, G + 1)
                    if G >= 4:
                        act.wait_ge(s_pv, G - 3)
                    act.activation(PT[:, G % 4, 0:w], ps[:, G % 2, 0:w], ACT.Copy).then_inc(s_ptsb, 1)

            def attention(name):
                a, b, _, _ = JOBS[name]
                for i in range(a, b + 2):
                    if i < b:
                        exps(i)
                    if a <= i - 2:
                        turned(i - 2)

            act.wait_ge(s_small, 80)
            act.wait_ge(s_scond, 1)
            act.activation(scond[:, :, 0:2], cond[:, :, :], ACT.Silu).then_inc(s_scond, 1)
            squares("n0")
            group_sums("n0")
            ada_rows(0, 0)
            act.wait_ge(s_gain, 1)
            act.activation(lams[:, 2:4], lams[:, 0:2], ACT.Exp).then_inc(s_lamex, 1)
            act.wait_ge(s_gain, 2)
            shift("n0")
            copy_out(st["q0"], lambda c: qk[:, c, :], scale=0.125)
            copy_out(st["k0"], lambda c: qk[:, 8 + c, :])
            copy_out(st["v0"], lambda c: vv[:, c % 4, (c // 4) * 512:(c // 4 + 1) * 512])
            ada_rows(0, 1)
            attention("da")
            squares("sub")
            ada_rows(0, 2)
            group_sums("sub")
            squares("n1")
            ada_rows(1, 0)
            group_sums("n1")
            shift("n1")
            silu(st["gu0"], TOK)
            squares("n2")
            ada_rows(1, 1)
            group_sums("n2")
            shift("n2")
            copy_out(st["q1"], lambda c: qk[:, c, lat], scale=0.125)
            copy_out(st["k1"], lambda c: qk[:, 8 + c, :])
            copy_out(st["v1"], lambda c: vv[:, c % 4, (c // 4) * 512:(c // 4 + 1) * 512])
            ada_rows(1, 2)
            squares("nmem")
            group_sums("nmem")
            attention("na")
            squares("n3")
            copy_out(st["memk"], lambda c: memk[:, c, :])
            group_sums("n3")
            copy_out(st["memv"], lambda c: memv[:, c % 2, (c // 2) * 512:(c // 2 + 1) * 512])
            shift("n3")
            silu(st["gu1"], LAT)
            squares("nf")
            group_sums("nf")
            squares("nmix")
            group_sums("nmix")
            s = st["win"]
            rest = s.units % SLOTS
            for c in range(rest):
                chunk_ready(act, s, 0, c)
                act.activation(u[:, c, :], ps[:, (s.c0 + c) % 4, 0:LAT], ACT.Copy).then_inc(s_freeA, 1)
            with act.Fori(0, s.units // SLOTS) as i:
                for c in range(rest, rest + SLOTS):
                    chunk_ready(act, s, i, c, SLOTS)
                    act.activation(big[:, bass.ds(i * (SLOTS * LAT) + c * LAT, LAT)], ps[:, (s.c0 + c) % 4, 0:LAT],
                                   ACT.Copy).then_inc(s_freeA, 1)
            copy_out(st["wing"], lambda c: u[:, 27 + c, :], func=ACT.Sigmoid, bias_col=lambda c: col("b_gate", c))
            copy_out(st["winr"], lambda c: u[:, 43, :])
            squares("nq")
            group_sums("nq")
            squares("nkv")
            group_sums("nkv")
            copy_out(st["uq"], lambda c: mq[:, c, :])
            copy_out(st["uk"], lambda c: mk[:, c, :])
            copy_out(st["uv"], lambda c: mv[:, c // 2, (c % 2) * 512:(c % 2 + 1) * 512])
            attention("mla")
            squares("nq2")
            group_sums("nq2")
            copy_out(st["memq"], lambda c: mq[:, c, :])
            attention("mem")
            squares("nmoe")
            group_sums("nmoe")
            act.wait_ge(s_rmax, 1)
            for q in range(2):
                ins = act.activation(aff[:, q, :], ps[:, 6, NE * q:NE * (q + 1)], ACT.Exp,
                                     bias=small[:, 120 + q:121 + q], accum_out=small[:, 122 + q:123 + q])
            ins.then_inc(s_rexp, 1)
            act.wait_ge(s_moe, 2)
            for q in range(2):
                ins = act.activation(hs[:, q, :].rearrange("p (a b) -> p a b", a=2), ps[:, 2 * q:2 * q + 2, :],
                                     ACT.Copy)
            ins.then_inc(s_moeA, 1)
            for k in range(KC):
                act.wait_ge(s_moe, 5 + k)
                act.activation(xg[:, k, :], ps[:, k % 4, :], ACT.Copy).then_inc(s_moeA, 1)
            act.wait_ge(s_moe, 13)
            for h in range(2):
                act.activation(gT[:, 4 * h:4 * h + 4, :].rearrange("p (a g) t -> p a (g t)", a=2),
                               ps[:, 4 + 2 * h:6 + 2 * h, :], ACT.Copy).then_inc(s_moeA, 1)
            u0 = st["experts"].u0
            with act.Fori(0, NE // 2) as pair:
                act.wait_ge(s_used, pair * 48 + (u0 + 16))
                act.activation(sg, ps[:, 4, :], ACT.Silu).then_inc(s_sg, 1)
                act.wait_ge(s_hturn, pair + 1)
                act.activation(hTe, ps[:, 6, :].rearrange("p (c n) -> p c n", c=4), ACT.Copy).then_inc(s_hT, 1)
                act.wait_ge(s_used, pair * 48 + (u0 + 48))
                act.activation(ye, ps[:, 7, :], ACT.Copy).then_inc(s_ye, 1)
            act.wait_ge(s_scat, NE // 2)
            for q in range(2):
                act.activation(otok[:, q, :].rearrange("p (a b) -> p a b", a=2), ps[:, 2 * q:2 * q + 2, :], ACT.Square,
                               accum_out=small[:, 112 + q:113 + q]).then_inc(s_ssq, 1)

        @block.vector
        def _(dve):
            steps = Steps(dve, c_dve)
            link = steps.link
            neg_lam = lams[:, 5:6]
            gsub = small[:, 124:125]

            def squares(name):
                N = NORM[name]
                for sm, v in READY[name]:
                    dve.wait_ge(sm, v)
                if N["n"]:
                    dve.wait_ge(s_stat, N["n"])
                dve.tensor_tensor(sq[:, 4:8, 0:N["T"]], N["src"][:, 4:8, :], N["src"][:, 4:8, :],
                                  ALU.mult).then_inc(s_sqD, 1)

            def newton(v, y, z):
                link(dve.tensor_scalar(y.bitcast(I32), v.bitcast(I32), -0.5, float(0x5F3759DF), ALU.mult, ALU.add))
                for _ in range(4):
                    link(dve.tensor_tensor(z, y, y, ALU.mult))
                    link(dve.scalar_tensor_tensor(z, z, -0.5, v, ALU.mult, ALU.mult))
                    link(dve.scalar_tensor_tensor(y, z, 1.5, y, ALU.add, ALU.mult))

            def rstd(name, n):
                dve.wait_ge(s_stat, NORM[name]["n"] + 1)
                v = var[:, 0:n]
                if name == "sub":
                    for b in range(2):
                        ins = dve.tensor_scalar(
                            v[:, 16 * b:16 * b + 16].rearrange("p (j q) -> p q j", j=4),
                            ps[:, 4 + 3 * b, :].rearrange("p (q j r) -> p q j r", q=4, j=4)[:, :, :, 0], EPS, None,
                            ALU.add)
                    link(ins)
                else:
                    link(dve.tensor_scalar(v, ps[:, 4, 0:n], EPS, None, ALU.add))
                newton(v, rs[:, 0:n], tmp[:, 0:n])

            diags = [0]

            def broadcast(r, nt):
                if diags[0]:
                    dve.wait_ge(s_bc, diags[0])
                diags[0] += 1
                dve.tensor_tensor(diag[:, 0:nt, :], ident.unsqueeze(1).to_broadcast([P, nt, P]),
                                  r.unsqueeze(2).to_broadcast([P, nt, P]), ALU.mult).then_inc(s_diag, 1)
                dve.wait_ge(s_bc, diags[0])
                return ps[:, 6 + diags[0] % 2, 0:nt * P]

            def norm(name):
                nt = NORM[name]["T"] // P
                rstd(name, nt)
                scale(name, broadcast(rs[:, 0:nt], nt))

            def scale(name, bc):
                N = NORM[name]
                for k in range(N["nk"]):
                    src, dst = N["src"][:, k, :], N["dst"][:, k, :]
                    if N["m"] is None:
                        ins = dve.scalar_tensor_tensor(dst, src, col(N["g"], k), bc, ALU.mult, ALU.mult)
                    elif N["T"] == TOK:
                        for c, sl in enumerate((slice(0, CTX), lat)):
                            ins = dve.scalar_tensor_tensor(dst[:, sl], src[:, sl], gain[:, N["m"], k, c:c + 1],
                                                           bc[:, sl], ALU.mult, ALU.mult)
                    else:
                        ins = dve.scalar_tensor_tensor(dst, src, gain[:, N["m"], k, 1:2], bc, ALU.mult, ALU.mult)
                    ins.then_inc(s_nD, 1)

            def head_norms():
                rstd("sub", 32)
                link(dve.tensor_scalar(gsub, col("subln"), 1.0 - LAM_INIT, None, ALU.mult))
                for h in range(KC):
                    bc = broadcast(rs[:, 4 * h:4 * h + 4], 4)
                    dve.scalar_tensor_tensor(xn[:, h, :], xn[:, h, :], gsub, bc, ALU.mult, ALU.mult).then_inc(s_nD, 1)

            def ada(l, g):
                s = st[f"turn{l}{g}"]
                chunk_ready(dve, s, 0, 0)
                src = ps[:, s.c0 % 4, :].rearrange("p (c j r) -> p j c r", c=4, j=4)
                for o in range(2):
                    ins = dve.tensor_tensor(mod[:, l, 16 * g:16 * g + 16, o].rearrange("p (j c) -> p j c", j=4),
                                            src[:, :, :, o],
                                            col("ada_b", 48 * l + 16 * g, 16).rearrange("p (j c) -> p j c", j=4),
                                            ALU.add)
                ins.then_inc(s_freeD, 1)

            def gains(m, after, g):
                l, part = MODS[m]
                dve.wait_ge(s_freeD, after.d1)
                dve.scalar_tensor_tensor(gain[:, m, :, :], mod[:, l, 8 * (part + 1):8 * (part + 2), :], 1.0,
                                         col(g, 0, 8).unsqueeze(2).to_broadcast([P, 8, 2]), ALU.add,
                                         ALU.mult).then_inc(s_gain, 1)

            def gated_add(s, l, part, T):
                for c in range(KC):
                    chunk_ready(dve, s, 0, c)
                    b = (s.c0 + c) % 4
                    if T == TOK:
                        dve.scalar_tensor_tensor(hT[:, c, 0:CTX], ps[:, b, 0:CTX], mod[:, l, 8 * part + c, 0:1],
                                                 hT[:, c, 0:CTX], ALU.mult, ALU.add)
                    dve.scalar_tensor_tensor(hT[:, c, lat], ps[:, b, T - LAT:T], mod[:, l, 8 * part + c, 1:2],
                                             hT[:, c, lat], ALU.mult, ALU.add).then_inc(s_freeD, 1)

            def add(s):
                for c in range(KC):
                    chunk_ready(dve, s, 0, c)
                    dve.tensor_tensor(hT[:, c, lat], ps[:, (s.c0 + c) % 4, 0:LAT], hT[:, c, lat],
                                      ALU.add).then_inc(s_freeD, 1)

            def products(s, T):
                def one(i, m):
                    chunk_ready(dve, s, i, 2 * m + 1, 8)
                    dve.wait_ge(s_freeA, i * 4 + (s.a0 + m + 1))
                    dve.tensor_tensor(big[:, bass.ds(i * (4 * TOK) + m * TOK, T)], silu_out[:, m % 2, 0:T],
                                      ps[:, (s.c0 + 2 * m + 1) % 4, 0:T], ALU.mult).then_inc(s_freeD, 1)
                for m in range(2):
                    one(0, m)
                with dve.Fori(0, (FC - 2) // 4) as i:
                    for m in range(4):
                        one(i, 2 + m)

            def rope(s, xs, cos, sin):
                for c, x in enumerate(xs):
                    chunk_ready(dve, s, 0, c)
                    n = x.shape[1]
                    a, b = ropet[:, 2 * (c % 2), 0:n, :], ropet[:, 2 * (c % 2) + 1, 0:n, :]
                    rot = ps[:, (s.c0 + c) % 4, 0:n * LAT].rearrange("p (n t) -> p n t", n=n)
                    dve.tensor_tensor(a, x, cos.unsqueeze(1).to_broadcast([P, n, LAT]), ALU.mult)
                    link(dve.tensor_tensor(b, rot, sin.unsqueeze(1).to_broadcast([P, n, LAT]), ALU.mult))
                    dve.tensor_tensor(x, a, b, ALU.add).then_inc(s_freeD, 1)

            def maxima(j):
                J, bf = jobs[j], j % 2
                dve.wait_ge(s_scores, j + 1)
                m = amax[:, 2 * bf:2 * bf + 2]
                link(dve.tensor_reduce(m, ps[:, 4 + 2 * bf:6 + 2 * bf, 0:J["n"]], AX.X, ALU.max))
                dve.tensor_scalar(anm[:, 2 * bf:2 * bf + 2], m, -J["scale"], None, ALU.mult).then_inc(s_max, 1)

            def normalise(j):
                J, bf = jobs[j], j % 2
                dve.wait_ge(s_exp, j + 1)
                r = arec[:, 2 * bf:2 * bf + 2]
                link(dve.reciprocal(r, asum[:, 2 * bf:2 * bf + 2]))
                n = J["n"]
                e0, e1 = E[:, j % 3, 0, 0:n], E[:, j % 3, 1, 0:n]
                if J["da"]:
                    dve.tensor_scalar(r[:, 1:2], r[:, 1:2], neg_lam, None, ALU.mult)
                    link(dve.tensor_scalar(e0, e0, r[:, 0:1], None, ALU.mult))
                    dve.scalar_tensor_tensor(e0, e1, r[:, 1:2], e0, ALU.mult, ALU.add).then_inc(s_prob, 1)
                else:
                    dve.tensor_scalar(e0, e0, r[:, 0:1], None, ALU.mult)
                    dve.tensor_scalar(e1, e1, r[:, 1:2], None, ALU.mult).then_inc(s_prob, 1)

            def outs(j):
                J = jobs[j]
                if J["evac"] is None:
                    return
                dve.wait_ge(s_pv, groups_before(j + 1))
                src = ps[:, 2 + J["o"] % 2, 0:J["out"][2]]
                if len(J["evac"].shape) == 3:
                    src = src.rearrange("p (a t) -> p a t", a=2)
                dve.tensor_copy(J["evac"], src).then_inc(s_osb, 1)

            def attention(name):
                a, b, _, _ = JOBS[name]
                for i in range(a, b + 3):
                    if i < b:
                        maxima(i)
                    if a <= i - 1 < b:
                        normalise(i - 1)
                    if a <= i - 3 < b:
                        outs(i - 3)

            dve.memset(scond[:, :, :], 0.0).then_inc(s_scond, 1)
            dve.memset(thirty[:, :], 1.0 / 32)
            dve.wait_ge(s_lamin, 16)
            for a in range(2):
                link(dve.tensor_tensor(small[:, 128:192], lamv[:, 2 * a, :], lamv[:, 2 * a + 1, :], ALU.mult))
                ins = dve.tensor_reduce(lams[:, a:a + 1], small[:, 128:192], AX.X, ALU.add)
                if a == 0:
                    link(ins)
            ins.then_inc(s_gain, 1)
            squares("n0")
            rstd("n0", 4)
            bc = broadcast(rs[:, 0:4], 4)
            ada(0, 0)
            gains(0, st["turn00"], "mix0")
            dve.wait_ge(s_lamex, 1)
            link(dve.tensor_tensor(lams[:, 4:5], lams[:, 3:4], lams[:, 2:3], ALU.subtract))
            link(dve.tensor_scalar(neg_lam, lams[:, 4:5], -LAM_INIT, None, ALU.add))
            dve.wait_ge(s_gain, 2)
            scale("n0", bc)
            rope(st["rope0"], [qk[:, 2 * c:2 * c + 2, lat] for c in range(8)], const("cos_a"), const("sin_a"))
            ada(0, 1)
            attention("da")
            squares("sub")
            ada(0, 2)
            gains(1, st["turn02"], "ffn0")
            head_norms()
            gated_add(st["wo0"], 0, 2, TOK)
            squares("n1")
            ada(1, 0)
            gains(2, st["turn10"], "mix1")
            norm("n1")
            products(st["gu0"], TOK)
            gated_add(st["down0"], 0, 5, TOK)
            squares("n2")
            ada(1, 1)
            norm("n2")
            ada(1, 2)
            gains(3, st["turn12"], "ffn1")
            squares("nmem")
            norm("nmem")
            attention("na")
            gated_add(st["wo1"], 1, 2, LAT)
            squares("n3")
            norm("n3")
            products(st["gu1"], LAT)
            gated_add(st["down1"], 1, 5, LAT)
            squares("nf")
            norm("nf")
            squares("nmix")
            norm("nmix")
            norm("nq")
            norm("nkv")
            link(dve.tensor_tensor(u[:, 0:8, :], u[:, 0:8, :], u[:, 16:24, :], ALU.mult))
            for k in range(KC):
                ins = dve.tensor_scalar(u[:, 16 + k, :], u[:, k, :], col("conv_w", 8 + k), col("conv_b", k), ALU.mult,
                                        ALU.add)
            link(ins)
            for tap, o, i in ((0, slice(1, LAT), slice(0, LAT - 1)), (2, slice(0, LAT - 1), slice(1, LAT))):
                for k in range(KC):
                    ins = dve.scalar_tensor_tensor(u[:, 16 + k, o], u[:, k, i], col("conv_w", 8 * tap + k),
                                                   u[:, 16 + k, o], ALU.mult, ALU.add)
                link(ins)
            dve.tensor_tensor(u[:, 8:16, :], u[:, 8:16, :], u[:, 16:24, :], ALU.mult).then_inc(s_conv, 1)
            rope(st["rope2"], [mq[:, 8:10, :], mq[:, 10:12, :], u[:, 43:44, :]], const("cos_b"), const("sin_b"))
            attention("mla")
            s = st["conv"]
            for c in range(KC):
                chunk_ready(dve, s, 0, c)
                dve.tensor_tensor(u[:, c, :], ps[:, (s.c0 + c) % 4, 0:LAT], u[:, 27 + c, :], ALU.mult)\
                   .then_inc(s_freeD, 1)
            s = st["mla"]
            for c in range(KC):
                chunk_ready(dve, s, 0, c)
                link(dve.tensor_tensor(u[:, 16 + c, :], ps[:, (s.c0 + c) % 4, 0:LAT], u[:, 35 + c, :], ALU.mult))
                dve.tensor_tensor(u[:, 16 + c, :], u[:, 16 + c, :], u[:, c, :], ALU.add).then_inc(s_freeD, 1)
            add(st["mix"])
            squares("nq2")
            norm("nq2")
            attention("mem")
            add(st["memo"])
            squares("nmoe")
            norm("nmoe")
            dve.wait_ge(s_moe, 1)
            link(dve.tensor_reduce(small[:, 118:120], ps[:, 6, 0:2 * NE].rearrange("p (q e) -> p q e", q=2), AX.X,
                                   ALU.max))
            dve.tensor_scalar(small[:, 120:122], small[:, 118:120], -1.0, None, ALU.mult).then_inc(s_rmax, 1)
            dve.wait_ge(s_rexp, 1)
            link(dve.reciprocal(small[:, 126:128], small[:, 122:124]))
            dve.tensor_tensor(aff, aff, small[:, 126:128].unsqueeze(2).to_broadcast([P, 2, NE]),
                              ALU.mult).then_inc(s_moeD, 1)
            dve.wait_ge(s_moe, 3)
            link(dve.tensor_copy(affT, ps[0:NE, 7, 0:LAT]))
            for r in range(CAP // 8):
                a = slice(8 * r, 8 * r + 8)
                link(dve.max(top[:, a], affT))
                link(dve.max_index(topi[:, a], top[:, a], affT))
                link(dve.match_replace(affT, top[:, a], affT, -1.0))
            link(dve.tensor_copy(topf, topi))
            blocks = const("experts")[0:NE, :].rearrange("p (e n) -> p e n", e=NE)
            for a, v in enumerate((topf, top)):
                ins = dve.tensor_tensor(spread[:, a, :].rearrange("p (e n) -> p e n", e=NE), blocks,
                                        v.unsqueeze(1).to_broadcast([NE, NE, CAP]), ALU.mult)
            ins.then_inc(s_moeD, 1)
            dve.wait_ge(s_moe, 4)
            for q in range(2):
                ins = dve.tensor_scalar(sel[:, q, :], ps[:, 4, :], const("token")[:, q:q + 1], None, ALU.is_equal)
            ins.then_inc(s_moeD, 1)
            dve.wait_ge(s_moeD, 3)
            for q in range(2):
                for h in range(2):
                    ins = dve.tensor_tensor(gsel[:, q, :, h, :], ps[:, 5, :].rearrange("p (e n) -> p e n", e=NE),
                                            sel[:, q, :].rearrange("p (e n) -> p e n", e=NE), ALU.mult)
            ins.then_inc(s_moeD, 1)
            dve.wait_ge(s_moeA, 11)
            dve.tensor_copy(xe, xg[:, :, 0:2 * CAP]).then_inc(s_xe, 1)
            u0 = st["experts"].u0

            def pair_steps(pair, last):
                for h in range(2):
                    ins = dve.tensor_scalar(gx[:, h, :], aux[:, bass.ds(pair * LAT, LAT)], const("halves")[:, h:h + 1],
                                            None, ALU.mult)
                ins.then_inc(s_gx, 1)
                dve.wait_ge(s_sg, pair + 1)
                dve.wait_ge(s_used, pair * 48 + (u0 + 32))
                dve.tensor_tensor(hp, sg, ps[:, 5, :], ALU.mult).then_inc(s_he, 1)
                if not last:
                    dve.tensor_copy(xe, xg[:, :, bass.ds(pair * (2 * CAP) + 2 * CAP, 2 * CAP)]).then_inc(s_xe, 1)
                    dve.wait_ge(s_scat, pair + 1)

            with dve.Fori(0, NE // 2 - 1) as pair:
                pair_steps(pair, False)
            pair_steps(NE // 2 - 1, True)
            dve.wait_ge(s_ssq, 2)
            link(dve.tensor_scalar(var[:, 0:2], small[:, 112:114], 1.0 / D, EPS, ALU.mult, ALU.add))
            newton(var[:, 0:2], rs[:, 0:2], tmp[:, 0:2])
            dve.wait_ge(s_grow, 16)
            for q in range(2):
                dve.scalar_tensor_tensor(otok[:, q, :].rearrange("p (a b) -> p a b", a=2), ps[:, 2 * q:2 * q + 2, :],
                                         rs[:, q:q + 1], grow.rearrange("p (a b) -> p a b", a=2), ALU.mult,
                                         ALU.mult).then_inc(s_res, 1)


def _rope_tables(seq, first):
    f = np.float32
    if first:
        half = HD // 2
        freqs = (f(1.0) / (f(10000.0) ** (np.arange(0, half, 2, dtype=f) / f(half)))).astype(f)
        pos = np.arange(seq)
        ar = (pos // GRID_W).astype(f)[:, None] * freqs
        ac = (pos % GRID_W).astype(f)[:, None] * freqs
        ang = np.concatenate([ar, ar, ac, ac], axis=-1)
    else:
        inv = (f(1.0) / (f(10000.0) ** (np.arange(0, HD, 2, dtype=f) / f(HD)))).astype(f)
        a = np.arange(seq, dtype=f)[:, None] * inv
        ang = np.concatenate([a, a], axis=-1)
    ang = np.concatenate([ang, ang], axis=-1).T
    return np.cos(ang).astype(f), np.sin(ang).astype(f)


def _rotation(half):
    m = np.zeros((P, P), np.float32)
    for b in range(0, P, 2 * half):
        for j in range(half):
            m[b + half + j, b + j] = -1.0
            m[b + j, b + half + j] = 1.0
    return m


def _constants():
    c = np.zeros((P, NCONST), np.float32)

    def put(name, v):
        c[:, CONST[name][0]:CONST[name][1]] = v
    put("ident", np.eye(P))
    put("ones", 1.0)
    put("rot_a", _rotation(HD // 4))
    put("rot_b", _rotation(HD // 2))
    for n, first in (("a", True), ("b", False)):
        cos, sin = _rope_tables(LAT, first)
        put("cos_" + n, cos)
        put("sin_" + n, sin)
    q = np.arange(P) % GRID_W
    start = np.clip(q - 8, 0, GRID_W - 16)
    k = np.arange(GRID_W)
    inside = (k[None, :] >= start[:, None]) & (k[None, :] < start[:, None] + 16)
    put("mask", np.where(inside, 0.0, NEG))
    put("inv", np.repeat([1.0 / 1024, 1.0 / 256, 1.0 / 128], 32)[None, :])
    put("halves", (np.arange(P)[:, None] // CAP % 2 == np.arange(2)[None, :]).astype(np.float32))
    put("token", np.arange(P)[:, None] + np.array([[0, P]]))
    e = np.arange(NE * CAP) // CAP
    put("experts", (np.arange(P)[:, None] == e[None, :]).astype(np.float32))
    return c


def _blocks(w):
    K, M = w.shape
    return np.ascontiguousarray(w.reshape(K // P, P, M // P, P).transpose(2, 1, 0, 3)).reshape(M // P, P, K)


def _features(x):
    return np.ascontiguousarray(x.reshape(x.shape[0], -1, P).transpose(2, 1, 0))


def _column(v):
    return v.reshape(-1, P).T


def kernel(**inputs):
    import concourse.bacc as bacc
    from concourse.bass_utils import run_bass_kernel_spmd

    a = {k: np.asarray(v) for k, v in inputs.items()}
    arrays = {
        "consts": _constants(),
        "cond": np.ascontiguousarray(np.stack([a["c_ctx"], a["c"][0]]).reshape(2, KC, P).transpose(2, 1, 0)),
        "ctxT": _features(a["ctx"][0]), "xT": _features(a["x"][0]), "memT": _features(a["mem_2"][0]),
        "lam": np.concatenate([a["da_lambda_q1"], a["da_lambda_k1"], a["da_lambda_q2"], a["da_lambda_k2"]]),
        "final2": a["norm_final_g_2"],
        "rpb": np.ascontiguousarray(a["na_rpb"][0]),
        "wr": np.ascontiguousarray(a["w_router_2"][0].reshape(KC, P, NE).transpose(1, 0, 2)),
    }
    vectors = {
        "mix0": a["norm_mix"][0], "mix1": a["norm_mix"][1], "ffn0": a["norm_ffn"][0], "ffn1": a["norm_ffn"][1],
        "final": a["norm_final"], "mix2": a["norm_mix_g_2"][0], "mem": a["norm_mem_g_2"][0],
        "memkv": a["norm_memkv_g_2"][0], "moe": a["norm_moe_g_2"][0],
        "qn": a["q_norm_g_2"][0], "kvn": a["kv_norm_g_2"][0], "subln": a["da_subln"][0],
        "conv_w": a["conv_w_2"][0], "conv_b": a["conv_b_2"][0], "b_gate": a["b_gate_2"][0], "ada_b": a["ada_b"],
    }
    arrays["cols"] = np.ascontiguousarray(np.concatenate([_column(vectors[n]) for n, _ in _COLS], axis=1))
    for l in range(2):
        arrays[f"ada{l}"] = np.ascontiguousarray(
            a["ada_w"][l].reshape(KC, P, 3, 2, D).transpose(2, 0, 3, 1, 4)).reshape(3 * 16, P, D)
        gu = _blocks(a["ffn_w_gate_up"][l]).reshape(2, FC, P, D)
        arrays[f"gu{l}"] = np.ascontiguousarray(gu.transpose(1, 0, 2, 3)).reshape(2 * FC, P, D)
        arrays[f"down{l}"] = _blocks(a["ffn_w_down"][l]).reshape(KC, P, 2, WIDE).transpose(0, 2, 1, 3)            .reshape(2 * KC, P, WIDE)
    arrays["wqkv0"], arrays["wqkv1"] = _blocks(a["da_wqkv"][0]), _blocks(a["na_wqkv"][0])
    arrays["wo0"], arrays["wo1"] = _blocks(a["da_wo"][0]), _blocks(a["na_wo"][0])
    w = a["w_in_2"][0]
    kr = w[:, 3456:3520]
    arrays["win"] = _blocks(np.concatenate([w[:, 0:3456], w[:, 3520:5568], kr, kr], axis=1))
    wq = a["w_uq_2"][0].reshape(256, MLA_H, 192)
    wq = np.concatenate([wq[:, :, 0:P].reshape(256, -1), wq[:, :, P:].reshape(256, -1)], axis=1)
    arrays["uq"] = np.ascontiguousarray(_blocks(wq).reshape(3, 4, P, 256).transpose(0, 2, 1, 3)).reshape(3, P, D)
    wkv = a["w_ukv_2"][0].reshape(P, MLA_H, 2, P)
    arrays["ukv"] = np.ascontiguousarray(wkv.transpose(2, 0, 1, 3)).reshape(2, P, D)
    for n, src in (("conv_out", "w_conv_out_2"), ("mla_out", "w_mla_out_2"), ("mix_out", "w_mix_out_2"),
                   ("memq", "w_mem_q_2"), ("memkv", "w_mem_kv_2"), ("memo", "w_mem_out_2")):
        arrays[n] = _blocks(a[src][0])
    for n, src in (("gate", "w_exp_gate_2"), ("up", "w_exp_up_2"), ("down", "w_exp_down_2")):
        arrays[n] = a[src][0].reshape(NE * KC, P, D)

    nc = bacc.Bacc("TRN2", target_bir_lowering=False, num_devices=1)
    t = {n: nc.dram_tensor(f"in_{n}", v.shape, mybir.dt.from_np(v.dtype), kind="ExternalInput").ap()
         for n, v in arrays.items()}
    out = nc.dram_tensor("out_0", (2, P, D), F32, kind="ExternalOutput").ap()
    diffusion_moe_kernel(nc, t, out)
    r = run_bass_kernel_spmd(nc, [{f"in_{n}": v for n, v in arrays.items()}], core_ids=[0])
    got = r.results[0]["out_0"]
    return got.reshape(1, LAT, D)
```

```python
from contextlib import ExitStack

import numpy as np

import concourse.bass as bass
from concourse import mybir

F32 = mybir.dt.float32
I32 = mybir.dt.int32
U32 = mybir.dt.uint32
ALU = mybir.AluOpType
ACT = mybir.ActivationFunctionType
AX = mybir.AxisListType

P = 128
D = 1024
KC = D // P
CTX = 256
LAT = 256
TOK = CTX + LAT
FF = 2816
FC = FF // P
GRID_W = 64
HEADS = 16
HD = 64
RPB_R, RPB_C = 15, 31
NEG = -1e30
EPS = 1e-6
LAM_INIT = 0.8 - 0.6 * float(np.exp(-0.3 * 0))
MLA_H = 8
MEM_H = 4
NE = 16
CAP = 2 * LAT // NE
SLOTS = 8
EXPERT_SLOTS = 12
BEHIND = 4
UNIT = KC * P
EARLY = 2 * KC
WIDE = FC // 2 * P

_COLS = [("mix0", 8), ("mix1", 8), ("ffn0", 8), ("ffn1", 8), ("final", 8), ("mix2", 8), ("mem", 8), ("memkv", 8),
         ("moe", 8), ("qn", 2), ("kvn", 1), ("subln", 1), ("conv_w", 24), ("conv_b", 8),
         ("b_gate", 16), ("ada_b", 96)]
COL, _n = {}, 0
for _name, _w in _COLS:
    COL[_name] = (_n, _n + _w)
    _n += _w
NCOLS = _n

_CONST = [("ident", 128), ("ones", 128), ("rot_a", 128), ("rot_b", 128), ("cos", LAT), ("sin", LAT),
          ("mask", GRID_W), ("inv", 3 * 32), ("token", 2), ("halves", 2), ("groups", NE)]
CONST, _n = {}, 0
for _name, _w in _CONST:
    CONST[_name] = (_n, _n + _w)
    _n += _w
NCONST = _n


class Stage:

    readers = []

    def __init__(self, name, weights, units, chunks, owner, width=UNIT, share=None, beside=None):
        self.name, self.weights, self.units, self.chunks, self.owner, self.width = (
            name, weights, units, chunks, owner, width)
        self.beside = beside
        self.share = share

    def raises(self, c):
        if self.share is None:
            return "used", self.u0 + (c + 1) * self.units // self.chunks
        cs, us = self.share
        if us and c % cs == cs - 1:
            return "used", self.u0 + (c // cs + 1) * us
        return "chunk", self.k0 + (c - c // cs if us else c) + 1


def plan():
    def ada(l, g):
        return [Stage(f"ada{l}{g}", (f"ada{l}", 16 * g), 16, 1, "A"),
                Stage(f"turn{l}{g}", None, 0, 1, "D", share=(1, 0))]

    def beside(l, g):
        return [Stage(f"ada{l}{g}", None, 0, 1, "A")]

    stages = [
        Stage("memk", ("memkv", 0), 24, 8, "D", beside=(0, 0)), *beside(0, 0),
        Stage("memva", ("memkv", 8), 4, 2, "A", share=(2, 4)),
        Stage("turn00", None, 0, 1, "D", share=(1, 0)),
        Stage("memvb", ("memkv", 12), 4, 2, "A", share=(2, 4)),
        Stage("q0", ("wqkv0", 0), 24, 8, "A", beside=(0, 1)), *beside(0, 1),
        Stage("k0", ("wqkv0", 8), 8, 8, "A"),
        Stage("turn01", None, 0, 1, "D", share=(1, 0)),
        Stage("v0", ("wqkv0", 16), 8, 8, "A", share=(4, 4)),
        *ada(0, 2),
        Stage("wo0", ("wo0", 0), 8, 8, "D"),
        *ada(1, 0),
        Stage("gu0", ("gu0", 0), 2 * FC, 2 * FC, "AD"), Stage("down0", ("down0", 0), 16, 8, "D", WIDE),
        *ada(1, 1),
        Stage("q1", ("wqkv1", 0), 8, 8, "A"), Stage("k1", ("wqkv1", 8), 8, 8, "A"),
        Stage("v1", ("wqkv1", 16), 8, 8, "A", share=(4, 4)),
        Stage("wo1", ("wo1", 0), 8, 8, "D"),
        *ada(1, 2),
        Stage("gu1", ("gu1", 0), 2 * FC, 2 * FC, "AD"), Stage("down1", ("down1", 0), 16, 8, "D", WIDE),
        Stage("win", ("win", 0), 27, 27, "A"), Stage("wing", ("win", 27), 16, 16, "A"),
        Stage("winr", ("win", 43), 1, 1, "A"),
        Stage("uq", ("uq", 0), 3, 12, "A", share=(4, 1)), Stage("uk", ("ukv", 0), 1, 8, "A", share=(8, 1)),
        Stage("uv", ("ukv", 1), 1, 4, "A", share=(4, 1)),
        Stage("conv", ("conv_out", 0), 8, 8, "D"), Stage("mla", ("mla_out", 0), 8, 8, "D"),
        Stage("mix", ("mix_out", 0), 8, 8, "D"),
        Stage("memq", ("memq", 0), 8, 8, "D"), Stage("memo", ("memo", 0), 8, 8, "D"),
        Stage("experts", None, 0, 0, "D"),
    ]
    Stage.readers.clear()
    unit = chunk = a = d = k = 0
    for s in stages:
        s.u0, s.c0, s.a0, s.d0, s.k0 = unit, chunk, a, d, k
        for c in range(s.chunks):
            by = s.owner[c % len(s.owner)]
            Stage.readers.append((by, (a if by == "A" else d) + c // len(s.owner) + 1))
        unit += s.units
        chunk += s.chunks
        a += {"A": s.chunks, "D": 0, "AD": s.chunks // 2}[s.owner]
        d += {"D": s.chunks, "A": 0, "AD": s.chunks // 2}[s.owner]
        s.a1, s.d1, s.c1 = a, d, chunk
        if s.share:
            k += s.chunks - (s.chunks // s.share[0] if s.share[1] else 0)
    return {s.name: s for s in stages}


class Steps:

    def __init__(self, eng, sem):
        self.eng, self.sem, self.n = eng, sem, 0

    def link(self, ins):
        self.n += 1
        ins.then_inc(self.sem, 1)
        self.eng.wait_ge(self.sem, self.n)


def diffusion_moe_kernel(nc, t, out):
    st = plan()
    ctx = ExitStack()
    with ctx:
        def sb(name, shape, dt=F32):
            return ctx.enter_context(nc.sbuf_tensor(name, shape, dt))

        def sem(name):
            return ctx.enter_context(nc.semaphore(name))

        ring = sb("ring", [P, SLOTS, WIDE])
        hT = sb("hT", [P, KC, TOK])
        xn = sb("xn", [P, KC, TOK])
        big = sb("big", [P, 12288])
        aux = sb("aux", [P, 12288])
        work = sb("work", [P, 6144])
        cst = sb("cst", [P, NCONST])
        cols = sb("cols", [P, NCOLS])
        cond = sb("cond", [P, KC, 2])
        scond = sb("scond", [P, KC, 32])
        mod = sb("mod", [P, 2, 48, 2])
        gain = sb("gain", [P, 4, KC, 2])
        lamv = sb("lamv", [P, 4, HD])
        lams = sb("lams", [P, 8])
        small = sb("small", [P, 192])
        memr = lams[:, 6:8]
        wr = sb("wr", [P, KC, 32])

        rpb_copies = nc.dram_tensor("rpb_copies", (GRID_W, HEADS * RPB_R * RPB_C), F32, kind="Internal").ap()
        ps = ctx.enter_context(nc.psum_tensor("ps", [P, 8, 512], F32))

        def const(name):
            a, b = CONST[name]
            return cst[:, a:b]

        def col(name, k=0, n=1):
            a = COL[name][0] + k
            return cols[:, a:a + n]

        ident, ones = const("ident"), const("ones")
        thirty = sb("thirty", [P, 1])
        lat = slice(CTX, TOK)
        sq = work[:, 0:KC * TOK].rearrange("p (k t) -> p k t", k=KC)
        diag = work[:, 4096:4608].rearrange("p (a b) -> p a b", b=P)
        diag2 = work[:, 5120:5632].rearrange("p (a b) -> p a b", b=P)
        var, rs, tmp = small[:, 0:32], small[:, 32:64], small[:, 64:96]
        qk = big[:, 0:16 * TOK].rearrange("p (c t) -> p c t", c=16)
        vv = big[:, 8192:12288].rearrange("p (k d) -> p k d", k=4)
        hid = big[:, 0:FC * TOK].rearrange("p (k t) -> p k t", k=FC)
        stats = work[:, 4608:5120]
        stats2 = work[:, 5120:6144].rearrange("p (b t) -> p b t", b=2)
        silu_out = work[:, 5120:6144].rearrange("p (b t) -> p b t", b=2)
        ropet = work[:, 0:2048].rearrange("p (b c t) -> p b c t", b=4, c=2)
        bias = aux[:, 0:8192].rearrange("p (q h k) -> p q h k", q=2, h=HEADS)
        u = big[:, 0:44 * LAT].rearrange("p (c t) -> p c t", c=44)
        mq = aux[:, 0:12 * LAT].rearrange("p (c t) -> p c t", c=12)
        mk = aux[:, 3072:5120].rearrange("p (c t) -> p c t", c=8)
        mv = aux[:, 5120:7168].rearrange("p (k d) -> p k d", k=2)
        memk = aux[:, 8192:10240].rearrange("p (c t) -> p c t", c=8)
        memv = aux[:, 10240:12288].rearrange("p (k d) -> p k d", k=2)
        x2 = xn[:, :, 0:LAT]
        h2 = hT[:, :, lat]
        memT = big[:, 0:KC * LAT].rearrange("p (k t) -> p k t", k=KC)
        memG = big[:, KC * LAT:2 * KC * LAT].rearrange("p (k t) -> p k t", k=KC)
        sq_heads = aux[:, 0:KC * TOK].rearrange("p (k t) -> p k t", k=KC)
        E = work[:, 0:3072].rearrange("p (b c n) -> p b c n", b=3, c=2)
        PT = work[:, 3072:5120].rearrange("p (b n) -> p b n", b=4)
        anm = small[:, 100:104]
        asum, arec = small[:, 104:108], small[:, 108:112]
        early = [big[:, j * UNIT:(j + 1) * UNIT] for j in range(12)]
        early += [aux[:, 7168 + j * UNIT:7168 + (j + 1) * UNIT] for j in range(EARLY - len(early))]
        flat = ring[:, :, :].rearrange("p s n -> p (s n)")
        expert_ring = [flat[:, j * UNIT:(j + 1) * UNIT] for j in range(SLOTS * WIDE // UNIT)]
        expert_ring += [work[:, 5120:5120 + UNIT]]
        assert len(expert_ring) == EXPERT_SLOTS
        hs = aux[:, 0:2048].rearrange("p (s d) -> p s d", s=2)
        sel = aux[:, 2048:3072].rearrange("p (s n) -> p s n", s=2)
        gsel = aux[:, 3072:5120].rearrange("p (s e h n) -> p s e h n", s=2, e=NE, h=2)
        aff = aux[:, 5120:5152].rearrange("p (s e) -> p s e", s=2)
        affT = aux[0:NE, 5152:5408]
        top = aux[0:NE, 5408:5440]
        topi = aux[0:NE, 5440:5472].bitcast(U32)
        topf = aux[0:NE, 5472:5504]
        spread = aux[0:NE, 5504:6528].rearrange("p (a n) -> p a n", a=2)
        own = aux[0:NE, 6528:7040]
        grow = aux[:, 3072:4096]
        otok = aux[:, 0:2048].rearrange("p (q d) -> p q d", q=2)
        xe = aux[:, 11264:11776].rearrange("p (k n) -> p k n", k=KC)
        xg = xn
        gT = work[:, 0:2048].rearrange("p (g t) -> p g t", g=NE // 2)
        gx = work[:, 2048:2560].rearrange("p (h t) -> p h t", h=2)
        sg, hp = work[:, 2560:3072], work[:, 3072:3584]
        hTe = work[:, 3584:4096].rearrange("p (c n) -> p c n", c=4)
        ye = work[:, 4096:4608]

        s_small = sem("small_inputs_loaded")
        s_x = sem("tokens_loaded")
        s_early = sem("early_units_landed")
        s_tab = sem("second_tables_loaded")
        s_bias = sem("rpb_loaded")
        s_copies = sem("rpb_copied")
        s_biasm = sem("bias_masked")
        s_mem = sem("mem_loaded")
        s_land = [sem(f"unit_landed_{i}") for i in range(SLOTS)]
        s_eland = [sem(f"expert_unit_landed_{i}") for i in range(EXPERT_SLOTS)]
        s_used = sem("unit_used")
        s_chunk = sem("chunk_computed")
        s_freeA = sem("chunk_read_by_scalar")
        s_freeD = sem("chunk_read_by_vector")
        s_grow = sem("final_weight_loaded")
        s_acopy = sem("group_sums_in_sbuf")
        s_part = sem("group_sums")
        s_scond = sem("silu_of_cond")
        s_gain = sem("gains")
        s_lamin = sem("lambda_sums")
        s_lamex = sem("lambda_exps")
        s_sqA = sem("squares_by_scalar")
        s_stat = sem("mean_squares")
        s_diag = sem("rstd_diagonals")
        s_bc = sem("rstd_broadcast")
        s_nD = sem("normed_by_vector")
        s_nA = sem("shifted_by_scalar")
        s_scores = sem("scores")
        s_max = sem("score_max")
        s_exp = sem("exps")
        s_prob = sem("probs")
        s_pt = sem("probs_transposed")
        s_ptsb = sem("probs_transposed_in_sbuf")
        s_pv = sem("heads_out")
        s_osb = sem("heads_out_in_sbuf")
        s_rope = sem("rotated")
        s_ropeD = sem("rotation_used")
        s_conv = sem("conv_ready")
        s_logits = sem("router_group_sums")
        s_sel = sem("first_choices")
        s_rmax = sem("router_max")
        s_rexp = sem("router_exp")
        s_moe = sem("moe_pe")
        s_moeD = sem("moe_vector")
        s_moeA = sem("moe_scalar")
        s_sg = sem("expert_silu")
        s_he = sem("expert_hidden")
        s_xe = sem("expert_tokens")
        s_gx = sem("expert_gates_staged")
        s_hturn = sem("expert_hidden_turned")
        s_hT = sem("expert_hidden_turned_in_sbuf")
        s_ye = sem("expert_out_in_sbuf")
        s_scat = sem("expert_out_scattered")
        s_half = sem("expert_out_scattered_to_first_tokens")
        s_ssq = sem("output_squares")
        s_res = sem("output_rows")
        s_out = sem("output_stored")
        c_dve = sem("vector_steps")

        norms = [
            ("nmem", memT, memG, KC, LAT, "memkv", 0, None),
            ("n0", hT[:, :, :], xn[:, :, :], KC, TOK, "mix0", 0, 0),
            ("sub", xn[:, :, :], xn[:, :, :], KC, TOK, "subln", 2, None),
            ("n1", hT[:, :, :], xn[:, :, :], KC, TOK, "ffn0", 0, 1),
            ("n2", hT[:, :, :], xn[:, :, :], KC, TOK, "mix1", 0, 2),
            ("n3", h2, x2, KC, LAT, "ffn1", 0, 3),
            ("nfm", h2, x2, KC, TOK, "final", 0, None),
            ("nq", u[:, 24:26, :], u[:, 24:26, :], 2, LAT, "qn", 1, None),
            ("nkv", u[:, 26:27, :], u[:, 26:27, :], 1, LAT, "kvn", 2, None),
            ("nq2", h2, x2, KC, LAT, "mem", 0, None),
            ("nmoe", h2, x2, KC, LAT, "moe", 0, None),
        ]
        NORM, nd, na = {}, 0, 0
        for n, (name, src, dst, nk, T, g, inv, m) in enumerate(norms):
            NORM[name] = dict(n=n, src=src, dst=dst, nk=nk, T=T, g=g, inv=inv, m=m, n0=nd, a0=na)
            nd += nk
            na += nk if m is not None else 0
            NORM[name].update(nd=nd, na=na)
        MODS = [(0, 0), (0, 3), (1, 0), (1, 3)]

        def da_jobs():
            for h in range(8):
                for q in (0, 2, 1, 3):
                    n = CTX if q < 2 else TOK
                    yield dict(
                        n=n, da=True,
                        scores=[[(qk[64 * c:64 * c + 64, h, q * P:q * P + P], qk[64 * c:64 * c + 64, 8 + h, 0:n], 0, n)]
                                for c in range(2)],
                        groups=[[(None, k) for k in range(n // P)]],
                        pv=[[(0, P, q * P, vv[:, k, h * P:h * P + P], k * P, P, k == 0, k == n // P - 1)
                             for k in range(n // P)]],
                        first=q == 0, evac=xn[:, h, :] if q == 3 else None, out=(0, P, TOK))

        def na_jobs():
            for h in range(HEADS):
                o, c = 64 * (h % 2), h // 2
                yield dict(
                    n=TOK, da=False,
                    scores=[[(qk[o:o + 64, c, CTX + p * P:CTX + p * P + P], qk[o:o + 64, 8 + c, :], 0, TOK),
                             (ident, bias[:, p, h, :], CTX, LAT)] for p in range(2)],
                    groups=[[(p, 2 * g + k) for k in range(2) for p in range(2)] for g in range(2)],
                    pv=[[(o, 64, 0, vv[:, 2 * g + k, h * 64:h * 64 + 64], k * 256, 256, g + k == 0, g + k == 2)
                         for k in range(2)] for g in range(2)],
                    first=h % 2 == 0, evac=xn[:, c, 0:LAT] if h % 2 else None, out=(0, P, LAT))

        def mla_jobs():
            for h in range(MLA_H):
                o = 64 * (h % 2)
                yield dict(
                    n=LAT, da=False,
                    scores=[[(mq[:, h, p * P:p * P + P], mk[:, h, :], 0, LAT),
                             (mq[o:o + 64, 8 + h // 2, p * P:p * P + P], u[o:o + 64, 43, :], 0, LAT)]
                            for p in range(2)],
                    groups=[[(p, k) for k in range(2) for p in range(2)]],
                    pv=[[(0, P, 0, mv[:, k, h * P:h * P + P], k * 256, 256, k == 0, k == 1) for k in range(2)]],
                    first=True, evac=x2[:, h, :], out=(0, P, LAT))

        def mem_jobs():
            for h in range(MEM_H):
                yield dict(
                    n=LAT, da=False,
                    scores=[[(mq[:, 2 * h + k, p * P:p * P + P], memk[:, 2 * h + k, :], 0, LAT) for k in range(2)]
                            for p in range(2)],
                    groups=[[(p, k) for k in range(2) for p in range(2)]],
                    pv=[[(0, P, 256 * e, memv[:, k, h * 256 + e * P:h * 256 + e * P + P], k * 256, 256, k == 0, k == 1)
                         for e in range(2) for k in range(2)]],
                    first=True, evac=x2[:, 2 * h:2 * h + 2, :], out=(0, P, 2 * LAT))

        JOBS, jobs, job_groups, job_outs = {}, [], [], []
        for name, made in (("da", da_jobs()), ("na", na_jobs()), ("mla", mla_jobs()), ("mem", mem_jobs())):
            a = len(jobs)
            for j in made:
                j["g0"] = sum(job_groups)
                j["o"] = sum(job_outs)
                job_groups.append(len(j["groups"]))
                job_outs.append(1 if j["evac"] is not None else 0)
                jobs.append(j)
            JOBS[name] = (a, len(jobs), sum(job_groups), sum(job_outs))
        g_end = sum(job_groups)

        def groups_before(j):
            return jobs[j]["g0"] if j < len(jobs) else g_end

        block = ctx.enter_context(nc.Block())

        @block.sync
        def _(sp):
            sp.dma_start(memT, t["memT"]).then_inc(s_mem, 16)
            sp.dma_start(cst[:, :], t["consts"]).then_inc(s_small, 16)
            sp.dma_start(cond[:, :, :], t["cond"]).then_inc(s_small, 16)
            sp.dma_start(cols[:, :], t["cols"]).then_inc(s_small, 16)

            def stream(src, u0, off, n, width):
                full = n // SLOTS if n > 3 * SLOTS and u0 >= SLOTS else 0

                def load(i, j):
                    s = (u0 + j) % SLOTS
                    if u0 + j >= SLOTS or not isinstance(i, int):
                        sp.wait_ge(s_used, i * SLOTS + (u0 + j - SLOTS + 1))
                    sp.dma_start(ring[:, s, 0:width], src[i * SLOTS + (off + j)]).then_inc(s_land[s], 16)

                if full:
                    with sp.Fori(0, full) as i:
                        for j in range(SLOTS):
                            load(i, j)
                for j in range(full * SLOTS, n):
                    load(0, j)

            def early_units(a, b):
                for j in range(a, b):
                    sp.dma_start(early[j], t["down"][KC * (j % 2) + j // 2]).then_inc(s_early, 16)

            for s in st.values():
                if s.name == "memo":
                    sp.wait_ge(s_used, st["mix"].u0 + 8)
                    early_units(0, 12)
                if s.beside:
                    l, g = s.beside
                    for j in range(s.units // 3):
                        stream(t[s.weights[0]], s.u0 + 3 * j, s.weights[1] + j, 1, s.width)
                        stream(t[f"ada{l}"], s.u0 + 3 * j + 1, 16 * g + 2 * j, 2, UNIT)
                        if s.name == "memk" and j == 3:
                            sp.dma_start(hT[:, :, 0:CTX], t["ctxT"]).then_inc(s_x, 16)
                            sp.dma_start(hT[:, :, lat], t["xT"]).then_inc(s_x, 16)
                elif s.units:
                    stream(t[s.weights[0]], s.u0, s.weights[1], s.units, s.width)
            sp.wait_ge(s_osb, JOBS["mem"][3])
            early_units(12, EARLY)
            u0 = st["experts"].u0

            sp.wait_ge(s_used, u0)

            def pair_units(i, base, pair, parts):
                for part, name in enumerate(parts):
                    for j in range(16):
                        n = 16 * part + j
                        slot = (base + n) % EXPERT_SLOTS
                        if base + n >= EXPERT_SLOTS:
                            sp.wait_ge(s_used, i * 48 + (u0 + base + n - EXPERT_SLOTS + 1))
                        sp.dma_start(expert_ring[slot],
                                     t[name][i * 16 + (16 * pair + KC * (j % 2) + j // 2)])\
                          .then_inc(s_eland[slot], 16)

            pair_units(0, 0, 0, ("gate", "up"))
            with sp.Fori(0, NE // 2 - 1) as i:
                pair_units(i, 32, 1, ("gate", "up", "down"))
            for q in range(2):
                sp.wait_ge(s_res, q + 1)
                sp.dma_start(out[q], otok[:, q, :]).then_inc(s_out, 16)
            sp.wait_ge(s_out, 32)

        @block.gpsimd
        def _(pool):
            pool.dma_start(lamv[:, :, :].rearrange("p a b -> p (a b)"),
                           bass.AP(t["lam"].tensor, 0, [[0, P], [1, 4 * HD]])).then_inc(s_lamin, 16)
            pool.wait_ge(s_scond, 1)
            pool.dma_start(wr[:, :, 0:NE], t["wr"]).then_inc(s_bias, 16)
            pool.wait_ge(s_acopy, NORM["sub"]["n"] + 1)
            table = HEADS * RPB_R * RPB_C
            pool.dma_start(rpb_copies, bass.AP(t["rpb"].tensor, 0, [[0, GRID_W], [1, table]])).then_inc(s_copies, 16)
            pool.wait_ge(s_copies, 16)
            for r in range(4):
                for rr in range(4):
                    o = 64 * (r % 2)
                    pool.dma_start(
                        bias[o:o + 64, r // 2, :, rr * GRID_W:(rr + 1) * GRID_W],
                        bass.AP(rpb_copies.tensor, (rr - r + 7) * RPB_C + 15,
                                [[table - 1, GRID_W], [RPB_R * RPB_C, HEADS], [1, GRID_W]])).then_inc(s_bias, 16)
            pool.wait_ge(s_bias, 17 * 16)
            pool.wait_ge(s_small, 48)
            bm = aux[:, 0:8192].rearrange("p (n c) -> p n c", c=GRID_W)
            pool.tensor_tensor(bm, bm, const("mask").unsqueeze(1).to_broadcast([P, P, GRID_W]),
                               ALU.add).then_inc(s_biasm, 1)
            pool.wait_ge(s_ropeD, 8)
            pool.dma_start(cst[:, CONST["cos"][0]:CONST["sin"][1]], t["rope2"]).then_inc(s_tab, 16)
            pool.wait_ge(s_osb, JOBS["mla"][3])
            pool.dma_start(own, t["own"]).then_inc(s_tab, 16)
            pool.wait_ge(s_moe, 15)
            pool.dma_start(grow, bass.AP(t["final2"].tensor, 0, [[0, P], [1, D]])).then_inc(s_grow, 16)

        @block.tensor
        def _(pe):
            def landed(u0, i, j, per=SLOTS):
                pe.wait_ge(s_land[(u0 + j) % SLOTS], i * (16 * per // SLOTS) + 16 * ((u0 + j) // SLOTS + 1))

            def slot(u0, j):
                return (u0 + j) % SLOTS

            def banks_read(s):
                if s.a0:
                    pe.wait_ge(s_freeA, s.a0)
                if s.d0:
                    pe.wait_ge(s_freeD, s.d0)

            def bank_free(s, i, c, per=0):
                if isinstance(i, int):
                    if s.c0 + c >= 4:
                        by, n = Stage.readers[s.c0 + c - 4]
                        pe.wait_ge(s_freeA if by == "A" else s_freeD, n)
                elif s.owner == "AD":
                    base, sm = (s.a0, s_freeA) if c % 2 == 0 else (s.d0, s_freeD)
                    pe.wait_ge(sm, i * (per // 2) + (base + c // 2 - 2 + 1))
                elif s.owner == "A":
                    pe.wait_ge(s_freeA, i * per + (s.a0 + c - 3))
                else:
                    pe.wait_ge(s_freeD, i * per + (s.d0 + c - 3))

            def bank(s, c):
                return (s.c0 + c) % 4

            def computed(s, c, mm):
                if s.raises(c)[0] == "used":
                    mm.then_inc(s_used, s.share[1])
                else:
                    mm.then_inc(s_chunk, 1)

            def rows(s, rhs, T, nk=KC, per_chunk=1, ready=None, between=None):
                kper = nk // per_chunk
                rest = s.units % SLOTS if s.units > 3 * SLOTS else s.units

                def unit(i, j):
                    c, part = (j // 3, 0) if s.beside else (j // per_chunk, j % per_chunk)
                    landed(s.u0, i, j)
                    if part == 0:
                        bank_free(s, i, c, SLOTS // per_chunk)
                    for k in range(kper):
                        kk = part * kper + k
                        if ready and j < per_chunk:
                            pe.wait_ge(ready[0], ready[1] + kk)
                        mm = pe.matmul(ps[:, bank(s, c), 0:T], ring[:, slot(s.u0, j), k * P:(k + 1) * P], rhs(kk),
                                       start=kk == 0, stop=kk == nk - 1)
                    mm.then_inc(s_used, 1)

                if s.beside:
                    for j in range(s.chunks):
                        unit(0, 3 * j)
                        ada(*s.beside, 2 * j, 2 * j + 2, s)
                        if between:
                            between(j)
                    return
                for j in range(rest):
                    unit(0, j)
                    if between:
                        between(j)
                if s.units > rest:
                    if rest < 4:
                        banks_read(s)
                    with pe.Fori(0, (s.units - rest) // SLOTS) as i:
                        for j in range(SLOTS):
                            unit(i, rest + j)

            def ada(l, g, a=0, b=16, host=None):
                s = st[f"ada{l}{g}"]
                if a == 0 and not host:
                    bank_free(s, 0, 0)
                for j in range(a, b):
                    k, part = j // 2, j % 2
                    n = 3 * k + 1 + part if host else j
                    first = host.u0 if host else s.u0
                    landed(first, 0, n)
                    for half in range(2):
                        o = 64 * part + 32 * half
                        mm = pe.matmul(ps[o:o + 32, 6 if host else bank(s, 0), :], scond[:, k, :],
                                       ring[:, slot(first, n), half * 512:(half + 1) * 512], start=k == 0,
                                       stop=k == KC - 1)
                    mm.then_inc(s_used, 1)

            def ada_turn(l, g):
                s = st[f"turn{l}{g}"]
                pe.wait_ge(s_freeA, s.a0)
                bank_free(s, 0, 0)
                for c in range(4):
                    mm = pe.transpose(ps[:, bank(s, 0), c * P:(c + 1) * P], stats[:, c * P:(c + 1) * P], ident)
                computed(s, 0, mm)

            def tokens(s, lhs, ntile, after=None):
                c = 0
                for g in range(s.units // 4):
                    for j in range(4):
                        landed(s.u0, 0, 4 * g + j)
                    s0 = slot(s.u0, 4 * g)
                    for q in range(ntile):
                        bank_free(s, 0, c)
                        for k in range(KC):
                            mm = pe.matmul(ps[:, bank(s, c), 0:512], lhs(k, q),
                                           ring[:, s0:s0 + 4, k * P:(k + 1) * P], start=k == 0, stop=k == KC - 1)
                        computed(s, c, mm)
                        if after:
                            after(c)
                        c += 1

            def norm_sums(name):
                N = NORM[name]
                nk = N["nk"]
                inv = const("inv")[:, 32 * N["inv"]:32 * N["inv"] + 32]
                for k in range(nk):
                    o = 32 * (k % 4)
                    pe.wait_ge(s_sqA, N["n0"] + k + 1)
                    if name == "sub":
                        mm = pe.matmul(ps[o:o + 32, 5 + k // 4, :], inv, sq_heads[:, k, :], start=True, stop=True)
                    else:
                        mm = pe.matmul(ps[o:o + 32, 5, 0:N["T"]], inv, sq[:, k, 0:N["T"]], start=k < 4,
                                       stop=k + 4 >= nk)
                mm.then_inc(s_part, 1)

            def norm_stat(name, src=stats):
                N = NORM[name]
                nt = N["T"] // P
                pe.wait_ge(s_acopy, N["n"] + 1)
                if name == "sub":
                    for b in range(2):
                        for q in range(nt):
                            mm = pe.transpose(ps[:, 4 + 3 * b, q * P:(q + 1) * P], stats2[:, b, q * P:(q + 1) * P],
                                              ident)
                else:
                    g = 32 * min(N["nk"], 4)
                    for q in range(nt):
                        mm = pe.matmul(ps[:, 4, q:q + 1], src[0:g, q * P:(q + 1) * P], thirty[0:g, :], start=True,
                                       stop=True)
                mm.then_inc(s_stat, 1)

            def norm_whole(name):
                norm_sums(name)
                norm_stat(name)
                norm_bc(name)

            def norm_beside(name, l, g, turn_first=False):
                ada(l, g, 0, 8)
                norm_sums(name)
                ada(l, g, 8, 12)
                norm_stat(name)
                ada(l, g, 12, 16)
                if turn_first:
                    ada_turn(l, g)
                norm_bc(name)
                if not turn_first:
                    ada_turn(l, g)

            diags = [0]

            def norm_bc(name):
                N = NORM[name]
                for h in range(KC if name == "sub" else 1):
                    diags[0] += 1
                    b = 6 + diags[0] % 2
                    pe.wait_ge(s_diag, diags[0])
                    pe.matmul(ps[:, b, 0:N["T"]], ones, (diag, diag2)[h % 2][:, 0:N["T"] // P, :], start=True,
                              stop=True).then_inc(s_bc, 1)

            def attention(name):
                a, b, _, _ = JOBS[name]

                def scores(j):
                    J, bf = jobs[j], j % 2
                    if j >= 2:
                        pe.wait_ge(s_exp, j - 1)
                    for p in range(2):
                        for n, (l, r, o, w) in enumerate(J["scores"][p]):
                            mm = pe.matmul(ps[:, 4 + 2 * bf + p, o:o + w], l, r, start=n == 0,
                                           stop=n == len(J["scores"][p]) - 1)
                    mm.then_inc(s_scores, 1)

                def turn(j):
                    J, bf = jobs[j], j % 3
                    pe.wait_ge(s_prob, j + 1)
                    for g, blocks in enumerate(J["groups"]):
                        G = J["g0"] + g
                        if G >= 2:
                            pe.wait_ge(s_ptsb, G - 1)
                        for n, (p, k) in enumerate(blocks):
                            src = E[:, bf, p or 0, k * P:(k + 1) * P]
                            mm = pe.transpose(ps[:, G % 2, n * P:(n + 1) * P], src, ident)
                        mm.then_inc(s_pt, 1)

                def values(j):
                    J = jobs[j]
                    if J["first"] and J["o"] >= 2:
                        pe.wait_ge(s_osb, J["o"] - 1)
                    for g, mms in enumerate(J["pv"]):
                        G = J["g0"] + g
                        pe.wait_ge(s_ptsb, G + 1)
                        for o, m, c, v, r, w, first, last in mms:
                            mm = pe.matmul(ps[o:o + m, 2 + J["o"] % 2, c:c + w], v, PT[:, G % 4, r:r + w],
                                           start=first, stop=last)
                        mm.then_inc(s_pv, 1)

                for i in range(a, b + BEHIND):
                    if i < b:
                        scores(i)
                    if a <= i - 2 < b:
                        turn(i - 2)
                    if a <= i - BEHIND < b:
                        values(i - BEHIND)

            def all_read(s):
                if s.a1:
                    pe.wait_ge(s_freeA, s.a1)
                if s.d1:
                    pe.wait_ge(s_freeD, s.d1)

            def rotate(c, pair, rot):
                if c >= 4:
                    pe.wait_ge(s_ropeD, c - 3)
                for n, a in enumerate(pair):
                    mm = pe.matmul(ps[:, 4 + c % 4, n * LAT:(n + 1) * LAT], rot, a, start=True, stop=True)
                mm.then_inc(s_rope, 1)

            def heads_read(name):
                pe.wait_ge(s_osb, JOBS[name][3])

            pe.wait_ge(s_small, 48)
            pe.wait_ge(s_scond, 2)

            def norm_steps(name):
                def between(c):
                    if c < 3:
                        (norm_sums, norm_stat, norm_bc)[c](name)
                return between

            rows(st["memk"], lambda k: memG[:, k, :], LAT, ready=(s_nD, NORM["nmem"]["n0"] + 1),
                 between=norm_steps("nmem"))
            tokens(st["memva"], lambda k, q: memG[:, k, q * P:(q + 1) * P], 2,
                   lambda c: norm_sums("n0") if c == 0 else None)
            ada_turn(0, 0)
            norm_stat("n0", stats2[:, 0, :])
            tokens(st["memvb"], lambda k, q: memG[:, k, q * P:(q + 1) * P], 2,
                   lambda c: norm_bc("n0") if c == 0 else None)
            rows(st["q0"], lambda k: xn[:, k, :], TOK, ready=(s_nA, NORM["n0"]["a0"] + 1))
            rows(st["k0"], lambda k: xn[:, k, :], TOK)
            ada_turn(0, 1)

            def rotate_two(c):
                if c == 0:
                    pe.wait_ge(s_freeA, st["k0"].a1)
                rotate(c, [qk[:, 2 * c, lat], qk[:, 2 * c + 1, lat]], const("rot_a"))

            tokens(st["v0"], lambda k, q: xn[:, k, q * P:(q + 1) * P], 4, rotate_two)
            all_read(st["v0"])
            pe.wait_ge(s_ropeD, 8)
            attention("da")
            heads_read("da")
            norm_beside("sub", 0, 2)
            rows(st["wo0"], lambda k: xn[:, k, :], TOK, ready=(s_nD, NORM["sub"]["n0"] + 1))
            norm_beside("n1", 1, 0)
            rows(st["gu0"], lambda k: xn[:, k, :], TOK, ready=(s_nA, NORM["n1"]["a0"] + 1))
            rows(st["down0"], lambda k: hid[:, k, :], TOK, nk=FC, per_chunk=2, ready=(s_freeD, st["gu0"].d0 + 1))
            norm_beside("n2", 1, 1)
            rows(st["q1"], lambda k: xn[:, k, lat], LAT, ready=(s_nA, NORM["n2"]["a0"] + 1))
            rows(st["k1"], lambda k: xn[:, k, :], TOK)
            tokens(st["v1"], lambda k, q: xn[:, k, q * P:(q + 1) * P], 4)
            all_read(st["v1"])
            pe.wait_ge(s_biasm, 1)
            attention("na")
            heads_read("na")
            rows(st["wo1"], lambda k: x2[:, k, :], LAT)
            norm_beside("n3", 1, 2, turn_first=True)
            rows(st["gu1"], lambda k: x2[:, k, :], LAT, ready=(s_nA, NORM["n3"]["a0"] + 1))
            rows(st["down1"], lambda k: hid[:, k, 0:LAT], LAT, nk=FC, per_chunk=2, ready=(s_freeD, st["gu1"].d0 + 1))
            norm_whole("nfm")
            rows(st["win"], lambda k: x2[:, k, :], LAT, ready=(s_nD, NORM["nfm"]["n0"] + 1))


            def small_norms(c):
                for n, name in enumerate(("nq", "nkv")):
                    if c == 6 * n + 1:
                        norm_sums(name)
                    elif c == 6 * n + 3:
                        norm_stat(name)
                    elif c == 6 * n + 5:
                        norm_bc(name)

            rows(st["wing"], lambda k: x2[:, k, :], LAT, between=small_norms)
            rows(st["winr"], lambda k: x2[:, k, :], LAT)
            pe.wait_ge(s_nD, NORM["nkv"]["nd"])
            small_rows = [("uq", 4, 2, lambda k: u[:, 24 + k, :]), ("uk", 8, 1, lambda k: u[:, 26, :])]
            for name, mper, nk, rhs in small_rows:
                s = st[name]
                for c in range(s.chunks):
                    j = c // mper
                    if c % mper == 0:
                        landed(s.u0, 0, j)
                    bank_free(s, 0, c)
                    for k in range(nk):
                        n = (c % mper) * nk + k
                        mm = pe.matmul(ps[:, bank(s, c), 0:LAT], ring[:, slot(s.u0, j), n * P:(n + 1) * P], rhs(k),
                                       start=k == 0, stop=k == nk - 1)
                    computed(s, c, mm)
            for c, pair in enumerate(([mq[:, 8, :], mq[:, 9, :]], [mq[:, 10, :], mq[:, 11, :]], [u[:, 43, :]])):
                rotate(8 + c, pair, const("rot_b"))
            s = st["uv"]
            landed(s.u0, 0, 0)
            for c in range(4):
                bank_free(s, 0, c)
                computed(s, c, pe.matmul(ps[:, bank(s, c), 0:512], u[:, 26, (c // 2) * P:(c // 2 + 1) * P],
                                         ring[:, slot(s.u0, 0), (c % 2) * 512:(c % 2 + 1) * 512], start=True,
                                         stop=True))
            all_read(st["uv"])
            pe.wait_ge(s_ropeD, 11)
            attention("mla")
            heads_read("mla")
            pe.wait_ge(s_conv, 1)
            rows(st["conv"], lambda k: u[:, 8 + k, :], LAT)
            rows(st["mla"], lambda k: x2[:, k, :], LAT)
            pe.wait_ge(s_freeD, st["mla"].d1)
            rows(st["mix"], lambda k: u[:, 16 + k, :], LAT)
            rows(st["memq"], lambda k: x2[:, k, :], LAT, ready=(s_nD, NORM["nq2"]["n0"] + 1),
                 between=norm_steps("nq2"))
            all_read(st["memq"])
            attention("mem")
            heads_read("mem")
            rows(st["memo"], lambda k: x2[:, k, :], LAT)
            norm_whole("nmoe")
            for k in range(KC):
                o = 32 * (k % 4)
                pe.wait_ge(s_nD, NORM["nmoe"]["n0"] + k + 1)
                mm = pe.matmul(ps[o:o + 32, 5, 0:LAT], wr[:, k, :], x2[:, k, :], start=k < 4, stop=k >= 4)
            mm.then_inc(s_logits, 1)
            for q in range(2):
                for k in range(KC):
                    mm = pe.transpose(ps[:, 2 * q + k // 4, (k % 4) * P:(k % 4 + 1) * P],
                                      x2[:, k, q * P:(q + 1) * P], ident)
                if q == 0:
                    pe.wait_ge(s_acopy, NORM["nmoe"]["n"] + 2)
                    for r in range(2):
                        lg = pe.matmul(ps[:, 4, NE * r:NE * r + NE], stats[:, r * P:(r + 1) * P], const("groups"),
                                       start=True, stop=True)
                    lg.then_inc(s_moe, 1)
            mm.then_inc(s_moe, 1)
            pe.wait_ge(s_moeD, 1)
            for q in range(2):
                mm = pe.transpose(ps[0:NE, 7, q * P:(q + 1) * P], aff[:, q, :], ident)
            mm.then_inc(s_moe, 1)
            pe.wait_ge(s_moeA, 1)
            for q in range(2):
                for k in range(KC):
                    pe.matmul(ps[:, 2 * q + k // 4, (k % 4) * P:(k % 4 + 1) * P], h2[:, k, q * P:(q + 1) * P], ident,
                              start=k % 4 == 0, stop=False, skip_group_check=True)
            pe.wait_ge(s_moeD, 2)
            for a in range(2):
                mm = pe.matmul(ps[:, 4 + a, :], ones[0:NE, :], spread[:, a, :], start=True, stop=True)
            mm.then_inc(s_moe, 1)
            pe.wait_ge(s_sel, 1)
            for k in range(KC):
                for q in range(2):
                    mm = pe.matmul(ps[:, 6 + k // 4, (k % 4) * P:(k % 4 + 1) * P], hs[:, q, k * P:(k + 1) * P],
                                   sel[:, q, 0:P], start=q == 0, stop=q == 1)
            mm.then_inc(s_moe, 1)
            u0 = st["experts"].u0

            def other_tokens(k):
                pe.wait_ge(s_moeA, max(2, 2 + k - 1))
                for q in range(2):
                    mm = pe.matmul(ps[:, 6 + k % 2, P:512], hs[:, q, k * P:(k + 1) * P], sel[:, q, P:512],
                                   start=q == 0, stop=q == 1)
                mm.then_inc(s_moe, 1)

            def turned_choices(k):
                if k not in (2, 5):
                    return
                r = k // 3
                pe.wait_ge(s_moeA, 2 + KC + r)
                for g in range(4):
                    for q in range(2):
                        o = (g % 2) * LAT + q * P
                        mm = pe.transpose(
                            ps[:, 6 + g // 2, o:o + P],
                            gsel[:, q, 8 * r + 2 * g:8 * r + 2 * g + 2, :, :].rearrange("p e h n -> p (e h n)"), ident)
                mm.then_inc(s_moe, 1)

            def product(i, base, part, lhs, ahead=False, between=None):
                for j in range(16):
                    k, e = j // 2, j % 2
                    n = 16 * part + j
                    if ahead:
                        src = early[j]
                    else:
                        pe.wait_ge(s_eland[(base + n) % EXPERT_SLOTS],
                                   i * (48 // EXPERT_SLOTS * 16) + 16 * ((base + n) // EXPERT_SLOTS + 1))
                        src = expert_ring[(base + n) % EXPERT_SLOTS]
                    for h in range(2):
                        o = 64 * e + 32 * h
                        mm = pe.matmul(ps[o:o + 32, (4, 5, 7)[part], :], lhs(k, e), src[:, h * 512:(h + 1) * 512],
                                       start=k == 0, stop=k == KC - 1)
                    if not ahead:
                        mm.then_inc(s_used, 1)
                    if between and e:
                        between(k)
                return mm

            def pair_steps(i, pair, base):
                pe.wait_ge(s_xe, i + (pair + 1))
                if pair == 0:
                    pe.wait_ge(s_moeD, 3)
                product(i, base, 0, lambda k, e: xe[:, k, e * CAP:(e + 1) * CAP],
                        between=other_tokens if pair == 0 else None)
                if pair == 0:
                    pe.wait_ge(s_moeD, 4)
                product(i, base, 1, lambda k, e: xe[:, k, e * CAP:(e + 1) * CAP],
                        between=turned_choices if pair == 0 else None)
                if pair == 0:
                    pe.wait_ge(s_moeA, 4 + KC)
                pe.wait_ge(s_he, i + (pair + 1))
                for c in range(4):
                    mm = pe.transpose(ps[:, 6, c * P:(c + 1) * P], hp[:, c * P:(c + 1) * P], ident)
                mm.then_inc(s_hturn, 1)
                pe.wait_ge(s_hT, i + (pair + 1))
                if pair == 0:
                    pe.wait_ge(s_early, 16 * EARLY)
                mm = product(i, base, 2,
                             lambda k, e: hTe[:, k % 4, 64 * e + 32 * (k // 4):64 * e + 32 * (k // 4) + 32],
                             ahead=pair == 0)
                if pair == 0:
                    mm.then_inc(s_moe, 1)
                pe.wait_ge(s_ye, i + (pair + 1))
                pe.wait_ge(s_gx, i + (pair + 1))
                for q in range(2):
                    if q:
                        mm.then_inc(s_half, 1)
                    for h in range(2):
                        mm = pe.matmul(ps[:, 2 * q + h, :], gx[:, h, q * P:(q + 1) * P], ye, start=False, stop=False,
                                       skip_group_check=True)
                mm.then_inc(s_scat, 1)

            pair_steps(0, 0, 0)
            with pe.Fori(0, NE // 2 - 1) as i:
                pair_steps(i, 1, 32)

        def chunk_ready(eng, s, i, c, per=0):
            which, n = s.raises(c)
            eng.wait_ge(s_used if which == "used" else s_chunk, i * (per * s.units // s.chunks) + n)

        def square_inputs(name, k):
            added = {"n1": "wo0", "n2": "down0", "n3": "wo1", "nfm": "down1", "nq2": "mix", "nmoe": "memo"}
            if name in added:
                return s_freeD, st[added[name]].d0 + k + 1
            return {"nmem": (s_mem, 16), "n0": (s_x, 32), "sub": (s_osb, k + 1), "nq": (s_freeA, st["win"].a1),
                    "nkv": (s_freeA, st["win"].a1)}[name]

        @block.scalar
        def _(act):
            def squares(name, only=None):
                N = NORM[name]
                dst, T = (sq_heads, TOK) if name == "sub" else (sq, N["src"].shape[-1])
                if N["n"] and not only:
                    act.wait_ge(s_part, N["n"])
                for k in range(N["nk"]) if only is None else (only,):
                    act.wait_ge(*square_inputs(name, k))
                    ins = act.activation(dst[:, k, 0:T], N["src"][:, k, :], ACT.Square)
                    if name == "nfm":
                        ins = act.activation(dst[:, k, T:2 * T], N["src"][:, k, :], ACT.Square, scale=col("final", k))
                    ins.then_inc(s_sqA, 1)

            def group_sums(name, dst=stats):
                N = NORM[name]
                act.wait_ge(s_part, N["n"] + 1)
                if name == "sub":
                    act.activation(stats2, ps[:, 5:7, :], ACT.Copy).then_inc(s_acopy, 1)
                else:
                    g = 32 * min(N["nk"], 4)
                    act.activation(dst[0:g, 0:N["T"]], ps[0:g, 5, 0:N["T"]], ACT.Copy).then_inc(s_acopy, 1)

            def ada_rows(l, g, bank=None):
                s = st[f"ada{l}{g}"]
                chunk_ready(act, s, 0, 0)
                act.activation(stats, ps[:, bank or s.c0 % 4, :], ACT.Copy).then_inc(s_freeA, 1)

            def shift(name):
                N = NORM[name]
                l, part = MODS[N["m"]]
                for k in range(KC):
                    act.wait_ge(s_nD, N["n0"] + k + 1)
                    if N["T"] == TOK:
                        act.activation(xn[:, k, 0:CTX], xn[:, k, 0:CTX], ACT.Identity,
                                       bias=mod[:, l, 8 * part + k, 0:1])
                        dst = xn[:, k, lat]
                    else:
                        dst = xn[:, k, 0:LAT]
                    act.activation(dst, dst, ACT.Identity, bias=mod[:, l, 8 * part + k, 1:2]).then_inc(s_nA, 1)

            def copy_out(s, dst, scale=1.0, func=ACT.Copy, bias_col=None, only=None):
                for c in only or range(s.chunks):
                    chunk_ready(act, s, 0, c)
                    d = dst(c)
                    src = ps[:, (s.c0 + c) % 4, 0:d.shape[-1]]
                    if bias_col is not None:
                        act.activation(d, src, func, bias=bias_col(c)).then_inc(s_freeA, 1)
                    else:
                        act.activation(d, src, func, scale=scale).then_inc(s_freeA, 1)

            def silu(s, T):
                def one(i, m):
                    chunk_ready(act, s, i, 2 * m, 8)
                    if m >= 2 or not isinstance(i, int):
                        act.wait_ge(s_freeD, i * 4 + (s.d0 + m - 1))
                    act.activation(silu_out[:, m % 2, 0:T], ps[:, (s.c0 + 2 * m) % 4, 0:T],
                                   ACT.Silu).then_inc(s_freeA, 1)
                for m in range(2):
                    one(0, m)
                with act.Fori(0, (FC - 2) // 4) as i:
                    for m in range(4):
                        one(i, 2 + m)

            def exps(j):
                J, bf = jobs[j], j % 2
                act.wait_ge(s_max, j + 1)
                if j >= 3:
                    act.wait_ge(s_pt, groups_before(j - 2))
                for p in range(2):
                    mm = act.activation(E[:, j % 3, p, 0:J["n"]], ps[:, 4 + 2 * bf + p, 0:J["n"]], ACT.Exp,
                                        bias=anm[:, 2 * bf + p:2 * bf + p + 1],
                                        accum_out=asum[:, 2 * bf + p:2 * bf + p + 1])
                mm.then_inc(s_exp, 1)

            def turned(j):
                J = jobs[j]
                for g, blocks in enumerate(J["groups"]):
                    G, w = J["g0"] + g, len(blocks) * P
                    act.wait_ge(s_pt, G + 1)
                    if G >= 4:
                        act.wait_ge(s_pv, G - 3)
                    act.activation(PT[:, G % 4, 0:w], ps[:, G % 2, 0:w], ACT.Copy).then_inc(s_ptsb, 1)

            def attention(name):
                a, b, _, _ = JOBS[name]
                for i in range(a, b + 2):
                    if a <= i - 2:
                        turned(i - 2)
                    if i < b:
                        exps(i)
                    done = i - BEHIND - 1
                    if name == "da" and done >= a and jobs[done]["evac"] is not None:
                        squares("sub", jobs[done]["o"])
                if name == "da":
                    for j in range(b + 2 - BEHIND - 1, b):
                        if jobs[j]["evac"] is not None:
                            squares("sub", jobs[j]["o"])

            squares("nmem")
            act.wait_ge(s_small, 48)
            act.wait_ge(s_scond, 1)
            act.activation(scond[:, :, 0:2], cond[:, :, :], ACT.Silu).then_inc(s_scond, 1)
            group_sums("nmem")
            act.wait_ge(s_gain, 1)
            act.activation(lams[:, 2:4], lams[:, 0:2], ACT.Exp).then_inc(s_lamex, 1)
            squares("n0")
            ada_rows(0, 0, bank=6)


            def memory_values(half, q):
                s = st[("memva", "memvb")[half]]
                chunk_ready(act, s, 0, q)
                act.activation(memv[:, q, 512 * half:512 * half + 512], ps[:, (s.c0 + q) % 4, :], ACT.Identity,
                               scale=memr[:, q:q + 1]).then_inc(s_freeA, 1)

            act.wait_ge(s_diag, 1)
            memory_values(0, 0)
            group_sums("n0", stats2[:, 0, :])
            memory_values(0, 1)
            memory_values(1, 0)
            act.wait_ge(s_gain, 2)
            shift("n0")
            memory_values(1, 1)
            copy_out(st["q0"], lambda c: qk[:, c, :], scale=0.125)
            ada_rows(0, 1, bank=6)
            copy_out(st["k0"], lambda c: qk[:, 8 + c, :])
            copy_out(st["v0"], lambda c: vv[:, c % 4, (c // 4) * 512:(c // 4 + 1) * 512])
            attention("da")
            group_sums("sub")
            ada_rows(0, 2)
            squares("n1")
            group_sums("n1")
            ada_rows(1, 0)
            shift("n1")
            silu(st["gu0"], TOK)
            squares("n2")
            group_sums("n2")
            ada_rows(1, 1)
            shift("n2")
            copy_out(st["q1"], lambda c: qk[:, c, lat], scale=0.125)
            copy_out(st["k1"], lambda c: qk[:, 8 + c, :])
            copy_out(st["v1"], lambda c: vv[:, c % 4, (c // 4) * 512:(c // 4 + 1) * 512])
            attention("na")
            squares("n3")
            group_sums("n3")
            ada_rows(1, 2)
            shift("n3")
            silu(st["gu1"], LAT)
            squares("nfm")
            group_sums("nfm")
            s = st["win"]
            rest = s.units % SLOTS
            for c in range(rest):
                chunk_ready(act, s, 0, c)
                act.activation(u[:, c, :], ps[:, (s.c0 + c) % 4, 0:LAT], ACT.Copy).then_inc(s_freeA, 1)
            with act.Fori(0, s.units // SLOTS) as i:
                for c in range(rest, rest + SLOTS):
                    chunk_ready(act, s, i, c, SLOTS)
                    act.activation(big[:, bass.ds(i * (SLOTS * LAT) + c * LAT, LAT)], ps[:, (s.c0 + c) % 4, 0:LAT],
                                   ACT.Copy).then_inc(s_freeA, 1)

            def gates(a, b):
                copy_out(st["wing"], lambda c: u[:, 27 + c, :], func=ACT.Sigmoid,
                         bias_col=lambda c: col("b_gate", c), only=range(a, b))

            squares("nq")
            gates(0, 2)
            group_sums("nq")
            squares("nkv")
            gates(2, 8)
            group_sums("nkv")
            gates(8, 16)
            copy_out(st["winr"], lambda c: u[:, 43, :])
            copy_out(st["uq"], lambda c: mq[:, c, :], scale=float(192 ** -0.5))
            copy_out(st["uk"], lambda c: mk[:, c, :])
            copy_out(st["uv"], lambda c: mv[:, c // 2, (c % 2) * 512:(c % 2 + 1) * 512])
            attention("mla")
            squares("nq2")
            group_sums("nq2")
            attention("mem")
            squares("nmoe")
            group_sums("nmoe")
            act.wait_ge(s_logits, 1)
            act.activation(stats[:, 0:LAT], ps[:, 5, 0:LAT], ACT.Copy).then_inc(s_acopy, 1)
            act.wait_ge(s_rmax, 1)
            for q in range(2):
                ins = act.activation(aff[:, q, :], ps[:, 4, NE * q:NE * (q + 1)], ACT.Exp,
                                     bias=small[:, 120 + q:121 + q], accum_out=small[:, 122 + q:123 + q])
            ins.then_inc(s_rexp, 1)
            act.wait_ge(s_moe, 2)
            for q in range(2):
                ins = act.activation(hs[:, q, :].rearrange("p (a b) -> p a b", a=2), ps[:, 2 * q:2 * q + 2, :],
                                     ACT.Copy)
            ins.then_inc(s_moeA, 1)
            act.wait_ge(s_moe, 5)
            gathered = ps[:, 6:8, :].rearrange("p a (k n) -> p (a k) n", k=4)
            act.activation(xe, gathered[:, :, 0:2 * CAP], ACT.Copy).then_inc(s_xe, 1)
            act.activation(xg[:, :, 0:P], gathered, ACT.Copy).then_inc(s_moeA, 1)
            u0 = st["experts"].u0

            def pair_steps(i, pair, base):
                if isinstance(i, int):
                    for k in range(KC):
                        act.wait_ge(s_moe, 6 + k)
                        act.activation(xg[:, k, P:512], ps[:, 6 + k % 2, P:512], ACT.Copy).then_inc(s_moeA, 1)
                act.wait_ge(s_used, i * 48 + (base + 16))
                act.activation(sg, ps[:, 4, :], ACT.Silu).then_inc(s_sg, 1)
                if isinstance(i, int):
                    for r in range(2):
                        act.wait_ge(s_moe, 14 + r)
                        act.activation(gT[:, 4 * r:4 * r + 4, :].rearrange("p (a g) t -> p a (g t)", a=2),
                                       ps[:, 6:8, :], ACT.Copy).then_inc(s_moeA, 1)
                act.wait_ge(s_hturn, i + (pair + 1))
                act.activation(hTe, ps[:, 6, :].rearrange("p (c n) -> p c n", c=4), ACT.Copy).then_inc(s_hT, 1)
                if isinstance(i, int):
                    act.wait_ge(s_moe, 16)
                else:
                    act.wait_ge(s_used, i * 48 + (base + 48))
                act.activation(ye, ps[:, 7, :], ACT.Copy).then_inc(s_ye, 1)

            pair_steps(0, 0, u0)
            with act.Fori(0, NE // 2 - 1) as i:
                pair_steps(i, 1, u0 + 32)
            for q in range(2):
                act.wait_ge((s_half, s_scat)[q], NE // 2)
                act.activation(otok[:, q, :].rearrange("p (a b) -> p a b", a=2), ps[:, 2 * q:2 * q + 2, :], ACT.Square,
                               accum_out=small[:, 112 + q:113 + q]).then_inc(s_ssq, 1)

        @block.vector
        def _(dve):
            steps = Steps(dve, c_dve)
            link = steps.link
            neg_lam = lams[:, 5:6]
            gsub = small[:, 124:125]

            def newton(v, y, z):
                link(dve.tensor_scalar(y.bitcast(I32), v.bitcast(I32), -0.5, float(0x5F3759DF), ALU.mult, ALU.add))
                for _ in range(3):
                    link(dve.tensor_tensor(z, y, y, ALU.mult))
                    link(dve.scalar_tensor_tensor(z, z, -0.5, v, ALU.mult, ALU.mult))
                    link(dve.scalar_tensor_tensor(y, z, 1.5, y, ALU.add, ALU.mult))

            def weighted(name, k):
                N = NORM[name]
                dve.tensor_scalar(N["dst"][:, k, :], N["src"][:, k, :], col(N["g"], k), None,
                                  ALU.mult).then_inc(s_nD, 1)

            def scaled_out(s, dst, by, bc):
                row = stats2[:, 1, 0:LAT]
                link(dve.tensor_copy(row, bc))
                for c in range(s.chunks):
                    chunk_ready(dve, s, 0, c)
                    dve.scalar_tensor_tensor(dst[:, c, :], ps[:, (s.c0 + c) % 4, 0:LAT], by, row, ALU.mult,
                                             ALU.mult).then_inc(s_freeD, 1)

            def rstd(name, n, r=rs):
                dve.wait_ge(s_stat, NORM[name]["n"] + 1)
                v = var[:, 0:n]
                if name == "sub":
                    for b in range(2):
                        ins = dve.tensor_scalar(
                            v[:, 16 * b:16 * b + 16].rearrange("p (j q) -> p q j", j=4),
                            ps[:, 4 + 3 * b, :].rearrange("p (q j r) -> p q j r", q=4, j=4)[:, :, :, 0], EPS, None,
                            ALU.add)
                    link(ins)
                else:
                    link(dve.tensor_scalar(v, ps[:, 4, 0:n], EPS, None, ALU.add))
                newton(v, r[:, 0:n], tmp[:, 0:n])

            diags = [0]

            def diagonal(r, nt, buffer=diag, between=0):
                if diags[0] > between:
                    dve.wait_ge(s_bc, diags[0] - between)
                diags[0] += 1
                dve.tensor_tensor(buffer[:, 0:nt, :], ident.unsqueeze(1).to_broadcast([P, nt, P]),
                                  r.unsqueeze(2).to_broadcast([P, nt, P]), ALU.mult).then_inc(s_diag, 1)

            def spread_row(nt):
                dve.wait_ge(s_bc, diags[0])
                return ps[:, 6 + diags[0] % 2, 0:nt * P]

            def broadcast(r, nt):
                diagonal(r, nt)
                return spread_row(nt)

            def norm(name):
                nt = NORM[name]["T"] // P
                rstd(name, nt)
                scale(name, broadcast(rs[:, 0:nt], nt))

            def scale(name, bc):
                N = NORM[name]
                for k in range(N["nk"]):
                    src, dst = N["src"][:, k, :], N["dst"][:, k, :]
                    if N["m"] is None:
                        ins = dve.scalar_tensor_tensor(dst, src, col(N["g"], k), bc, ALU.mult, ALU.mult)
                    elif N["T"] == TOK:
                        for c, sl in enumerate((slice(0, CTX), lat)):
                            ins = dve.scalar_tensor_tensor(dst[:, sl], src[:, sl], gain[:, N["m"], k, c:c + 1],
                                                           bc[:, sl], ALU.mult, ALU.mult)
                    else:
                        ins = dve.scalar_tensor_tensor(dst, src, gain[:, N["m"], k, 1:2], bc, ALU.mult, ALU.mult)
                    ins.then_inc(s_nD, 1)

            def head_norms():
                rstd("sub", 32)
                link(dve.tensor_scalar(gsub, col("subln"), 1.0 - LAM_INIT, None, ALU.mult))
                diagonal(rs[:, 0:4], 4)
                for h in range(KC):
                    n = diags[0]
                    bc = ps[:, 6 + n % 2, :]
                    if h + 1 < KC:
                        diagonal(rs[:, 4 * h + 4:4 * h + 8], 4, (diag, diag2)[(h + 1) % 2], 1)
                    dve.wait_ge(s_bc, n)
                    dve.scalar_tensor_tensor(xn[:, h, :], xn[:, h, :], gsub, bc, ALU.mult, ALU.mult).then_inc(s_nD, 1)

            def ada(l, g):
                s = st[f"turn{l}{g}"]
                chunk_ready(dve, s, 0, 0)
                src = ps[:, s.c0 % 4, :].rearrange("p (c j r) -> p j c r", c=4, j=4)
                for o in range(2):
                    ins = dve.tensor_tensor(mod[:, l, 16 * g:16 * g + 16, o].rearrange("p (j c) -> p j c", j=4),
                                            src[:, :, :, o],
                                            col("ada_b", 48 * l + 16 * g, 16).rearrange("p (j c) -> p j c", j=4),
                                            ALU.add)
                ins.then_inc(s_freeD, 1)

            def gains(m, after, g):
                l, part = MODS[m]
                dve.wait_ge(s_freeD, after.d1)
                dve.scalar_tensor_tensor(gain[:, m, :, :], mod[:, l, 8 * (part + 1):8 * (part + 2), :], 1.0,
                                         col(g, 0, 8).unsqueeze(2).to_broadcast([P, 8, 2]), ALU.add,
                                         ALU.mult).then_inc(s_gain, 1)

            def gated_add(s, l, part, T):
                for c in range(KC):
                    chunk_ready(dve, s, 0, c)
                    b = (s.c0 + c) % 4
                    if T == TOK:
                        dve.scalar_tensor_tensor(hT[:, c, 0:CTX], ps[:, b, 0:CTX], mod[:, l, 8 * part + c, 0:1],
                                                 hT[:, c, 0:CTX], ALU.mult, ALU.add)
                    dve.scalar_tensor_tensor(hT[:, c, lat], ps[:, b, T - LAT:T], mod[:, l, 8 * part + c, 1:2],
                                             hT[:, c, lat], ALU.mult, ALU.add).then_inc(s_freeD, 1)

            def add(s, c):
                chunk_ready(dve, s, 0, c)
                dve.tensor_tensor(hT[:, c, lat], ps[:, (s.c0 + c) % 4, 0:LAT], hT[:, c, lat],
                                  ALU.add).then_inc(s_freeD, 1)

            def products(s, T):
                def one(i, m):
                    chunk_ready(dve, s, i, 2 * m + 1, 8)
                    dve.wait_ge(s_freeA, i * 4 + (s.a0 + m + 1))
                    dve.tensor_tensor(big[:, bass.ds(i * (4 * TOK) + m * TOK, T)], silu_out[:, m % 2, 0:T],
                                      ps[:, (s.c0 + 2 * m + 1) % 4, 0:T], ALU.mult).then_inc(s_freeD, 1)
                for m in range(2):
                    one(0, m)
                with dve.Fori(0, (FC - 2) // 4) as i:
                    for m in range(4):
                        one(i, 2 + m)

            def rope(first, xs, cos, sin):
                for c, x in enumerate(xs, first):
                    dve.wait_ge(s_rope, c + 1)
                    n = x.shape[1]
                    a, b = ropet[:, 2 * (c % 2), 0:n, :], ropet[:, 2 * (c % 2) + 1, 0:n, :]
                    rot = ps[:, 4 + c % 4, 0:n * LAT].rearrange("p (n t) -> p n t", n=n)
                    dve.tensor_tensor(a, x, cos.unsqueeze(1).to_broadcast([P, n, LAT]), ALU.mult)
                    link(dve.tensor_tensor(b, rot, sin.unsqueeze(1).to_broadcast([P, n, LAT]), ALU.mult))
                    dve.tensor_tensor(x, a, b, ALU.add).then_inc(s_ropeD, 1)

            def maxima(j):
                J, bf = jobs[j], j % 2
                dve.wait_ge(s_scores, j + 1)
                dve.tensor_reduce(anm[:, 2 * bf:2 * bf + 2], ps[:, 4 + 2 * bf:6 + 2 * bf, 0:J["n"]], AX.X, ALU.max,
                                  negate=True).then_inc(s_max, 1)

            def normalise(j):
                J, bf = jobs[j], j % 2
                dve.wait_ge(s_exp, j + 1)
                r = arec[:, 2 * bf:2 * bf + 2]
                link(dve.reciprocal(r, asum[:, 2 * bf:2 * bf + 2]))
                n = J["n"]
                e0, e1 = E[:, j % 3, 0, 0:n], E[:, j % 3, 1, 0:n]
                if J["da"]:
                    dve.tensor_scalar(r[:, 1:2], r[:, 1:2], neg_lam, None, ALU.mult)
                    link(dve.tensor_scalar(e0, e0, r[:, 0:1], None, ALU.mult))
                    dve.scalar_tensor_tensor(e0, e1, r[:, 1:2], e0, ALU.mult, ALU.add).then_inc(s_prob, 1)
                else:
                    dve.tensor_scalar(e0, e0, r[:, 0:1], None, ALU.mult)
                    dve.tensor_scalar(e1, e1, r[:, 1:2], None, ALU.mult).then_inc(s_prob, 1)

            def outs(j):
                J = jobs[j]
                if J["evac"] is None:
                    return
                dve.wait_ge(s_pv, groups_before(j + 1))
                src = ps[:, 2 + J["o"] % 2, 0:J["out"][2]]
                if len(J["evac"].shape) == 3:
                    src = src.rearrange("p (a t) -> p a t", a=2)
                dve.tensor_copy(J["evac"], src).then_inc(s_osb, 1)

            def attention(name):
                a, b, _, _ = JOBS[name]
                for i in range(a, b + BEHIND):
                    if i < b:
                        maxima(i)
                    if a <= i - 1 < b:
                        normalise(i - 1)
                    if a <= i - BEHIND < b:
                        outs(i - BEHIND)

            dve.memset(thirty[:, :], 1.0 / 32)
            dve.memset(wr[:, :, :], 0.0)
            dve.memset(scond[:, :, :], 0.0).then_inc(s_scond, 1)
            dve.wait_ge(s_lamin, 16)
            for a in range(2):
                link(dve.tensor_tensor(small[:, 128:192], lamv[:, 2 * a, :], lamv[:, 2 * a + 1, :], ALU.mult))
                ins = dve.tensor_reduce(lams[:, a:a + 1], small[:, 128:192], AX.X, ALU.add)
                if a == 0:
                    link(ins)
            ins.then_inc(s_gain, 1)
            dve.wait_ge(s_mem, 16)
            dve.wait_ge(s_small, 48)
            for k in range(KC):
                weighted("nmem", k)
            rstd("nmem", 2, memr)
            scaled_out(st["memk"], memk, 1.0, broadcast(memr, 2))
            ada(0, 0)
            gains(0, st["turn00"], "mix0")
            dve.wait_ge(s_lamex, 1)
            link(dve.tensor_tensor(lams[:, 4:5], lams[:, 3:4], lams[:, 2:3], ALU.subtract))
            link(dve.tensor_scalar(neg_lam, lams[:, 4:5], -LAM_INIT, None, ALU.add))
            dve.wait_ge(s_gain, 2)
            norm("n0")
            ada(0, 1)
            rope(0, [qk[:, 2 * c:2 * c + 2, lat] for c in range(8)], const("cos"), const("sin"))
            attention("da")
            head_norms()
            ada(0, 2)
            gains(1, st["turn02"], "ffn0")
            gated_add(st["wo0"], 0, 2, TOK)
            norm("n1")
            ada(1, 0)
            gains(2, st["turn10"], "mix1")
            products(st["gu0"], TOK)
            gated_add(st["down0"], 0, 5, TOK)
            norm("n2")
            ada(1, 1)
            attention("na")
            gated_add(st["wo1"], 1, 2, LAT)
            rstd("n3", 2)
            diagonal(rs[:, 0:2], 2)
            ada(1, 2)
            gains(3, st["turn12"], "ffn1")
            dve.wait_ge(s_gain, 5)
            scale("n3", spread_row(2))
            products(st["gu1"], LAT)
            gated_add(st["down1"], 1, 5, LAT)
            dve.wait_ge(s_stat, NORM["nfm"]["n"] + 1)
            link(dve.tensor_scalar(var[:, 0:2], ps[:, 4, 0:2], EPS, None, ALU.add))
            link(dve.scalar_tensor_tensor(var[:, 2:4], var[:, 0:2], EPS, ps[:, 4, 2:4], ALU.mult, ALU.add))
            newton(var[:, 0:4], rs[:, 0:4], tmp[:, 0:4])
            diagonal(rs[:, 0:4], 4)
            link(dve.tensor_tensor(small[:, 128:136], col("final", 0, 8), col("mix2", 0, 8), ALU.mult))
            bc = spread_row(4)
            for k in range(KC):
                dve.scalar_tensor_tensor(x2[:, k, :], hT[:, k, lat], small[:, 128 + k:129 + k], bc[:, LAT:2 * LAT],
                                         ALU.mult, ALU.mult).then_inc(s_nD, 1)
            for k in range(KC):
                ins = dve.scalar_tensor_tensor(hT[:, k, lat], hT[:, k, lat], col("final", k), bc[:, 0:LAT], ALU.mult,
                                               ALU.mult)
            link(ins)
            norm("nq")
            norm("nkv")
            link(dve.tensor_tensor(u[:, 0:8, :], u[:, 0:8, :], u[:, 16:24, :], ALU.mult))
            for k in range(KC):
                ins = dve.tensor_scalar(u[:, 16 + k, :], u[:, k, :], col("conv_w", 8 + k), col("conv_b", k), ALU.mult,
                                        ALU.add)
            link(ins)
            for tap, o, i in ((0, slice(1, LAT), slice(0, LAT - 1)), (2, slice(0, LAT - 1), slice(1, LAT))):
                for k in range(KC):
                    ins = dve.scalar_tensor_tensor(u[:, 16 + k, o], u[:, k, i], col("conv_w", 8 * tap + k),
                                                   u[:, 16 + k, o], ALU.mult, ALU.add)
                link(ins)
            dve.tensor_tensor(u[:, 8:16, :], u[:, 8:16, :], u[:, 16:24, :], ALU.mult).then_inc(s_conv, 1)
            dve.wait_ge(s_tab, 16)
            rope(8, [mq[:, 8:10, :], mq[:, 10:12, :], u[:, 43:44, :]], const("cos"), const("sin"))
            attention("mla")
            s = st["conv"]
            for c in range(KC):
                chunk_ready(dve, s, 0, c)
                dve.tensor_tensor(u[:, c, :], ps[:, (s.c0 + c) % 4, 0:LAT], u[:, 27 + c, :], ALU.mult)\
                   .then_inc(s_freeD, 1)
            s = st["mla"]
            for c in range(KC):
                chunk_ready(dve, s, 0, c)
                link(dve.tensor_tensor(u[:, 16 + c, :], ps[:, (s.c0 + c) % 4, 0:LAT], u[:, 35 + c, :], ALU.mult))
                dve.tensor_tensor(u[:, 16 + c, :], u[:, 16 + c, :], u[:, c, :], ALU.add).then_inc(s_freeD, 1)
            s = st["mix"]
            for c in range(KC + 1):
                if c < KC:
                    add(s, c)
                if c:
                    dve.wait_ge(s_freeD, s.d0 + c)
                    weighted("nq2", c - 1)
            rstd("nq2", 2)
            scaled_out(st["memq"], mq, 1.0 / 16.0, broadcast(rs[:, 0:2], 2))
            attention("mem")
            for c in range(KC):
                add(st["memo"], c)
            norm("nmoe")
            dve.wait_ge(s_moe, 1)
            link(dve.tensor_reduce(small[:, 118:120], ps[:, 4, 0:2 * NE].rearrange("p (q e) -> p q e", q=2), AX.X,
                                   ALU.max))
            dve.tensor_scalar(small[:, 120:122], small[:, 118:120], -1.0, None, ALU.mult).then_inc(s_rmax, 1)
            dve.wait_ge(s_rexp, 1)
            link(dve.reciprocal(small[:, 126:128], small[:, 122:124]))
            dve.tensor_tensor(aff, aff, small[:, 126:128].unsqueeze(2).to_broadcast([P, 2, NE]),
                              ALU.mult).then_inc(s_moeD, 1)
            dve.wait_ge(s_moe, 3)
            link(dve.tensor_copy(affT, ps[0:NE, 7, 0:LAT]))
            for r in range(CAP // 8):
                a = slice(8 * r, 8 * r + 8)
                link(dve.max(top[:, a], affT))
                link(dve.max_index(topi[:, a], top[:, a], affT))
                link(dve.match_replace(affT, top[:, a], affT, -1.0))
            link(dve.tensor_copy(topf, topi))
            dve.wait_ge(s_tab, 32)
            blocks = own.rearrange("p (e n) -> p e n", e=NE)
            for a, v in enumerate((topf, top)):
                ins = dve.tensor_tensor(spread[:, a, :].rearrange("p (e n) -> p e n", e=NE), blocks,
                                        v.unsqueeze(1).to_broadcast([NE, NE, CAP]), ALU.mult)
            ins.then_inc(s_moeD, 1)
            dve.wait_ge(s_moe, 4)
            for cut, signal in ((slice(0, P), s_sel), (slice(P, 512), s_moeD)):
                for q in range(2):
                    ins = dve.tensor_scalar(sel[:, q, cut], ps[:, 4, cut], const("token")[:, q:q + 1], None,
                                            ALU.is_equal)
                ins.then_inc(signal, 1)
            dve.wait_ge(s_moeD, 3)
            for q in range(2):
                for h in range(2):
                    ins = dve.tensor_tensor(gsel[:, q, :, h, :], ps[:, 5, :].rearrange("p (e n) -> p e n", e=NE),
                                            sel[:, q, :].rearrange("p (e n) -> p e n", e=NE), ALU.mult)
            ins.then_inc(s_moeD, 1)
            u0 = st["experts"].u0

            def pair_steps(i, pair, base, last=False):
                dve.wait_ge(s_sg, i + (pair + 1))
                dve.wait_ge(s_used, i * 48 + (base + 32))
                dve.tensor_tensor(hp, sg, ps[:, 5, :], ALU.mult).then_inc(s_he, 1)
                if pair == 0:
                    dve.wait_ge(s_moeA, 4 + KC)
                for h in range(2):
                    ins = dve.tensor_scalar(gx[:, h, :], work[:, bass.ds(i * LAT + pair * LAT, LAT)],
                                            const("halves")[:, h:h + 1], None, ALU.mult)
                ins.then_inc(s_gx, 1)
                if not last:
                    dve.tensor_copy(xe, xg[:, :, bass.ds(i * (2 * CAP) + (pair + 1) * 2 * CAP, 2 * CAP)])\
                       .then_inc(s_xe, 1)
                    dve.wait_ge(s_scat, i + (pair + 1))

            pair_steps(0, 0, u0)
            with dve.Fori(0, NE // 2 - 2) as i:
                pair_steps(i, 1, u0 + 32)
            pair_steps(NE // 2 - 2, 1, u0 + 32, last=True)
            dve.wait_ge(s_ssq, 2)
            link(dve.tensor_scalar(var[:, 0:2], small[:, 112:114], 1.0 / D, EPS, ALU.mult, ALU.add))
            newton(var[:, 0:2], rs[:, 0:2], tmp[:, 0:2])
            dve.wait_ge(s_grow, 16)
            for q in range(2):
                dve.scalar_tensor_tensor(otok[:, q, :].rearrange("p (a b) -> p a b", a=2), ps[:, 2 * q:2 * q + 2, :],
                                         rs[:, q:q + 1], grow.rearrange("p (a b) -> p a b", a=2), ALU.mult,
                                         ALU.mult).then_inc(s_res, 1)


def _rope_tables(seq, first):
    f = np.float32
    if first:
        half = HD // 2
        freqs = (f(1.0) / (f(10000.0) ** (np.arange(0, half, 2, dtype=f) / f(half)))).astype(f)
        pos = np.arange(seq)
        ar = (pos // GRID_W).astype(f)[:, None] * freqs
        ac = (pos % GRID_W).astype(f)[:, None] * freqs
        ang = np.concatenate([ar, ar, ac, ac], axis=-1)
    else:
        inv = (f(1.0) / (f(10000.0) ** (np.arange(0, HD, 2, dtype=f) / f(HD)))).astype(f)
        a = np.arange(seq, dtype=f)[:, None] * inv
        ang = np.concatenate([a, a], axis=-1)
    ang = np.concatenate([ang, ang], axis=-1).T
    return np.cos(ang).astype(f), np.sin(ang).astype(f)


def _rotation(half):
    m = np.zeros((P, P), np.float32)
    for b in range(0, P, 2 * half):
        for j in range(half):
            m[b + half + j, b + j] = -1.0
            m[b + j, b + half + j] = 1.0
    return m


def _constants():
    c = np.zeros((P, NCONST), np.float32)

    def put(name, v):
        c[:, CONST[name][0]:CONST[name][1]] = v
    put("ident", np.eye(P))
    put("ones", 1.0)
    put("rot_a", _rotation(HD // 4))
    put("rot_b", _rotation(HD // 2))
    cos, sin = _rope_tables(LAT, True)
    put("cos", cos)
    put("sin", sin)
    q = np.arange(P) % GRID_W
    start = np.clip(q - 8, 0, GRID_W - 16)
    k = np.arange(GRID_W)
    inside = (k[None, :] >= start[:, None]) & (k[None, :] < start[:, None] + 16)
    put("mask", np.where(inside, 0.0, NEG))
    put("inv", np.repeat([1.0 / 1024, 1.0 / 256, 1.0 / 128], 32)[None, :])
    put("halves", (np.arange(P)[:, None] // CAP % 2 == np.arange(2)[None, :]).astype(np.float32))
    put("groups", np.arange(P)[:, None] % 32 == np.arange(NE)[None, :])
    put("token", np.arange(P)[:, None] + np.array([[0, P]]))
    return c


def _blocks(w):
    K, M = w.shape
    return np.ascontiguousarray(w.reshape(K // P, P, M // P, P).transpose(2, 1, 0, 3)).reshape(M // P, P, K)


def _features(x):
    return np.ascontiguousarray(x.reshape(x.shape[0], -1, P).transpose(2, 1, 0))


def _column(v):
    return v.reshape(-1, P).T


def kernel(**inputs):
    import concourse.bacc as bacc
    from concourse.bass_utils import run_bass_kernel_spmd

    a = {k: np.asarray(v) for k, v in inputs.items()}
    arrays = {
        "consts": _constants(),
        "cond": np.ascontiguousarray(np.stack([a["c_ctx"], a["c"][0]]).reshape(2, KC, P).transpose(2, 1, 0)),
        "ctxT": _features(a["ctx"][0]), "xT": _features(a["x"][0]), "memT": _features(a["mem_2"][0]),
        "rope2": np.concatenate(_rope_tables(LAT, False), axis=1),
        "own": (np.arange(NE)[:, None] == (np.arange(NE * CAP) // CAP)[None, :]).astype(np.float32),
        "lam": np.concatenate([a["da_lambda_q1"], a["da_lambda_k1"], a["da_lambda_q2"], a["da_lambda_k2"]]),
        "final2": a["norm_final_g_2"],
        "rpb": np.ascontiguousarray(a["na_rpb"][0]),
        "wr": np.ascontiguousarray(a["w_router_2"][0].reshape(KC, P, NE).transpose(1, 0, 2)),
    }
    vectors = {
        "mix0": a["norm_mix"][0], "mix1": a["norm_mix"][1], "ffn0": a["norm_ffn"][0], "ffn1": a["norm_ffn"][1],
        "final": a["norm_final"], "mix2": a["norm_mix_g_2"][0], "mem": a["norm_mem_g_2"][0],
        "memkv": a["norm_memkv_g_2"][0], "moe": a["norm_moe_g_2"][0],
        "qn": a["q_norm_g_2"][0], "kvn": a["kv_norm_g_2"][0], "subln": a["da_subln"][0],
        "conv_w": a["conv_w_2"][0], "conv_b": a["conv_b_2"][0], "b_gate": a["b_gate_2"][0], "ada_b": a["ada_b"],
    }
    arrays["cols"] = np.ascontiguousarray(np.concatenate([_column(vectors[n]) for n, _ in _COLS], axis=1))
    for l in range(2):
        arrays[f"ada{l}"] = np.ascontiguousarray(
            a["ada_w"][l].reshape(KC, P, 3, 2, D).transpose(2, 0, 3, 1, 4)).reshape(3 * 16, P, D)
        gu = _blocks(a["ffn_w_gate_up"][l]).reshape(2, FC, P, D)
        arrays[f"gu{l}"] = np.ascontiguousarray(gu.transpose(1, 0, 2, 3)).reshape(2 * FC, P, D)
        arrays[f"down{l}"] = _blocks(a["ffn_w_down"][l]).reshape(KC, P, 2, WIDE)\
            .transpose(0, 2, 1, 3).reshape(2 * KC, P, WIDE)
    arrays["wqkv0"], arrays["wqkv1"] = _blocks(a["da_wqkv"][0]), _blocks(a["na_wqkv"][0])
    arrays["wo0"], arrays["wo1"] = _blocks(a["da_wo"][0]), _blocks(a["na_wo"][0])
    w = a["w_in_2"][0]
    kr = w[:, 3456:3520]
    arrays["win"] = _blocks(np.concatenate([w[:, 0:3456], w[:, 3520:5568], kr, kr], axis=1))
    wq = a["w_uq_2"][0].reshape(256, MLA_H, 192)
    wq = np.concatenate([wq[:, :, 0:P].reshape(256, -1), wq[:, :, P:].reshape(256, -1)], axis=1)
    arrays["uq"] = np.ascontiguousarray(_blocks(wq).reshape(3, 4, P, 256).transpose(0, 2, 1, 3)).reshape(3, P, D)
    wkv = a["w_ukv_2"][0].reshape(P, MLA_H, 2, P)
    arrays["ukv"] = np.ascontiguousarray(wkv.transpose(2, 0, 1, 3)).reshape(2, P, D)
    for n, src in (("conv_out", "w_conv_out_2"), ("mla_out", "w_mla_out_2"), ("mix_out", "w_mix_out_2"),
                   ("memq", "w_mem_q_2"), ("memkv", "w_mem_kv_2"), ("memo", "w_mem_out_2")):
        arrays[n] = _blocks(a[src][0])
    for n, src in (("gate", "w_exp_gate_2"), ("up", "w_exp_up_2"), ("down", "w_exp_down_2")):
        arrays[n] = a[src][0].reshape(NE * KC, P, D)

    nc = bacc.Bacc("TRN2", target_bir_lowering=False, num_devices=1)
    t = {n: nc.dram_tensor(f"in_{n}", v.shape, mybir.dt.from_np(v.dtype), kind="ExternalInput").ap()
         for n, v in arrays.items()}
    out = nc.dram_tensor("out_0", (2, P, D), F32, kind="ExternalOutput").ap()
    diffusion_moe_kernel(nc, t, out)
    r = run_bass_kernel_spmd(nc, [{f"in_{n}": v for n, v in arrays.items()}], core_ids=[0])
    got = r.results[0]["out_0"]
    return got.reshape(1, LAT, D)
```
